# Optimizing a Trainium2 kernel written in Bass

```python
import jax, jax.numpy as jnp
from jax import lax
import numpy as np

D_MODEL = 1024
BATCH = 1
SEQ = 128
DEPTH = 2
DEC_BATCH = 1
DEC_SEQ = 128
PAST_LEN = 128

GRID_W = 64
N_EVEN = (DEPTH + 1) // 2
N_ODD = DEPTH // 2
POOL_WINDOWS = (2, 4, 8, 16)
POOL_GROUPS = 4
POOL_GROUP_DIM = D_MODEL // 8
POOL_DIM = POOL_GROUPS * POOL_GROUP_DIM
HEAD_DIM = 64
N_Q_HEADS = (D_MODEL // 2) // HEAD_DIM
N_KV_HEADS = 2
Q_PER_KV = N_Q_HEADS // N_KV_HEADS
Q_DIM = N_Q_HEADS * HEAD_DIM
KV_DIM = N_KV_HEADS * HEAD_DIM
ATTN_WINDOW = 128
ATTN_BLOCK = 128
ATTN_SCALE = HEAD_DIM ** -0.5
ROPE_BASE = 10000.0
ROPE_AXIS_DIM = HEAD_DIM // 2
IN_AB = POOL_DIM + Q_DIM + 2 * KV_DIM
MIX_AB = POOL_DIM + Q_DIM
CONV_DIM = D_MODEL
CONV_WIDTH = 31
N_GROUPS = 4
EXPERTS_PER_GROUP = 4
N_EXPERTS = N_GROUPS * EXPERTS_PER_GROUP
TOP_K_IN_GROUP = 2
EXPERT_HIDDEN = D_MODEL // 2
EPS = 1e-6
NEG_BIG = -1e30

kernel_name = "hybrid_pool_swa_conformer_hmoe_dit_step"

def rmsnorm(x, g):
    xf = x.astype(jnp.float32)
    y = xf * lax.rsqrt(jnp.mean(xf * xf, axis=-1, keepdims=True) + EPS)
    return (y * g.astype(jnp.float32)).astype(x.dtype)

def layernorm(x, g, b):
    xf = x.astype(jnp.float32)
    mu = jnp.mean(xf, axis=-1, keepdims=True)
    var = jnp.mean(jnp.square(xf - mu), axis=-1, keepdims=True)
    y = (xf - mu) * lax.rsqrt(var + EPS) * g.astype(jnp.float32) + b.astype(jnp.float32)
    return y.astype(x.dtype)

def modulation(cond, w_ada, b_ada):
    m = jax.nn.silu(cond) @ w_ada + b_ada
    return jnp.split(m[:, None, :], 6, axis=-1)

def centred_mean(u, window):
    n = u.shape[1]
    lo = window // 2
    hi = window - lo - 1
    uf = u.astype(jnp.float32)
    cs = jnp.concatenate([jnp.zeros_like(uf[:, :1]), jnp.cumsum(uf, axis=1)], axis=1)
    t = jnp.arange(n)
    start = jnp.clip(t - lo, 0, n)
    end = jnp.clip(t + hi + 1, 0, n)
    total = cs[:, end] - cs[:, start]
    count = (end - start).astype(jnp.float32)[None, :, None]
    return (total / count).astype(u.dtype)

def pool_mixer(u, w_pool, pool_scale):
    b, n, _ = u.shape
    ug = u.reshape(b, n, POOL_GROUPS, POOL_GROUP_DIM)
    pooled = jnp.stack([centred_mean(ug[:, :, g], w) - ug[:, :, g]
                        for g, w in enumerate(POOL_WINDOWS)], axis=2)
    mixed = jnp.einsum('bngc,gcd->bngd', pooled, w_pool)
    return mixed.reshape(b, n, POOL_DIM) * pool_scale

def axial_rope_tables(n):
    rows = n // GRID_W
    t = jnp.arange(rows * GRID_W)
    row = (t // GRID_W).astype(jnp.float32)
    col = (t % GRID_W).astype(jnp.float32)
    inv = ROPE_BASE ** (-jnp.arange(0, ROPE_AXIS_DIM, 2, dtype=jnp.float32) / ROPE_AXIS_DIM)

    def table(p):
        ang = p[:, None] * inv[None, :]
        ang = jnp.concatenate([ang, ang], axis=-1)
        return jnp.cos(ang)[None, :, None, :], jnp.sin(ang)[None, :, None, :]

    return table(row), table(col)

def rotate(x, cos, sin):
    half = x.shape[-1] // 2
    rot = jnp.concatenate([-x[..., half:], x[..., :half]], axis=-1)
    return x * cos + rot * sin

def apply_axial_rope(x, tables):
    (cr, sr), (cc, sc) = tables
    xf = x.astype(jnp.float32)
    xr = rotate(xf[..., :ROPE_AXIS_DIM], cr, sr)
    xc = rotate(xf[..., ROPE_AXIS_DIM:], cc, sc)
    return jnp.concatenate([xr, xc], axis=-1).astype(x.dtype)

def split_ab(proj):
    b, n, _ = proj.shape
    a = proj[..., :POOL_DIM]
    q = proj[..., POOL_DIM:POOL_DIM + Q_DIM].reshape(b, n, N_Q_HEADS, HEAD_DIM)
    k = proj[..., POOL_DIM + Q_DIM:POOL_DIM + Q_DIM + KV_DIM].reshape(b, n, N_KV_HEADS, HEAD_DIM)
    v = proj[..., POOL_DIM + Q_DIM + KV_DIM:].reshape(b, n, N_KV_HEADS, HEAD_DIM)
    return a, q, k, v

def sink_logits(sink, shape):
    s = sink.astype(jnp.float32).reshape((1,) * (len(shape) - 4) + (N_KV_HEADS, Q_PER_KV, 1, 1))
    return jnp.broadcast_to(s, shape[:-1] + (1,))

def context_attention(q, k, v, sink):
    b, l = q.shape[0], q.shape[1]
    qg = q.reshape(b, l, N_KV_HEADS, Q_PER_KV, HEAD_DIM)
    s = jnp.einsum('bqhgd,bkhd->bhgqk', qg, k).astype(jnp.float32) * ATTN_SCALE
    p = jax.nn.softmax(jnp.concatenate([s, sink_logits(sink, s.shape)], axis=-1), axis=-1)[..., :-1]
    o = jnp.einsum('bhgqk,bkhd->bqhgd', p.astype(v.dtype), v)
    return o.reshape(b, l, Q_DIM)

def latent_window_attention(q, k, v, ck, cv, sink):
    b, n = q.shape[0], q.shape[1]
    nb = n // ATTN_BLOCK
    lc = ck.shape[1]
    qb = q.reshape(b, nb, ATTN_BLOCK, N_KV_HEADS, Q_PER_KV, HEAD_DIM)

    def band(x):
        xp = jnp.pad(x, ((0, 0), (ATTN_BLOCK, ATTN_BLOCK), (0, 0), (0, 0)))
        xp = xp.reshape(b, nb + 2, ATTN_BLOCK, N_KV_HEADS, HEAD_DIM)
        return jnp.concatenate([xp[:, :-2], xp[:, 1:-1], xp[:, 2:]], axis=2)

    kw, vw = band(k), band(v)
    blk = jnp.arange(nb)[:, None]
    qpos = blk * ATTN_BLOCK + jnp.arange(ATTN_BLOCK)[None, :]
    kpos = (blk - 1) * ATTN_BLOCK + jnp.arange(3 * ATTN_BLOCK)[None, :]
    valid = ((jnp.abs(qpos[:, :, None] - kpos[:, None, :]) <= ATTN_WINDOW)
             & (kpos[:, None, :] >= 0) & (kpos[:, None, :] < n))
    s_loc = jnp.einsum('bnqhgd,bnkhd->bnhgqk', qb, kw).astype(jnp.float32) * ATTN_SCALE
    s_loc = jnp.where(valid[None, :, None, None], s_loc, NEG_BIG)
    s_ctx = jnp.einsum('bnqhgd,bkhd->bnhgqk', qb, ck).astype(jnp.float32) * ATTN_SCALE
    p = jax.nn.softmax(jnp.concatenate([s_loc, s_ctx, sink_logits(sink, s_loc.shape)], axis=-1), axis=-1)
    wl = 3 * ATTN_BLOCK
    p_loc = p[..., :wl].astype(v.dtype)
    p_ctx = p[..., wl:wl + lc].astype(v.dtype)
    o = (jnp.einsum('bnhgqk,bnkhd->bnqhgd', p_loc, vw)
         + jnp.einsum('bnhgqk,bkhd->bnqhgd', p_ctx, cv))
    return o.reshape(b, n, Q_DIM)

def even_mixer_context(h, w_in, w_pool, pool_scale, sink, w_out):
    a, q, k, v = split_ab(h @ w_in)
    y = jnp.concatenate([pool_mixer(a, w_pool, pool_scale), context_attention(q, k, v, sink)], axis=-1)
    return y @ w_out, k, v

def even_mixer_latent(h, ck, cv, w_in, w_pool, pool_scale, sink, w_out):
    a, q, k, v = split_ab(h @ w_in)
    tables = axial_rope_tables(h.shape[1])
    q = apply_axial_rope(q, tables)
    k = apply_axial_rope(k, tables)
    y = jnp.concatenate([pool_mixer(a, w_pool, pool_scale),
                         latent_window_attention(q, k, v, ck, cv, sink)], axis=-1)
    return y @ w_out

def conformer_conv(h, w1, b1, w_dw, b_dw, ln_g, ln_b, w2, b2):
    u = h @ w1 + b1
    u = u[..., :CONV_DIM] * jax.nn.sigmoid(u[..., CONV_DIM:])
    u = lax.conv_general_dilated(u, w_dw[:, None, :], window_strides=(1,),
                                 padding=[(CONV_WIDTH // 2, CONV_WIDTH // 2)],
                                 dimension_numbers=('NWC', 'WIO', 'NWC'),
                                 feature_group_count=CONV_DIM) + b_dw
    u = jax.nn.silu(layernorm(u, ln_g, ln_b))
    return u @ w2 + b2

def hierarchical_moe(h, w_grp, w_exp, w1, w3, w2):
    b, n, d = h.shape
    t = h.reshape(b * n, d)
    g_prob = jax.nn.softmax((t @ w_grp).astype(jnp.float32), axis=-1)
    g_idx = jnp.argmax(g_prob, axis=-1)
    g_w = jnp.take_along_axis(g_prob, g_idx[:, None], axis=-1)
    e_logits = jnp.einsum('td,gde->tge', t, w_exp).astype(jnp.float32)
    e_logits = jnp.take_along_axis(e_logits, g_idx[:, None, None], axis=1)[:, 0]
    top_v, top_i = lax.top_k(e_logits, TOP_K_IN_GROUP)
    e_w = jax.nn.softmax(top_v, axis=-1) * g_w
    expert = g_idx[:, None] * EXPERTS_PER_GROUP + top_i
    gate = jnp.sum(jax.nn.one_hot(expert, N_EXPERTS, dtype=jnp.float32) * e_w[..., None], axis=1)
    hg = jnp.einsum('td,edf->tef', t, w1)
    hu = jnp.einsum('td,edf->tef', t, w3)
    a = jax.nn.silu(hg) * hu * gate[..., None].astype(t.dtype)
    y = jnp.einsum('tef,efd->td', a, w2)
    return y.reshape(b, n, d)

def setup_inputs(seed: int = 0) -> dict:
    key = jax.random.key(seed)
    ks = iter(jax.random.split(key, 40))

    def nrm(shape, scale):
        return jax.random.normal(next(ks), shape, jnp.float32) * scale

    D = D_MODEL
    return {
        "x_prompt": nrm((BATCH, SEQ, D), 1.0),
        "x_sample": nrm((DEC_BATCH, DEC_SEQ, D), 1.0),
        "cache_k": nrm((DEC_BATCH, N_EVEN, PAST_LEN, N_KV_HEADS, HEAD_DIM), 1.0),
        "cache_v": nrm((DEC_BATCH, N_EVEN, PAST_LEN, N_KV_HEADS, HEAD_DIM), 1.0),
        "c": nrm((DEC_BATCH, D), 1.0),
        "c_ctx": nrm((D,), 1.0),
        "w_ada": nrm((DEPTH, D, 6 * D), 0.5 * D ** -0.5),
        "b_ada": nrm((DEPTH, 6 * D), 0.02),
        "norm_mix_g": 1.0 + nrm((DEPTH, D), 0.05),
        "norm_ffn_g": 1.0 + nrm((DEPTH, D), 0.05),
        "w_in_ab": nrm((N_EVEN, D, IN_AB), D ** -0.5),
        "pool_w": nrm((N_EVEN, POOL_GROUPS, POOL_GROUP_DIM, POOL_GROUP_DIM), POOL_GROUP_DIM ** -0.5),
        "pool_scale": 1.0 + nrm((N_EVEN, POOL_DIM), 0.1),
        "attn_sink": nrm((N_EVEN, N_Q_HEADS), 0.5),
        "w_out_ab": nrm((N_EVEN, MIX_AB, D), MIX_AB ** -0.5),
        "conv_w1": nrm((N_ODD, D, 2 * CONV_DIM), D ** -0.5),
        "conv_b1": nrm((N_ODD, 2 * CONV_DIM), 0.02),
        "conv_dw": nrm((N_ODD, CONV_WIDTH, CONV_DIM), CONV_WIDTH ** -0.5),
        "conv_dw_b": nrm((N_ODD, CONV_DIM), 0.02),
        "conv_ln_g": 1.0 + nrm((N_ODD, CONV_DIM), 0.05),
        "conv_ln_b": nrm((N_ODD, CONV_DIM), 0.02),
        "conv_w2": nrm((N_ODD, CONV_DIM, D), CONV_DIM ** -0.5),
        "conv_b2": nrm((N_ODD, D), 0.02),
        "router_grp": nrm((DEPTH, D, N_GROUPS), D ** -0.5),
        "router_exp": nrm((DEPTH, N_GROUPS, D, EXPERTS_PER_GROUP), D ** -0.5),
        "moe_w1": nrm((DEPTH, N_EXPERTS, D, EXPERT_HIDDEN), D ** -0.5),
        "moe_w3": nrm((DEPTH, N_EXPERTS, D, EXPERT_HIDDEN), D ** -0.5),
        "moe_w2": nrm((DEPTH, N_EXPERTS, EXPERT_HIDDEN, D), EXPERT_HIDDEN ** -0.5),
        "final_g": 1.0 + nrm((D,), 0.05),
    }

def reference(x_prompt, x_sample, cache_k, cache_v, c, c_ctx, w_ada, b_ada, norm_mix_g, norm_ffn_g,
              w_in_ab, pool_w, pool_scale, attn_sink, w_out_ab, conv_w1, conv_b1, conv_dw, conv_dw_b,
              conv_ln_g, conv_ln_b, conv_w2, conv_b2, router_grp, router_exp, moe_w1, moe_w3, moe_w2,
              final_g):
    def channel_mixer(x, l, shift, scale, gate):
        h = rmsnorm(x, norm_ffn_g[l]) * (1 + scale) + shift
        return x + gate * hierarchical_moe(h, router_grp[l], router_exp[l], moe_w1[l], moe_w3[l], moe_w2[l])

    def odd_mixer(h, o):
        return conformer_conv(h, conv_w1[o], conv_b1[o], conv_dw[o], conv_dw_b[o],
                              conv_ln_g[o], conv_ln_b[o], conv_w2[o], conv_b2[o])

    x = x_prompt
    ks, vs = [], []
    for l in range(DEPTH):
        sh1, sc1, g1, sh2, sc2, g2 = modulation(c_ctx[None, :], w_ada[l], b_ada[l])
        h = rmsnorm(x, norm_mix_g[l]) * (1 + sc1) + sh1
        if l % 2 == 0:
            e = l // 2
            y, k, v = even_mixer_context(h, w_in_ab[e], pool_w[e], pool_scale[e], attn_sink[e], w_out_ab[e])
            ks.append(k)
            vs.append(v)
        else:
            y = odd_mixer(h, l // 2)
        x = x + g1 * y
        x = channel_mixer(x, l, sh2, sc2, g2)
    y_prompt = rmsnorm(x, final_g)
    state_k = jnp.stack(ks, axis=1)
    state_v = jnp.stack(vs, axis=1)

    x = x_sample
    for l in range(DEPTH):
        sh1, sc1, g1, sh2, sc2, g2 = modulation(c, w_ada[l], b_ada[l])
        h = rmsnorm(x, norm_mix_g[l]) * (1 + sc1) + sh1
        if l % 2 == 0:
            e = l // 2
            y = even_mixer_latent(h, cache_k[:, e], cache_v[:, e], w_in_ab[e], pool_w[e], pool_scale[e],
                                  attn_sink[e], w_out_ab[e])
        else:
            y = odd_mixer(h, l // 2)
        x = x + g1 * y
        x = channel_mixer(x, l, sh2, sc2, g2)
    y_sample = rmsnorm(x, final_g)

    return (y_prompt, y_sample, state_k, state_v)


_drawn_inputs = setup_inputs


def setup_inputs(seed=0):
    import zlib

    import numpy as np

    out = dict(_drawn_inputs(seed))
    spreads = {}
    factors = {'cache_k': 3.814,
     'cache_v': 3.112,
     'attn_sink': 38.298,
     'conv_b1': 8.0,
     'conv_dw_b': 6.477,
     'conv_ln_g': 4.683,
     'conv_ln_b': 8.0,
     'conv_b2': 6.939}
    for name, (base, spread) in spreads.items():
        noise = np.random.default_rng([zlib.crc32(name.encode()), seed]).standard_normal(out[name].shape)
        drawn = base * np.exp(spread * noise) if base else spread * noise
        out[name] = __import__('jax').numpy.asarray(drawn.astype(out[name].dtype))
    for name, factor in factors.items():
        out[name] = (out[name] * factor).astype(out[name].dtype)
    return out
```

```python
from contextlib import ExitStack

import numpy as np

import concourse.bass as bass
from concourse import mybir

P = 128
ALU = mybir.AluOpType
ACT = mybir.ActivationFunctionType
F32 = mybir.dt.float32
AX = mybir.AxisListType

D = 1024
DC = D // P
TG = 128
NT = 2 * TG
HD = 64
NH = 8
NE = 16
FF = 512
FC = FF // P
EPS = 1e-6
SCALE = HD ** -0.5
TAPS = 31
HALF = TAPS // 2
UL = TG + 2 * HALF
WINDOWS = (2, 4, 8, 16)
APAD = 8
AL = TG + 2 * APAD
SLOTS = 6
TW = 512

C_ID, C_ROT, C_COS, C_SIN, C_CNT = 0, 128, 256, 384, 512
C_W = 1024

V_NMIX, V_NFFN, V_FIN, V_CB1, V_DWB, V_LNG, V_LNB, V_CB2, V_PSC, V_CCTX, V_C = (
    0, 16, 32, 40, 56, 64, 72, 80, 88, 92, 100)
V_ROWS = 108


def weight_stream():
    ada = lambda l, parts: [("ada", l, 2 * p + h) for p in parts for h in range(2)]
    moe = lambda l: [(k, l, e) for e in range(NE) for k in ("w1", "w3", "w2")]
    return (ada(0, (0, 1)) + [("in", 0, n) for n in range(3)] + ada(0, (2, 3, 4, 5))
            + [("out", 0, n) for n in range(2)] + moe(0)
            + ada(1, (0, 1)) + [("cw1", 1, n) for n in (0, 2, 1, 3)] + ada(1, (2, 3, 4, 5))
            + [("cw2", 1, n) for n in range(2)] + moe(1))


STREAM = weight_stream()
TILE = {key: n for n, key in enumerate(STREAM)}


def backbone(nc, x_prompt, x_sample, cache_k, cache_v, c, c_ctx, w_ada, b_ada, norm_mix_g, norm_ffn_g,
             w_in_ab, pool_w, pool_scale, attn_sink, w_out_ab, conv_w1, conv_b1, conv_dw, conv_dw_b,
             conv_ln_g, conv_ln_b, conv_w2, conv_b2, router_grp, router_exp, moe_w1, moe_w3, moe_w2,
             final_g, shape_consts, y_prompt, y_sample, state_k, state_v):
    with ExitStack() as ctx:
        def sb(name, shape, dt=F32):
            return ctx.enter_context(nc.sbuf_tensor(name, shape, dt))

        def sem(name):
            return ctx.enter_context(nc.semaphore(name))

        ps = ctx.enter_context(nc.psum_tensor("ps", [P, 8, 512], F32))
        psx = ps[:, 0:4, :].rearrange("p b (h t) -> p (b h) t", h=2)
        ps_ada = ps[:, 7, 0:192].rearrange("p (l m g) -> p l m g", l=2, g=2)

        ring = sb("ring", [P, SLOTS, DC * TW])
        cst = sb("cst", [P, C_W])
        ones = sb("ones", [P, P])
        zrow = sb("zrow", [1, 512])
        xtok = sb("xtok", [P, 2, D])
        xT = sb("xT", [P, DC, NT])
        hT = sb("hT", [P, DC, NT])
        sq = sb("sq", [P, DC, NT])
        vec = sb("vec", [P, V_ROWS])
        bias = sb("bias", [P, 2, 48])
        dw = sb("dw", [P, DC, TAPS])
        wr = sb("wr", [P, 2, DC, 20])
        sinkrow = sb("sinkrow", [1, NH])
        sink = sb("sink", [P, NH])
        csil = sb("csil", [P, DC, 2])
        mod = sb("mod", [P, 2, 48, 2])
        gain = sb("gain", [P, 2, 2, DC, 2])
        rstd = sb("rstd", [P, NT])
        root = sb("root", [P, NT])
        mean = sb("mean", [P, NT])
        mixT = hT
        poolw = sb("poolw", [P, 4, P])
        apad = sb("apad", [P, 4, 2, AL])
        asum = sb("asum", [P, 2, 4, 2, AL])
        stage = sb("stage", [P, 4 * NT + 10 * TG])
        qT = stage[:, 0:4 * NT].rearrange("p (c t) -> p c t", c=4)
        rt, rt2 = (stage[:, 4 * NT + 5 * TG * n:4 * NT + 5 * TG * (n + 1)].rearrange(
            "p (c t) -> p c t", c=5) for n in range(2))
        sil = stage[:, 0:4 * NT].rearrange("p (c t) -> p c t", c=4)
        gated = stage[:, 4 * NT:8 * NT].rearrange("p (c t) -> p c t", c=4)
        kT = sb("kT", [P, 2, NT])
        ckT = sb("ckT", [P, 2, TG])
        cktok = sb("cktok", [P, P])
        cvtok = sb("cvtok", [P, P])
        kvctx = sb("kvctx", [P, 2 * P])
        vlat = sb("vlat", [P, P])
        smax = sb("smax", [P, 2, NH])
        nmax = sb("nmax", [P, 2, NH])
        rsum = sb("rsum", [P, 2, NH])
        esink = sb("esink", [P, 2, NH])
        rden = sb("rden", [P, 2, NH])
        work = sb("work", [P, 6144])
        rows_v = work[0:V_ROWS, 0:P]
        rows_b = work[0:96, P:2 * P]
        rows_r = work[0:80, 2 * P:6 * P]
        rows_dw = work[0:TAPS, 6 * P:6 * P + D]
        probs = work[:, 0:3072].rearrange("p (n k) -> p n k", k=TG)
        probsT = work[:, 3072:6144].rearrange("p (n k) -> p n k", k=TG)
        upad = work[:, 0:DC * 2 * UL].rearrange("p (c g t) -> p c g t", c=DC, g=2)
        conv = work[:, 2560:2560 + DC * NT].rearrange("p (c t) -> p c t", c=DC)
        gatebc = work[:, 0:NE * NT].rearrange("p (e t) -> p e t", e=NE)
        actT = work[:, NE * NT:NE * NT + 2 * FC * NT].rearrange("p (u f t) -> p u f t", u=2, f=FC)
        eps = sb("eps", [P, 1])
        mean4 = sb("mean4", [P, 2, TG])
        lg = sb("lg", [P, 2, 20])
        r1 = sb("r1", [P, 2, 16])
        rg = sb("rg", [P, 12, 2, 4])
        rs = sb("rs", [P, 12, 2])
        gate = sb("gate", [P, 2, NE])

        ident = cst[:, C_ID:C_ID + P]
        rot = cst[:, C_ROT:C_ROT + P]
        cos = cst[:, C_COS:C_COS + P]
        sin = cst[:, C_SIN:C_SIN + P]
        icnt = cst[:, C_CNT:C_CNT + 4 * P].rearrange("p (w t) -> p w t", w=4)

        slot_full = [sem(f"slot_full{s}") for s in range(SLOTS)]
        tiles_used = sem("tiles_used")
        s_x = sem("s_x")
        s_cst = sem("s_cst")
        s_rows = sem("s_rows")
        s_kv = sem("s_kv")
        s_fill = sem("s_fill")
        s_xt = sem("s_xt")
        s_vt = sem("s_vt")
        s_prep = sem("s_prep")
        s_vec = sem("s_vec")
        s_csil = sem("s_csil")
        mod_taken = sem("mod_taken")
        x_ready = [sem(f"x_ready{n}") for n in range(5)]
        sq_ready = [sem(f"sq_ready{n}") for n in range(5)]
        ss_done = [sem(f"ss_done{n}") for n in range(5)]
        root_ready = [sem(f"root_ready{n}") for n in range(5)]
        hpre_ready = [sem(f"hpre_ready{n}") for n in range(5)]
        h_ready = [sem(f"h_ready{n}") for n in range(5)]
        y_done = [sem(f"y_done{n}") for n in range(4)]
        s_dve = sem("s_dve")
        s_act = sem("s_act")
        s_pool = sem("s_pool")
        qkv_done = sem("qkv_done")
        a_ready = sem("a_ready")
        qraw_ready = sem("qraw_ready")
        rot_done = sem("rot_done")
        qk_ready = sem("qk_ready")
        kv_ready = sem("kv_ready")
        scores_done = sem("scores_done")
        nmax_ready = sem("nmax_ready")
        exp_ready = sem("exp_ready")
        probs_ready = sem("probs_ready")
        pt_done = sem("pt_done")
        pt_ready = sem("pt_ready")
        pv_done = sem("pv_done")
        pooled_ready = sem("pooled_ready")
        pool_done = sem("pool_done")
        mix_ready = sem("mix_ready")
        glu_done = sem("glu_done")
        sig_ready = sem("sig_ready")
        u_ready = sem("u_ready")
        tap_done = sem("tap_done")
        conv_ready = sem("conv_ready")
        mean_done = sem("mean_done")
        mean_ready = sem("mean_ready")
        cent_ready = sem("cent_ready")
        csq_ready = sem("csq_ready")
        var_done = sem("var_done")
        croot_ready = sem("croot_ready")
        cn_ready = sem("cn_ready")
        cs_ready = sem("cs_ready")
        yb_ready = sem("yb_ready")
        route_done = [sem(f"route_done{l}") for l in range(2)]
        gexp_in = [sem(f"gexp_in{l}") for l in range(2)]
        gexp_out = [sem(f"gexp_out{l}") for l in range(2)]
        gate_ready = [sem(f"gate_ready{l}") for l in range(2)]
        gbc_done = [sem(f"gbc_done{l}") for l in range(2)]
        hid_done = [sem(f"hid_done{l}") for l in range(2)]
        sil_ready = [sem(f"sil_ready{l}") for l in range(2)]
        gated_ready = [sem(f"gated_ready{l}") for l in range(2)]
        act_ready = [sem(f"act_ready{l}") for l in range(2)]
        gate_turns = sem("gate_turns")
        out_t = sem("out_t")
        out_ready = [sem(f"out_ready{g}") for g in range(2)]
        s_out = sem("s_out")

        def wtile(key):
            w = ring[:, TILE[key] % SLOTS, :]
            return w.rearrange("p (k n) -> p k n", k=FC if key[0] == "w2" else DC)

        def landed(eng, key):
            n = TILE[key]
            eng.wait_ge(slot_full[n % SLOTS], 16 * (n // SLOTS + 1))

        def used(eng, key):
            eng.wait_ge(tiles_used, TILE[key] + 1)

        def product(eng, done, kind, l, k):
            if k % 4 < 2:
                eng.wait_ge(done, k // 4 + 1)
            else:
                used(eng, (kind, l, k // 4))

        SOURCE = {
            "ada": lambda l, n: w_ada[l, :, n * TW:(n + 1) * TW],
            "in": lambda l, n: w_in_ab[0, :, n * TW:min((n + 1) * TW, 1280)],
            "out": lambda l, n: w_out_ab[0, :, n * TW:(n + 1) * TW],
            "cw1": lambda l, n: conv_w1[0, :, n * TW:(n + 1) * TW],
            "cw2": lambda l, n: conv_w2[0, :, n * TW:(n + 1) * TW],
        }
        LAST_IN = ("in", 0, 2)

        block = ctx.enter_context(nc.Block())

        @block.sync
        def _(sp):
            def load(key):
                n = TILE[key]
                src = SOURCE[key[0]](key[1], key[2])
                width = src.shape[1]
                dst = ring[:, n % SLOTS, 0:DC * width].rearrange("p (k n) -> p k n", k=DC)
                if n >= SLOTS:
                    sp.wait_ge(tiles_used, n - SLOTS + 1)
                sp.dma_start(dst, src.rearrange("(k p) n -> p k n", p=P)).then_inc(slot_full[n % SLOTS], 16)

            for g, x in enumerate((x_prompt, x_sample)):
                sp.dma_start(xtok[:, g, :], x[0]).then_inc(s_x, 16)
            for key in STREAM[:TILE["w1", 0, 0]]:
                load(key)

            def load_experts(l):
                first = TILE["w1", l, 0]
                with sp.Fori(0, NE // 2) as i:
                    for u in range(2):
                        for j, w in enumerate((moe_w1, moe_w3, moe_w2)):
                            n = first + 3 * u + j
                            k = FC if j == 2 else DC
                            dst = ring[:, n % SLOTS, :].rearrange("p (k n) -> p k n", k=k)
                            src = w[l, bass.ds(i * 2 + u, 1)].rearrange("o (k p) n -> p (o k) n", p=P)
                            sp.wait_ge(tiles_used, i * 6 + (n - SLOTS + 1))
                            sp.dma_start(dst, src).then_inc(slot_full[n % SLOTS], 16)

            load_experts(0)
            for key in STREAM[TILE["w2", 0, NE - 1] + 1:TILE["w1", 1, 0]]:
                load(key)
            load_experts(1)
            for g, y in enumerate((y_prompt, y_sample)):
                sp.wait_ge(out_ready[g], 2)
                sp.dma_start(y[0], xtok[:, g, :]).then_inc(s_out, 16)
            sp.wait_ge(s_out, 64)

        @block.tensor
        def _(pe):
            def mm(out, lhsT, rhs, start=True, stop=True):
                return nc.tensor.matmul(out, lhsT, rhs, start=start, stop=stop, skip_group_check=True)

            def ada(l, parts):
                for p in parts:
                    for h in range(2):
                        key = ("ada", l, 2 * p + h)
                        landed(pe, key)
                        w = wtile(key)
                        for m in range(4):
                            for k in range(DC):
                                last = mm(ps_ada[:, l, 8 * p + 4 * h + m, :], w[:, k, m * P:(m + 1) * P],
                                          csil[:, k, :], k == 0, k == DC - 1)
                        last.then_inc(tiles_used, 1)

            def column_sums(dst, src, ready, count, done):
                for k in range(DC):
                    pe.wait_ge(ready, count(k))
                    last = mm(dst, ones[:, :], src[:, k, :], k == 0, k == DC - 1)
                last.then_inc(done, 1)

            def norm_sums(n):
                column_sums(ps[:, 6, 0:NT], sq, sq_ready[n], lambda k: k + 1, ss_done[n])

            pe.wait_ge(s_cst, 16)
            pe.wait_ge(s_x, 32)
            for k in range(DC):
                for g in range(2):
                    last = nc.tensor.transpose(psx[:, k, g * TG:(g + 1) * TG], xtok[:, g, k * P:(k + 1) * P],
                                               ident)
                if k % 2:
                    last.then_inc(s_xt, 1)
            pe.wait_ge(s_rows, 16 * 16)
            nc.tensor.transpose(ps[:, 4, 0:V_ROWS], rows_v[:, :], ident[0:V_ROWS, 0:V_ROWS])
            nc.tensor.transpose(ps[:, 4, 128:224], rows_b[:, :], ident[0:96, 0:96])
            for k in range(DC):
                nc.tensor.transpose(ps[:, 5, k * TAPS:(k + 1) * TAPS], rows_dw[:, k * P:(k + 1) * P],
                                    ident[0:TAPS, 0:TAPS])
            rv = rows_r[:, :].rearrange("r (p e) -> r e p", e=4)
            for e in range(4):
                nc.tensor.transpose(ps[:, 6, e * 80:(e + 1) * 80], rv[:, e, :], ident[0:80, 0:80])
            pe.wait_ge(s_fill, 1)
            mm(ps[:, 4, 256:256 + NH], ones[0:1, :],
               sinkrow[0:1, :].rearrange("o (i r) -> o r i", r=2)).then_inc(s_vt, 1)

            pe.wait_ge(s_csil, 1)
            ada(0, (0, 1))
            pe.wait_ge(s_prep, 1)
            norm_sums(0)

            def project(key, out, ready=None):
                landed(pe, key)
                w = wtile(key)
                for m in range(4):
                    for k in range(DC):
                        if ready is not None and m == 0:
                            pe.wait_ge(ready, k + 1)
                        last = mm(out(m), w[:, k, m * P:(m + 1) * P], hT[:, k, :], k == 0, k == DC - 1)
                last.then_inc(tiles_used, 1)

            project(("in", 0, 0), lambda m: psx[:, m, :], h_ready[0])
            project(("in", 0, 1), lambda m: psx[:, 4 + m, :])
            landed(pe, LAST_IN)
            w = ring[:, TILE[LAST_IN] % SLOTS, 0:DC * 2 * P].rearrange("p (k n) -> p k n", k=DC)
            for k in range(DC):
                mm(ps[:, 4, 0:NT], w[:, k, 0:P], hT[:, k, :], k == 0, k == DC - 1)
            for k in range(DC):
                mm(ps[:, 5, 0:2 * P], hT[:, k, 0:TG], w[:, k, 0:2 * P], k == 0, k == DC - 1)
            for k in range(DC):
                last = mm(ps[:, 4, NT:NT + P], hT[:, k, TG:NT], w[:, k, P:2 * P], k == 0, k == DC - 1)
            last.then_inc(tiles_used, 1)
            pe.wait_ge(s_kv, 48)
            nc.tensor.transpose(ps[:, 4, NT + P:NT + 2 * P], cktok[:, :], ident).then_inc(qkv_done, 1)
            ada(0, (2, 3))
            pe.wait_ge(qraw_ready, 2)
            mm(ps[:, 6, :], rot, qT[:, :, TG:NT])
            mm(ps[:, 4, 0:P], rot, kT[:, 0, TG:NT]).then_inc(rot_done, 1)
            pe.wait_ge(a_ready, 1)
            pe.wait_ge(kv_ready, 1)
            pe.wait_ge(qk_ready, 2)
            for r in range(2):
                lo, hi = 64 * r, 64 * r + 64
                for i in range(4):
                    kv = (2 * i + r) // 4
                    mm(ps[:, r, i * P:(i + 1) * P], qT[lo:hi, i, 0:TG], kT[lo:hi, int(kv != r), 0:TG])
            nc_last = None
            for r in range(2):
                lo, hi = 64 * r, 64 * r + 64
                for i in range(4):
                    kv = (2 * i + r) // 4
                    at = (i % 2) * 2 * P
                    b = 2 + 2 * r + i // 2
                    mm(ps[:, b, at:at + P], qT[lo:hi, i, TG:NT], kT[lo:hi, int(kv != r), TG:NT])
                    nc_last = mm(ps[:, b, at + P:at + 2 * P], qT[lo:hi, i, TG:NT], ckT[lo:hi, int(kv != r), :])
            nc_last.then_inc(scores_done, 1)
            pe.wait_ge(mod_taken, 2)
            ada(0, (4, 5))
            for n in range(24):
                if n % 8 == 0:
                    pe.wait_ge(probs_ready, n // 8 + 1)
                last = nc.tensor.transpose(ps[:, n // 4, (n % 4) * P:(n % 4 + 1) * P], probs[:, n, :], ident)
                if n % 4 == 3:
                    last.then_inc(pt_done, 1)
            pe.wait_ge(pt_ready, 6)
            for r in range(2):
                for i in range(4):
                    h = r * 4 + i
                    kv = (2 * i + r) // 4
                    v = slice(64 * kv, 64 * kv + 64)
                    mm(psx[64 * r:64 * r + 64, i, 0:TG], kvctx[:, P + 64 * kv:P + 64 * kv + 64], probsT[:, h, :])
                    mm(psx[64 * r:64 * r + 64, i, TG:NT], vlat[:, v], probsT[:, 8 + 2 * h, :], True, False)
                    last = mm(psx[64 * r:64 * r + 64, i, TG:NT], cvtok[:, v], probsT[:, 9 + 2 * h, :], False, True)
            last.then_inc(pv_done, 1)
            pe.wait_ge(pooled_ready, 1)
            for m in range(4):
                last = mm(psx[:, 4 + m, :], poolw[:, m, :], apad[:, m, :, APAD:APAD + TG])
            last.then_inc(pool_done, 1)
            pe.wait_ge(mix_ready, 2)
            for n in range(2):
                key = ("out", 0, n)
                landed(pe, key)
                w = wtile(key)
                for m in range(4):
                    for k in range(DC):
                        last = mm(psx[:, 4 * n + m, :], w[:, k, m * P:(m + 1) * P], mixT[:, k, :],
                                  k == 0, k == DC - 1)
                    if m == 1:
                        last.then_inc(y_done[0], 1)
                last.then_inc(tiles_used, 1)
            norm_sums(1)

            def moe(l, n):
                for k in range(DC):
                    pe.wait_ge(h_ready[n], k + 1)
                for g in range(2):
                    for k in range(DC):
                        last = mm(ps[:, 6, 256 + 32 * g:276 + 32 * g], hT[:, k, g * TG:(g + 1) * TG],
                                  wr[:, l, k, :], k == 0, k == DC - 1)
                last.then_inc(route_done[l], 1)
                for b in range(4):
                    mm(ps[:, b, :], zrow[0:1, 0:P], zrow[0:1, :])
                pe.wait_ge(gate_ready[l], 1)
                for e in range(NE):
                    if e >= 8 and e % 2 == 0:
                        pe.wait_ge(act_ready[l], (e - 8) // 2 + 1)
                    for g in range(2):
                        at = (e % 2) * NT + g * TG
                        last = mm(ps[:, 4 + (e // 2) % 4, at:at + TG],
                                  gate[:, g, e:e + 1].to_broadcast([P, P]), ident)
                    if e % 2:
                        last.then_inc(gbc_done[l], 1)
                first = TILE["w1", l, 0]
                with pe.Fori(0, NE // 2) as i:
                    for u in range(2):
                        n1, n3, n2 = (first + 3 * u + j for j in range(3))
                        w1, w3, w2 = (ring[:, t % SLOTS, :].rearrange("p (k n) -> p k n", k=k)
                                      for t, k in ((n1, DC), (n3, DC), (n2, FC)))
                        pe.wait_ge(slot_full[n1 % SLOTS], i * 16 + 16 * (n1 // SLOTS + 1))
                        pe.wait_ge(slot_full[n3 % SLOTS], i * 16 + 16 * (n3 // SLOTS + 1))
                        for m in range(FC):
                            pe.wait_ge(act_ready[l], i * 8 + (4 * u + m + 5))
                            for w, at in ((w1, 0), (w3, NT)):
                                for k in range(DC):
                                    last = mm(ps[:, 4 + m, at:at + NT], w[:, k, m * P:(m + 1) * P], hT[:, k, :],
                                              k == 0, k == DC - 1)
                            last.then_inc(hid_done[l], 1)
                        pe.wait_ge(slot_full[n2 % SLOTS], i * 16 + 16 * (n2 // SLOTS + 1))
                        for f in range(FC):
                            pe.wait_ge(act_ready[l], i * 8 + (8 + 4 * u + f + 1))
                            for m in range(DC):
                                last = mm(psx[:, m, :], w2[:, f, m * P:(m + 1) * P], actT[:, u, f, :], False, True)
                                if f == 0 and m == 0:
                                    last.then_inc(tiles_used, 2)
                        last.then_inc(tiles_used, 1)

            moe(0, 1)
            ada(1, (0, 1))
            norm_sums(2)

            for h in range(2):
                for half, j in ((0, 0), (1, 2)):
                    key = ("cw1", 1, h + j)
                    landed(pe, key)
                    w = wtile(key)
                    for m in range(4):
                        b = (4 * h + m) % 7
                        if half == 0 and 4 * h + m == 7:
                            pe.wait_ge(u_ready, 1)
                        for k in range(DC):
                            if h == 0 and half == 0 and m == 0:
                                pe.wait_ge(h_ready[2], k + 1)
                            last = mm(ps[:, b, half * NT:(half + 1) * NT], w[:, k, m * P:(m + 1) * P],
                                      hT[:, k, :], k == 0, k == DC - 1)
                        if half and m < 3:
                            last.then_inc(glu_done, 1)
                    last.then_inc(tiles_used, 1)
            ada(1, (2, 3, 4, 5))
            pe.wait_ge(conv_ready, 1)
            column_sums(ps[:, 6, 0:NT], conv, conv_ready, lambda k: 1, mean_done)
            column_sums(ps[:, 6, NT:2 * NT], sq, csq_ready, lambda k: k + 1, var_done)
            for n in range(2):
                key = ("cw2", 1, n)
                landed(pe, key)
                w = wtile(key)
                for m in range(4):
                    for k in range(DC):
                        if n == 0 and m == 0:
                            pe.wait_ge(cs_ready, k + 1)
                        last = mm(psx[:, 4 * n + m, :], w[:, k, m * P:(m + 1) * P], hT[:, k, :],
                                  k == 0, k == DC - 1)
                    if m == 1:
                        last.then_inc(y_done[2], 1)
                last.then_inc(tiles_used, 1)
            norm_sums(3)
            moe(1, 3)
            norm_sums(4)
            pe.wait_ge(hpre_ready[4], DC)
            for g in range(2):
                for k in range(DC):
                    last = nc.tensor.transpose(ps[:, 2 * g + k // 4, (k % 4) * P:(k % 4 + 1) * P],
                                               hT[:, k, g * TG:(g + 1) * TG], ident)
                last.then_inc(out_t, 1)

        @block.scalar
        def _(act):
            def vrow(at, src):
                n = src.shape[0] // P
                act.dma_start(rows_v[at:at + n, :], src.rearrange("(r p) -> r p", p=P)).then_inc(s_rows, 16)

            act.dma_start(cst[:, :], shape_consts).then_inc(s_cst, 16)
            vrow(V_CCTX, c_ctx)
            vrow(V_C, c[0])
            act.dma_start(rows_v[V_NMIX:V_NMIX + 16, :],
                          norm_mix_g.rearrange("l (r p) -> (l r) p", p=P)).then_inc(s_rows, 16)
            act.dma_start(rows_v[V_NFFN:V_NFFN + 16, :],
                          norm_ffn_g.rearrange("l (r p) -> (l r) p", p=P)).then_inc(s_rows, 16)
            vrow(V_FIN, final_g)
            vrow(V_CB1, conv_b1[0])
            vrow(V_DWB, conv_dw_b[0])
            vrow(V_LNG, conv_ln_g[0])
            vrow(V_LNB, conv_ln_b[0])
            vrow(V_CB2, conv_b2[0])
            vrow(V_PSC, pool_scale[0])
            act.dma_start(rows_b[:, :], b_ada.rearrange("l (r p) -> (l r) p", p=P)).then_inc(s_rows, 16)
            act.dma_start(rows_dw[:, :], conv_dw[0]).then_inc(s_rows, 16)
            act.dma_start(rows_r[0:64, :],
                          router_exp.rearrange("l g (c p) e -> (l g c) (p e)", p=P)).then_inc(s_rows, 16)
            act.dma_start(rows_r[64:80, :],
                          router_grp.rearrange("l (c p) e -> (l c) (p e)", p=P)).then_inc(s_rows, 16)
            act.dma_start(sinkrow[:, :], attn_sink).then_inc(s_rows, 16)
            act.dma_start(cktok[:, :], cache_k[0, 0].rearrange("t h d -> t (h d)")).then_inc(s_kv, 16)
            act.dma_start(cvtok[:, :], cache_v[0, 0].rearrange("t h d -> t (h d)")).then_inc(s_kv, 16)
            act.dma_start(poolw[:, :, :], pool_w[0].rearrange("g c d -> c g d")).then_inc(s_kv, 16)

            act.wait_ge(s_vec, 1)
            nc.scalar.activation(csil[:, :, :], vec[:, V_CCTX:V_CCTX + 2 * DC].rearrange("p (g k) -> p k g", g=2),
                                 ACT.Silu).then_inc(s_csil, 1)

            def norm_act(n, shift):
                for k in range(DC):
                    act.wait_ge(x_ready[n], k + 1)
                    nc.scalar.activation(sq[:, k, :], xT[:, k, :], ACT.Square).then_inc(sq_ready[n], 1)
                act.wait_ge(ss_done[n], 1)
                nc.scalar.activation(root[:, :], ps[:, 6, 0:NT], ACT.Sqrt, bias=eps[:, 0:1],
                                     scale=1.0 / D).then_inc(root_ready[n], 1)
                if shift is None:
                    return
                for k in range(DC):
                    act.wait_ge(hpre_ready[n], k + 1)
                    for g in range(2):
                        last = nc.scalar.activation(hT[:, k, g * TG:(g + 1) * TG], hT[:, k, g * TG:(g + 1) * TG],
                                                    ACT.Identity, bias=mod[:, shift[0], shift[1] + k, g:g + 1])
                    last.then_inc(h_ready[n], 1)

            act.wait_ge(s_fill, 1)
            norm_act(0, (0, 0))
            used(act, ("in", 0, 0))
            act.wait_ge(s_fill, 2)
            nc.scalar.activation(apad[:, :, :, APAD:APAD + TG],
                                 psx[:, 0:4, :].rearrange("p c (g t) -> p c g t", g=2), ACT.Copy).then_inc(a_ready, 1)
            act.wait_ge(qkv_done, 1)
            nc.scalar.activation(kvctx[:, :], ps[:, 5, 0:2 * P], ACT.Copy).then_inc(kv_ready, 1)
            act.wait_ge(kv_ready, 1)
            act.dma_start(state_k[0, 0].rearrange("t h d -> t (h d)"), kvctx[:, 0:P]).then_inc(s_out, 16)
            act.dma_start(state_v[0, 0].rearrange("t h d -> t (h d)"), kvctx[:, P:2 * P]).then_inc(s_out, 16)
            act.wait_ge(nmax_ready, 1)
            for h in range(NH):
                nc.scalar.activation(probs[:, h, :], ps[:, h // 4, (h % 4) * P:(h % 4 + 1) * P], ACT.Exp,
                                     bias=nmax[:, 0, h:h + 1], scale=SCALE,
                                     accum_out=rsum[:, 0, h:h + 1]).then_inc(exp_ready, 1)
            for h in range(NH):
                nc.scalar.activation(probs[:, 8 + 2 * h:10 + 2 * h, :],
                                     ps[:, 2 + h // 2, (h % 2) * NT:(h % 2 + 1) * NT].rearrange(
                                         "p (s k) -> p s k", s=2), ACT.Exp,
                                     bias=nmax[:, 1, h:h + 1], scale=SCALE,
                                     accum_out=rsum[:, 1, h:h + 1]).then_inc(exp_ready, 1)
            act.wait_ge(nmax_ready, 2)
            nc.scalar.activation(esink[:, :, :], esink[:, :, :], ACT.Exp).then_inc(exp_ready, 1)
            for b in (1, 3, 5):
                act.wait_ge(pt_done, b + 1)
                nc.scalar.activation(probsT[:, 4 * b:4 * b + 4, :], ps[:, b, :], ACT.Copy).then_inc(pt_ready, 1)
            act.wait_ge(pv_done, 1)
            nc.scalar.activation(mixT[:, 4:8, :], psx[:, 0:4, :], ACT.Copy).then_inc(mix_ready, 1)
            norm_act(1, (0, 24))

            def moe_act(l):
                act.wait_ge(gexp_in[l], 1)
                nc.scalar.activation(rs[:, 2:4, :], rs[:, 0:2, :], ACT.Exp).then_inc(gexp_out[l], 1)
                nc.scalar.activation(rg[:, 1], rg[:, 0], ACT.Exp).then_inc(gexp_out[l], 1)
                with act.Fori(0, NE // 2) as i:
                    for u in range(2):
                        for m in range(FC):
                            act.wait_ge(hid_done[l], i * 8 + (4 * u + m + 1))
                            act.wait_ge(act_ready[l], i * 8 + (4 * u + m + 5))
                            nc.scalar.activation(sil[:, m, :], ps[:, 4 + m, 0:NT], ACT.Silu).then_inc(sil_ready[l], 1)

            moe_act(0)
            norm_act(2, (1, 0))
            for m in range(DC):
                if m % 4 == 3:
                    used(act, ("cw1", 1, 2 + m // 4))
                else:
                    act.wait_ge(glu_done, 3 * (m // 4) + m % 4 + 1)
                nc.scalar.activation(sq[:, m, :], ps[:, m % 7, NT:2 * NT], ACT.Sigmoid,
                                     bias=vec[:, V_CB1 + DC + m:V_CB1 + DC + m + 1]).then_inc(sig_ready, 1)
            act.wait_ge(mean_done, 1)
            nc.scalar.activation(mean[:, :], ps[:, 6, 0:NT], ACT.Copy, scale=1.0 / D).then_inc(mean_ready, 1)
            for k in range(DC):
                act.wait_ge(cent_ready, k + 1)
                nc.scalar.activation(sq[:, k, :], conv[:, k, :], ACT.Square).then_inc(csq_ready, 1)
            act.wait_ge(var_done, 1)
            nc.scalar.activation(root[:, :], ps[:, 6, NT:2 * NT], ACT.Sqrt, bias=eps[:, 0:1],
                                 scale=1.0 / D).then_inc(croot_ready, 1)
            for k in range(DC):
                act.wait_ge(cn_ready, k + 1)
                nc.scalar.activation(hT[:, k, :], conv[:, k, :], ACT.Silu, bias=vec[:, V_LNB + k:V_LNB + k + 1],
                                     scale=vec[:, V_LNG + k:V_LNG + k + 1]).then_inc(cs_ready, 1)
            for k in range(DC):
                product(act, y_done[2], "cw2", 1, k)
                nc.scalar.activation(sq[:, k, :], psx[:, k, :], ACT.Identity,
                                     bias=vec[:, V_CB2 + k:V_CB2 + k + 1]).then_inc(yb_ready, 1)
            norm_act(3, (1, 24))
            moe_act(1)
            norm_act(4, None)
            for g in range(2):
                act.wait_ge(out_t, g + 1)
                nc.scalar.activation(xtok[:, g, 0:512], ps[:, 2 * g, :], ACT.Copy).then_inc(out_ready[g], 1)

        @block.gpsimd
        def _(pool):
            nc.gpsimd.memset(ones[:, :], 1.0)
            nc.gpsimd.memset(eps[:, :], EPS)
            nc.gpsimd.memset(zrow[:, :], 0.0).then_inc(s_fill, 1)
            nc.gpsimd.memset(apad[:, :, :, :], 0.0).then_inc(s_fill, 1)
            pool.wait_ge(a_ready, 1)
            src, at = apad, 0
            for n in range(4):
                step = 1 << n
                length = AL - 2 * step + 1
                dst = asum[:, n % 2]
                nc.gpsimd.tensor_tensor(dst[:, n:4, :, 0:length], src[:, n:4, :, 0:length],
                                        src[:, n:4, :, step:step + length], ALU.add).then_inc(s_pool, 1)
                pool.wait_ge(s_pool, 3 * n + 1)
                lo = APAD - WINDOWS[n] // 2
                nc.gpsimd.tensor_tensor(mean4[:, :, :], dst[:, n, :, lo:lo + TG],
                                        icnt[:, n:n + 1, :].to_broadcast([P, 2, TG]), ALU.mult).then_inc(s_pool, 1)
                pool.wait_ge(s_pool, 3 * n + 2)
                last = nc.gpsimd.tensor_tensor(apad[:, n, :, APAD:APAD + TG], mean4[:, :, :],
                                               apad[:, n, :, APAD:APAD + TG], ALU.subtract).then_inc(s_pool, 1)
                pool.wait_ge(s_pool, 3 * n + 3)
                src = dst
            pool.sem_inc(pooled_ready, 1)

            for l in range(2):
                with pool.Fori(0, NE // 2) as i:
                    for u in range(2):
                        for m in range(FC):
                            pool.wait_ge(sil_ready[l], i * 8 + (4 * u + m + 1))
                            pool.wait_ge(act_ready[l], i * 8 + (4 * u + m + 5))
                            pool.sem_inc(gate_turns, 1)
                            nc.gpsimd.tensor_tensor(gated[:, m, :], sil[:, m, :],
                                                    gatebc[:, bass.ds(i * 2 + u, 1), :].rearrange("p o t -> p (o t)"),
                                                    ALU.mult).then_inc(gated_ready[l], 1)

        @block.vector
        def _(dve):
            chain = [0]
            V = nc.vector

            def link(ins):
                chain[0] += 1
                ins.then_inc(s_dve, 1)
                dve.wait_ge(s_dve, chain[0])

            def take_mod(l, p0, p1):
                used(dve, ("ada", l, 2 * p1 - 1))
                a, b = 8 * p0, 8 * p1
                link(V.tensor_tensor(mod[:, l, a:b, :], ps_ada[:, l, a:b, :],
                                     bias[:, l, a:b].unsqueeze(2).to_broadcast([P, b - a, 2]), ALU.add))
                for which, p, v in ((0, 1, V_NMIX), (1, 4, V_NFFN)):
                    if p0 <= p < p1:
                        g = vec[:, v + DC * l:v + DC * (l + 1)].unsqueeze(2).to_broadcast([P, DC, 2])
                        link(V.scalar_tensor_tensor(out=gain[:, l, which], in0=mod[:, l, 8 * p:8 * p + 8, :],
                                                    scalar=1.0, in1=g, op0=ALU.add, op1=ALU.mult))
                dve.sem_inc(mod_taken, 1)

            def norm_dve(n, g_of):
                dve.wait_ge(root_ready[n], 1)
                link(V.reciprocal(rstd[:, :], root[:, :]))
                for k in range(DC):
                    for g in range(2):
                        t = slice(g * TG, (g + 1) * TG)
                        last = V.scalar_tensor_tensor(out=hT[:, k, t], in0=xT[:, k, t], scalar=g_of(k, g),
                                                      in1=rstd[:, t], op0=ALU.mult, op1=ALU.mult)
                    last.then_inc(hpre_ready[n], 1)

            def residual(n, y, l, part, ready):
                for k in range(DC):
                    ready(k)
                    for g in range(2):
                        t = slice(g * TG, (g + 1) * TG)
                        last = V.scalar_tensor_tensor(out=xT[:, k, t], in0=y[:, k, t],
                                                      scalar=mod[:, l, 8 * part + k, g:g + 1],
                                                      in1=xT[:, k, t], op0=ALU.mult, op1=ALU.add)
                    last.then_inc(x_ready[n], 1)

            for k in range(DC):
                dve.wait_ge(s_xt, k // 2 + 1)
                V.tensor_copy(xT[:, k, :], psx[:, k, :]).then_inc(x_ready[0], 1)
            dve.wait_ge(s_vt, 1)
            V.tensor_copy(vec[:, :], ps[:, 4, 0:V_ROWS]).then_inc(s_vec, 1)
            V.tensor_copy(bias[:, :, :], ps[:, 4, 128:224].rearrange("p (l m) -> p l m", l=2))
            V.tensor_copy(dw[:, :, :], ps[:, 5, 0:DC * TAPS].rearrange("p (c t) -> p c t", c=DC))
            V.tensor_copy(sink[:, :], ps[:, 4, 256:256 + NH])
            pr = ps[:, 6, 0:320].rearrange("p (e r) -> p e r", e=4)
            for l in range(2):
                for g in range(4):
                    V.tensor_copy(wr[:, l, :, 4 * g:4 * g + 4],
                                  pr[:, :, 32 * l + 8 * g:32 * l + 8 * g + 8].rearrange("p e c -> p c e"))
                last = V.tensor_copy(wr[:, l, :, 16:20], pr[:, :, 64 + 8 * l:72 + 8 * l].rearrange("p e c -> p c e"))
            last.then_inc(s_prep, 1)
            dve.wait_ge(s_prep, 1)
            take_mod(0, 0, 2)
            norm_dve(0, lambda k, g: gain[:, 0, 0, k, g:g + 1])

            dve.wait_ge(qkv_done, 1)
            V.tensor_copy(qT, psx[:, 4:8, :]).then_inc(qraw_ready, 1)
            V.tensor_copy(kT[:, 0, :], ps[:, 4, 0:NT])
            V.tensor_copy(vlat[:, :], ps[:, 4, NT:NT + P])
            V.tensor_copy(ckT[:, 0, :], ps[:, 4, NT + P:NT + 2 * P]).then_inc(qraw_ready, 1)
            dve.wait_ge(qraw_ready, 2)
            V.tensor_copy(kT[0:64, 1, 0:TG], kT[64:128, 0, 0:TG])
            V.tensor_copy(kT[64:128, 1, 0:TG], kT[0:64, 0, 0:TG])
            V.tensor_copy(ckT[0:64, 1, :], ckT[64:128, 0, :])
            V.tensor_copy(ckT[64:128, 1, :], ckT[0:64, 0, :])
            V.tensor_tensor(rt[:, 0:4, :], qT[:, :, TG:NT], cos.unsqueeze(1).to_broadcast([P, 4, TG]), ALU.mult)
            link(V.tensor_tensor(rt[:, 4, :], kT[:, 0, TG:NT], cos, ALU.mult))
            dve.wait_ge(rot_done, 1)
            V.tensor_tensor(rt2[:, 0:4, :], ps[:, 6, :].rearrange("p (c t) -> p c t", c=4),
                            sin.unsqueeze(1).to_broadcast([P, 4, TG]), ALU.mult)
            link(V.tensor_tensor(rt2[:, 4, :], ps[:, 4, 0:P], sin, ALU.mult))
            V.tensor_tensor(qT[:, :, TG:NT], rt[:, 0:4, :], rt2[:, 0:4, :], ALU.add).then_inc(qk_ready, 1)
            link(V.tensor_tensor(kT[:, 0, TG:NT], rt[:, 4, :], rt2[:, 4, :], ALU.add))
            V.tensor_copy(kT[0:64, 1, TG:NT], kT[64:128, 0, TG:NT])
            V.tensor_copy(kT[64:128, 1, TG:NT], kT[0:64, 0, TG:NT]).then_inc(qk_ready, 1)
            take_mod(0, 2, 4)

            dve.wait_ge(scores_done, 1)
            V.tensor_reduce(smax[:, 0, :], ps[:, 0:2, :].rearrange("p b (h k) -> p (b h) k", h=4), AX.X, ALU.max)
            link(V.tensor_reduce(smax[:, 1, :], ps[:, 2:6, :].rearrange("p b (h k) -> p (b h) k", h=2), AX.X, ALU.max))
            link(V.scalar_tensor_tensor(out=nmax[:, :, :], in0=smax[:, :, :], scalar=SCALE,
                                        in1=sink[:, :].unsqueeze(1).to_broadcast([P, 2, NH]),
                                        op0=ALU.mult, op1=ALU.max))
            V.tensor_scalar(nmax[:, :, :], nmax[:, :, :], -1.0, None, ALU.mult).then_inc(nmax_ready, 1)
            dve.wait_ge(nmax_ready, 1)
            V.tensor_tensor(esink[:, :, :], nmax[:, :, :], sink[:, :].unsqueeze(1).to_broadcast([P, 2, NH]),
                            ALU.add).then_inc(nmax_ready, 1)
            dve.wait_ge(exp_ready, 17)
            link(V.tensor_tensor(rden[:, :, :], rsum[:, :, :], esink[:, :, :], ALU.add))
            link(V.reciprocal(rden[:, :, :], rden[:, :, :]))
            for h in range(NH):
                last = V.tensor_scalar(probs[:, h, :], probs[:, h, :], rden[:, 0, h:h + 1], None, ALU.mult)
            last.then_inc(probs_ready, 1)
            for h in range(NH):
                last = V.tensor_scalar(probs[:, 8 + 2 * h:10 + 2 * h, :], probs[:, 8 + 2 * h:10 + 2 * h, :],
                                       rden[:, 1, h:h + 1], None, ALU.mult)
                if h % 4 == 3:
                    last.then_inc(probs_ready, 1)
            take_mod(0, 4, 6)
            for b in (0, 2, 4):
                dve.wait_ge(pt_done, b + 1)
                V.tensor_copy(probsT[:, 4 * b:4 * b + 4, :], ps[:, b, :].rearrange("p (n k) -> p n k", n=4)).then_inc(
                    pt_ready, 1)
            dve.wait_ge(pool_done, 1)
            for m in range(4):
                last = V.tensor_scalar(mixT[:, m, :], psx[:, 4 + m, :], vec[:, V_PSC + m:V_PSC + m + 1], None,
                                       ALU.mult)
            last.then_inc(mix_ready, 1)
            residual(1, psx, 0, 2, lambda k: product(dve, y_done[0], "out", 0, k))
            norm_dve(1, lambda k, g: gain[:, 0, 1, k, g:g + 1])

            def first_match(out, eq, a, b):
                link(V.tensor_copy(a, eq))
                link(V.tensor_tensor(a[:, :, 1:4], eq[:, :, 1:4], eq[:, :, 0:3], ALU.add))
                link(V.tensor_copy(b, a))
                link(V.tensor_tensor(b[:, :, 2:4], a[:, :, 2:4], a[:, :, 0:2], ALU.add))
                link(V.scalar_tensor_tensor(out=out, in0=b, scalar=1.0, in1=eq, op0=ALU.is_equal, op1=ALU.mult))

            def wide(v, n=4):
                return v.unsqueeze(2).to_broadcast([P, 2, n])

            def route(l):
                dve.wait_ge(route_done[l], 1)
                link(V.tensor_copy(lg[:, :, :], ps[:, 6, 256:320].rearrange("p (g j) -> p g j", g=2)[:, :, 0:20]))
                gl = lg[:, :, 16:20]
                gmax, m1, m2, gsum, t0 = rs[:, 4], rs[:, 5], rs[:, 6], rs[:, 7], rs[:, 8]
                link(V.tensor_reduce(gmax, gl, AX.X, ALU.max))
                link(V.tensor_tensor(rg[:, 0], gl, wide(gmax), ALU.subtract))
                link(V.tensor_tensor(rg[:, 2], gl, wide(gmax), ALU.is_equal))
                first_match(rg[:, 3], rg[:, 2], rg[:, 4], rg[:, 5])
                sel = rg[:, 3].unsqueeze(3).to_broadcast([P, 2, 4, 4])
                r4 = r1[:, :, :].rearrange("p g (a e) -> p g a e", a=4)
                link(V.tensor_tensor(r4, lg[:, :, 0:16].rearrange("p g (a e) -> p g a e", a=4), sel, ALU.mult))
                link(V.tensor_reduce(rg[:, 6], r4.rearrange("p g a e -> p g e a"), AX.X, ALU.add))
                link(V.tensor_reduce(m1, rg[:, 6], AX.X, ALU.max))
                link(V.tensor_tensor(rg[:, 2], rg[:, 6], wide(m1), ALU.is_equal))
                first_match(rg[:, 7], rg[:, 2], rg[:, 4], rg[:, 5])
                link(V.scalar_tensor_tensor(out=rg[:, 8], in0=rg[:, 7], scalar=-1e30, in1=rg[:, 6],
                                            op0=ALU.mult, op1=ALU.add))
                link(V.tensor_reduce(m2, rg[:, 8], AX.X, ALU.max))
                link(V.tensor_tensor(rg[:, 2], rg[:, 8], wide(m2), ALU.is_equal))
                first_match(rg[:, 9], rg[:, 2], rg[:, 4], rg[:, 5])
                V.tensor_tensor(rs[:, 0], m1, m1, ALU.subtract)
                V.tensor_tensor(rs[:, 1], m2, m1, ALU.subtract).then_inc(gexp_in[l], 1)
                dve.wait_ge(gexp_out[l], 2)
                link(V.tensor_reduce(gsum, rg[:, 1], AX.X, ALU.add))
                link(V.tensor_tensor(t0, rs[:, 2], rs[:, 3], ALU.add))
                link(V.tensor_tensor(t0, t0, gsum, ALU.mult))
                link(V.reciprocal(t0, t0))
                link(V.tensor_tensor(rs[:, 9], rs[:, 2], t0, ALU.mult))
                link(V.tensor_tensor(rs[:, 10], rs[:, 3], t0, ALU.mult))
                link(V.tensor_tensor(rg[:, 7], rg[:, 7], wide(rs[:, 9]), ALU.mult))
                link(V.tensor_tensor(rg[:, 9], rg[:, 9], wide(rs[:, 10]), ALU.mult))
                link(V.tensor_tensor(rg[:, 10], rg[:, 7], rg[:, 9], ALU.add))
                V.tensor_tensor(gate[:, :, :].rearrange("p g (a e) -> p g a e", a=4), sel,
                                rg[:, 10].unsqueeze(2).to_broadcast([P, 2, 4, 4]), ALU.mult).then_inc(gate_ready[l], 1)
                for b in range(NE // 2):
                    dve.wait_ge(gbc_done[l], b + 1)
                    V.tensor_copy(gatebc[:, 2 * b:2 * b + 2, :],
                                  ps[:, 4 + b % 4, :].rearrange("p (e t) -> p e t", e=2)).then_inc(act_ready[l], 1)

            def experts(l):
                first = TILE["w1", l, 0]
                with dve.Fori(0, NE // 2) as i:
                    for u in range(2):
                        dve.wait_ge(tiles_used, i * 6 + (first + 3 * u - 3))
                        for m in range(FC):
                            dve.wait_ge(gated_ready[l], i * 8 + (4 * u + m + 1))
                            V.tensor_tensor(actT[:, u, m, :], gated[:, m, :], ps[:, 4 + m, NT:2 * NT],
                                            ALU.mult).then_inc(act_ready[l], 1)
                used(dve, ("w2", l, NE - 1))

            route(0)
            experts(0)
            residual(2, psx, 0, 5, lambda k: None)
            take_mod(1, 0, 2)
            norm_dve(2, lambda k, g: gain[:, 1, 0, k, g:g + 1])

            link(V.memset(upad[:, :, :, :], 0.0))
            for m in range(DC):
                dve.wait_ge(sig_ready, m + 1)
                V.scalar_tensor_tensor(out=upad[:, m, :, HALF:HALF + TG],
                                       in0=ps[:, m % 7, 0:NT].rearrange("p (g t) -> p g t", g=2),
                                       scalar=vec[:, V_CB1 + m:V_CB1 + m + 1],
                                       in1=sq[:, m, :].rearrange("p (g t) -> p g t", g=2),
                                       op0=ALU.add, op1=ALU.mult).then_inc(u_ready, 1)
            dve.wait_ge(u_ready, DC)
            cv = [conv[:, k, :].rearrange("p (g t) -> p g t", g=2) for k in range(DC)]
            for k in range(DC):
                V.tensor_scalar(cv[k], upad[:, k, :, 0:TG], dw[:, k, 0:1], vec[:, V_DWB + k:V_DWB + k + 1],
                                ALU.mult, ALU.add).then_inc(tap_done, 1)
            with dve.Fori(1, TAPS) as t:
                for k in range(DC):
                    dve.wait_ge(tap_done, t * DC + (k + 1 - DC))
                    V.scalar_tensor_tensor(out=cv[k], in0=upad[:, k, :, bass.ds(t, TG)], scalar=dw[:, k, bass.ds(t, 1)],
                                           in1=cv[k], op0=ALU.mult, op1=ALU.add).then_inc(tap_done, 1)
            dve.wait_ge(tap_done, TAPS * DC)
            dve.sem_inc(conv_ready, 1)
            take_mod(1, 2, 6)
            dve.wait_ge(mean_ready, 1)
            for k in range(DC):
                V.tensor_tensor(conv[:, k, :], conv[:, k, :], mean[:, :], ALU.subtract).then_inc(cent_ready, 1)
            dve.wait_ge(croot_ready, 1)
            link(V.reciprocal(rstd[:, :], root[:, :]))
            for k in range(DC):
                V.tensor_tensor(conv[:, k, :], conv[:, k, :], rstd[:, :], ALU.mult).then_inc(cn_ready, 1)
            residual(3, sq, 1, 2, lambda k: dve.wait_ge(yb_ready, k + 1))
            norm_dve(3, lambda k, g: gain[:, 1, 1, k, g:g + 1])
            route(1)
            experts(1)
            residual(4, psx, 1, 5, lambda k: None)
            norm_dve(4, lambda k, g: vec[:, V_FIN + k:V_FIN + k + 1])
            for g in range(2):
                dve.wait_ge(out_t, g + 1)
                V.tensor_copy(xtok[:, g, 512:1024], ps[:, 2 * g + 1, :]).then_inc(out_ready[g], 1)


def shape_constants():
    t = np.zeros((P, C_W), np.float32)
    t[:, C_ID:C_ID + P] = np.eye(P, dtype=np.float32)
    axis, half = HD // 2, HD // 4
    for d in range(P):
        j = d % axis
        if j < half:
            t[d + half, C_ROT + d] = -1.0
        else:
            t[d - half, C_ROT + d] = 1.0
    inv = (10000.0 ** (-np.arange(0, axis, 2, dtype=np.float32) / axis)).astype(np.float32)
    tok = np.arange(TG)
    pos = {0: (tok // 64).astype(np.float32), 1: (tok % 64).astype(np.float32)}
    for d in range(P):
        ang = pos[(d % HD) // axis] * inv[d % half]
        t[d, C_COS:C_COS + TG] = np.cos(ang)
        t[d, C_SIN:C_SIN + TG] = np.sin(ang)
    for w, size in enumerate(WINDOWS):
        lo, hi = size // 2, size - size // 2 - 1
        count = np.clip(tok + hi + 1, 0, TG) - np.clip(tok - lo, 0, TG)
        t[:, C_CNT + w * P:C_CNT + (w + 1) * P] = (1.0 / count).astype(np.float32)
    return t


INPUTS = ("x_prompt", "x_sample", "cache_k", "cache_v", "c", "c_ctx", "w_ada", "b_ada", "norm_mix_g",
          "norm_ffn_g", "w_in_ab", "pool_w", "pool_scale", "attn_sink", "w_out_ab", "conv_w1", "conv_b1",
          "conv_dw", "conv_dw_b", "conv_ln_g", "conv_ln_b", "conv_w2", "conv_b2", "router_grp", "router_exp",
          "moe_w1", "moe_w3", "moe_w2", "final_g")
OUTPUTS = (("y_prompt", (1, TG, D)), ("y_sample", (1, TG, D)), ("state_k", (1, 1, TG, 2, HD)),
           ("state_v", (1, 1, TG, 2, HD)))


def kernel(**inputs):
    import concourse.bacc as bacc
    from concourse.bass_utils import run_bass_kernel_spmd

    nc = bacc.Bacc("TRN2", target_bir_lowering=False, num_devices=1)
    arrays, args = {}, []
    for name in INPUTS:
        a = np.ascontiguousarray(inputs[name])
        arrays[f"in_{name}"] = a
        args.append(nc.dram_tensor(f"in_{name}", a.shape, mybir.dt.from_np(a.dtype), kind="ExternalInput").ap())
    arrays["in_shape_consts"] = shape_constants()
    args.append(nc.dram_tensor("in_shape_consts", (P, C_W), F32, kind="ExternalInput").ap())
    for name, shape in OUTPUTS:
        args.append(nc.dram_tensor(f"out_{name}", shape, F32, kind="ExternalOutput").ap())
    backbone(nc, *args)
    result = run_bass_kernel_spmd(nc, [arrays], core_ids=[0])
    return tuple(result.results[0][f"out_{name}"] for name, _ in OUTPUTS)
```

```python
from contextlib import ExitStack

import numpy as np

import concourse.bass as bass
from concourse import mybir

P = 128
ALU = mybir.AluOpType
ACT = mybir.ActivationFunctionType
F32 = mybir.dt.float32
AX = mybir.AxisListType

D = 1024
DC = D // P
TG = 128
NT = 2 * TG
HD = 64
NH = 8
NE = 16
FF = 512
FC = FF // P
EPS = 1e-6
SCALE = HD ** -0.5
TAPS = 31
HALF = TAPS // 2
UL = TG + 2 * HALF
WINDOWS = (2, 4, 8, 16)
APAD = 8
AL = TG + 2 * APAD
DVE_CHUNKS = 6
PE_CHUNKS = tuple(range(DVE_CHUNKS, DC))
DIAGS = 16
SLOTS = 6
PAIRS = NE // 2
CAP = 64
LIMIT = CAP + 0.5
TW = 512

C_ID, C_ROT, C_COS, C_SIN, C_CNT, C_SEL, C_IOTA, C_UPPER = 0, 128, 256, 384, 512, 1024, 1026, 1090
C_W = 1218

V_NMIX, V_NFFN, V_FIN, V_CB1, V_DWB, V_LNG, V_LNB, V_CB2, V_PSC, V_CCTX, V_C = (
    0, 16, 32, 40, 56, 64, 72, 80, 88, 92, 100)
V_ROWS = 108


def weight_stream():
    ada = lambda l, parts: [("ada", l, 2 * p + h) for p in parts for h in range(2)]
    moe = lambda l: [(k, l, 2 * i + u) for i in range(PAIRS) for k in ("w1", "w3", "w2") for u in range(2)]
    return (ada(0, (0, 1)) + [("in", 0, n) for n in range(3)] + ada(0, (2, 3, 4, 5))
            + [("out", 0, n) for n in range(2)] + moe(0)
            + ada(1, (0, 1)) + [("cw1", 1, n) for n in (0, 2, 1, 3)] + ada(1, (2, 3, 4, 5))
            + [("cw2", 1, n) for n in range(2)] + moe(1))


STREAM = weight_stream()
ada_keys = lambda l, parts: [("ada", l, 2 * p + h) for p in parts for h in range(2)]
ADA = {key: n for n, key in enumerate(k for k in STREAM if k[0] == "ada")}
TILE = {key: n for n, key in enumerate(STREAM)}


def backbone(nc, x_prompt, x_sample, cache_k, cache_v, c, c_ctx, w_ada, b_ada, norm_mix_g, norm_ffn_g,
             w_in_ab, pool_w, pool_scale, attn_sink, w_out_ab, conv_w1, conv_b1, conv_dw, conv_dw_b,
             conv_ln_g, conv_ln_b, conv_w2, conv_b2, router_grp, router_exp, moe_w1, moe_w3, moe_w2,
             final_g, shape_consts, y_prompt, y_sample, state_k, state_v):
    with ExitStack() as ctx:
        def sb(name, shape, dt=F32):
            return ctx.enter_context(nc.sbuf_tensor(name, shape, dt))

        def sem(name):
            return ctx.enter_context(nc.semaphore(name))

        ps = ctx.enter_context(nc.psum_tensor("ps", [P, 8, 512], F32))
        psx = ps[:, 0:4, :].rearrange("p b (h t) -> p (b h) t", h=2)
        ps_part = ps[:, 7, :]
        ps_ada = ps[:, 6, 384:480].rearrange("p (m g) -> p m g", g=2)
        ps_norm = ps[:, 5, 0:NT]
        ps_rank = ps[:, 5, NT + 64:NT + 112].rearrange("p (s e) -> p s e", s=3)
        ps_logit = ps[:, 5, NT:NT + 64].rearrange("p (g j) -> p g j", g=2)

        ring = sb("ring", [P, SLOTS, DC * TW])
        cst = sb("cst", [P, C_W])
        ones = sb("ones", [P, P])
        zrow = sb("zrow", [1, 512])
        xtok = sb("xtok", [P, 2, D])
        diag = xtok[:, :, :].rearrange("p g d -> p (g d)").rearrange("p (n q) -> p n q", q=P)
        xT = sb("xT", [P, DC, NT])
        hT = sb("hT", [P, DC, NT])
        sq = sb("sq", [P, DC, NT])
        vec = sb("vec", [P, V_ROWS])
        bias = sb("bias", [P, 2, 48])
        dw = sb("dw", [P, DC, TAPS])
        wr = sb("wr", [P, 2, DC, 20])
        sinkrow = sb("sinkrow", [1, NH])
        sink = sb("sink", [P, NH])
        csil = sb("csil", [P, DC, 32])
        part = sb("part", [P, 2, TW])
        mod = sb("mod", [P, 2, 48, 2])
        gain = sb("gain", [P, 2, 2, DC, 2])
        rstd = sb("rstd", [P, NT])
        root = sb("root", [P, NT])
        mean = sb("mean", [P, NT])
        mixT = hT
        poolw = sb("poolw", [P, 4, P])
        apad = sb("apad", [P, 4, 2, AL])
        asum = sb("asum", [P, 2, 4, 2, AL])
        stage = sb("stage", [P, 4 * NT + 10 * TG])
        qT = stage[:, 0:4 * NT].rearrange("p (c t) -> p c t", c=4)
        rt, rt2 = (stage[:, 4 * NT + 5 * TG * n:4 * NT + 5 * TG * (n + 1)].rearrange(
            "p (c t) -> p c t", c=5) for n in range(2))
        dense_sil = stage[:, 0:4 * NT].rearrange("p (c t) -> p c t", c=4)
        dense_act = stage[:, 4 * NT:8 * NT].rearrange("p (c t) -> p c t", c=4)
        kT = sb("kT", [P, 2, NT])
        ckT = sb("ckT", [P, 2, TG])
        cktok = sb("cktok", [P, P])
        cvtok = sb("cvtok", [P, P])
        kvctx = sb("kvctx", [P, 2 * P])
        vlat = sb("vlat", [P, P])
        smax = sb("smax", [P, 2, NH])
        nmax = sb("nmax", [P, 2, NH])
        rsum = sb("rsum", [P, 2, NH])
        esink = sb("esink", [P, 2, NH])
        rden = sb("rden", [P, 2, NH])
        work = sb("work", [P, 6144])
        rows_v = work[0:V_ROWS, 0:P]
        rows_b = work[0:96, P:2 * P]
        rows_r = work[0:80, 2 * P:6 * P]
        rows_dw = work[0:TAPS, 6 * P:6 * P + D]
        probs = work[:, 0:3072].rearrange("p (n k) -> p n k", k=TG)
        probsT = work[:, 3072:6144].rearrange("p (n k) -> p n k", k=TG)
        upad = work[:, 0:DC * 2 * UL].rearrange("p (c g t) -> p c g t", c=DC, g=2)
        conv = work[:, 2560:2560 + DC * NT].rearrange("p (c t) -> p c t", c=DC)
        pick = work[:, 0:2 * P].rearrange("p (g j) -> p g j", g=2)
        pick_gate = work[:, 2 * P:4 * P].rearrange("p (g j) -> p g j", g=2)
        spread = work[:, 4 * P:6 * P]
        hsel = work[:, 6 * P:14 * P].rearrange("p (k j) -> p k j", k=DC)
        sil = work[:, 14 * P:18 * P]
        hid = work[:, 18 * P:22 * P]
        hidT = work[:, 22 * P:26 * P].rearrange("p (f j) -> p f j", f=FC)
        ysel = work[:, 26 * P:34 * P]
        gate_diag = work[:, 34 * P:38 * P].rearrange("p (n t) -> p n t", n=4)
        gatebc = work[:, 38 * P:42 * P].rearrange("p (u t) -> p u t", u=2)
        htok = xtok
        eps = sb("eps", [P, 1])
        mean4 = sb("mean4", [P, 2, TG])
        lg = sb("lg", [P, 2, 20])
        r1 = sb("r1", [P, 2, 16])
        rg = sb("rg", [P, 12, 2, 4])
        rs = sb("rs", [P, 12, 2])
        gate = sb("gate", [P, 2, NE + 2])
        slot = sb("slot", [P, 2, NE + 2])
        mask = sb("mask", [P, 2, NE])
        crowd = sb("crowd", [P, PAIRS])
        overflow = sb("overflow", [P, PAIRS], mybir.dt.int32)

        ident = cst[:, C_ID:C_ID + P]
        rot = cst[:, C_ROT:C_ROT + P]
        cos = cst[:, C_COS:C_COS + P]
        sin = cst[:, C_SIN:C_SIN + P]
        sel = cst[:, C_SEL:C_SEL + 2]
        iota = cst[:, C_IOTA:C_IOTA + CAP]
        upper = cst[:, C_UPPER:C_UPPER + P]
        icnt = cst[:, C_CNT:C_CNT + 4 * P].rearrange("p (w t) -> p w t", w=4)

        slot_full = [sem(f"slot_full{s}") for s in range(SLOTS)]
        tiles_used = sem("tiles_used")
        s_x = sem("s_x")
        s_cst = sem("s_cst")
        s_rows = sem("s_rows")
        s_rows_conv = sem("s_rows_conv")
        s_kv = sem("s_kv")
        s_fill = sem("s_fill")
        s_xt = sem("s_xt")
        s_vt = sem("s_vt")
        s_prep = sem("s_prep")
        s_vec = sem("s_vec")
        s_csil = sem("s_csil")
        small_issued = sem("small_issued")
        part_done = sem("part_done")
        part_ready = sem("part_ready")
        mod_done = sem("mod_done")
        diag_ready = sem("diag_ready")
        diag_used = sem("diag_used")
        dconv_done = sem("dconv_done")
        dconv_ready = sem("dconv_ready")
        mod_taken = sem("mod_taken")
        x_ready = [sem(f"x_ready{n}") for n in range(5)]
        sq_ready = [sem(f"sq_ready{n}") for n in range(5)]
        ss_done = [sem(f"ss_done{n}") for n in range(5)]
        root_ready = [sem(f"root_ready{n}") for n in range(5)]
        hpre_ready = [sem(f"hpre_ready{n}") for n in range(5)]
        h_ready = [sem(f"h_ready{n}") for n in range(5)]
        y_done = [sem(f"y_done{n}") for n in range(4)]
        s_dve = sem("s_dve")
        s_act = sem("s_act")
        s_pool = sem("s_pool")
        qkv_done = sem("qkv_done")
        a_ready = sem("a_ready")
        qraw_ready = sem("qraw_ready")
        rot_done = sem("rot_done")
        qk_ready = sem("qk_ready")
        kv_ready = sem("kv_ready")
        scores_done = sem("scores_done")
        nmax_ready = sem("nmax_ready")
        exp_ready = sem("exp_ready")
        probs_ready = sem("probs_ready")
        pt_done = sem("pt_done")
        pt_ready = sem("pt_ready")
        pv_done = sem("pv_done")
        pooled_ready = sem("pooled_ready")
        pool_done = sem("pool_done")
        mix_ready = sem("mix_ready")
        glu_done = sem("glu_done")
        sig_ready = sem("sig_ready")
        u_ready = sem("u_ready")
        tap_done = sem("tap_done")
        conv_ready = sem("conv_ready")
        mean_done = sem("mean_done")
        mean_ready = sem("mean_ready")
        cent_ready = sem("cent_ready")
        csq_ready = sem("csq_ready")
        var_done = sem("var_done")
        croot_ready = sem("croot_ready")
        cn_ready = sem("cn_ready")
        cs_ready = sem("cs_ready")
        yb_ready = sem("yb_ready")
        route_done = sem("route_done")
        gexp_in = sem("gexp_in")
        gexp_out = sem("gexp_out")
        gate_ready = sem("gate_ready")
        mask_ready = sem("mask_ready")
        rank_done = sem("rank_done")
        htok_done = sem("htok_done")
        htok_ready = sem("htok_ready")
        pick_ready = sem("pick_ready")
        spread_done = sem("spread_done")
        spread_ready = sem("spread_ready")
        gather_done = sem("gather_done")
        hsel_lo = sem("hsel_lo")
        hsel_hi = sem("hsel_hi")
        sil_ready = sem("sil_ready")
        hid_ready = sem("hid_ready")
        turn_done = sem("turn_done")
        hidT_lo = sem("hidT_lo")
        hidT_hi = sem("hidT_hi")
        ysel_done = sem("ysel_done")
        ysel_lo = sem("ysel_lo")
        ysel_hi = sem("ysel_hi")
        pair_done = sem("pair_done")
        gdiag_ready = sem("gdiag_ready")
        gatebc_done = sem("gatebc_done")
        gatebc_ready = sem("gatebc_ready")
        dense_done = sem("dense_done")
        dense_sil_ready = sem("dense_sil_ready")
        dense_act_ready = sem("dense_act_ready")
        picked = sem("picked")
        gated = sem("gated")
        out_t = sem("out_t")
        out_ready = [sem(f"out_ready{g}") for g in range(2)]
        s_out = sem("s_out")

        def wtile(key):
            w = ring[:, TILE[key] % SLOTS, :]
            return w.rearrange("p (k n) -> p k n", k=FC if key[0] == "w2" else DC)

        def landed(eng, key):
            n = TILE[key]
            eng.wait_ge(slot_full[n % SLOTS], 16 * (n // SLOTS + 1))

        def used(eng, key):
            eng.wait_ge(tiles_used, TILE[key] + 1)

        def product(eng, done, kind, l, k):
            if k % 4 < 2:
                eng.wait_ge(done, k // 4 + 1)
            else:
                used(eng, (kind, l, k // 4))

        SOURCE = {
            "ada": lambda l, n: w_ada[l, :, n * TW:(n + 1) * TW],
            "in": lambda l, n: w_in_ab[0, :, n * TW:min((n + 1) * TW, 1280)],
            "out": lambda l, n: w_out_ab[0, :, n * TW:(n + 1) * TW],
            "cw1": lambda l, n: conv_w1[0, :, n * TW:(n + 1) * TW],
            "cw2": lambda l, n: conv_w2[0, :, n * TW:(n + 1) * TW],
        }
        LAST_IN = ("in", 0, 2)

        block = ctx.enter_context(nc.Block())

        @block.sync
        def _(sp):
            def load(key):
                n = TILE[key]
                src = SOURCE[key[0]](key[1], key[2])
                width = src.shape[1]
                dst = ring[:, n % SLOTS, 0:DC * width].rearrange("p (k n) -> p k n", k=DC)
                if n >= SLOTS:
                    sp.wait_ge(tiles_used, n - SLOTS + 1)
                sp.dma_start(dst, src.rearrange("(k p) n -> p k n", p=P)).then_inc(slot_full[n % SLOTS], 16)

            for g, x in enumerate((x_prompt, x_sample)):
                sp.dma_start(xtok[:, g, :], x[0]).then_inc(s_x, 16)
            sp.wait_ge(small_issued, 2)
            for key in STREAM[:TILE["w1", 0, 0]]:
                load(key)

            def load_experts(l):
                first = TILE["w1", l, 0]
                with sp.Fori(0, PAIRS) as i:
                    for j, w in enumerate((moe_w1, moe_w3, moe_w2)):
                        for u in range(2):
                            n = first + 2 * j + u
                            k = FC if j == 2 else DC
                            dst = ring[:, n % SLOTS, :].rearrange("p (k n) -> p k n", k=k)
                            src = w[l, bass.ds(i * 2 + u, 1)].rearrange("o (k p) n -> p (o k) n", p=P)
                            sp.wait_ge(tiles_used, i * 6 + (n - SLOTS + 1))
                            sp.dma_start(dst, src).then_inc(slot_full[n % SLOTS], 16)

            load_experts(0)
            for key in STREAM[TILE["w2", 0, NE - 1] + 1:TILE["w1", 1, 0]]:
                load(key)
            load_experts(1)
            for g, y in enumerate((y_prompt, y_sample)):
                sp.wait_ge(out_ready[g], 2)
                sp.dma_start(y[0], xtok[:, g, :]).then_inc(s_out, 16)
            sp.wait_ge(s_out, 64)

        @block.tensor
        def _(pe):
            def mm(out, lhsT, rhs, start=True, stop=True):
                return nc.tensor.matmul(out, lhsT, rhs, start=start, stop=stop, skip_group_check=True)

            def ada(l, parts):
                def turn(key):
                    n = ADA[key]
                    pe.wait_ge(part_ready, n + 1)
                    for m in range(4):
                        last = mm(ps_ada[:, 4 * key[2] + m, :], part[:, n % 2, m * P:(m + 1) * P], sel)
                    last.then_inc(mod_done, 1)

                keys = [("ada", l, 2 * p + h) for p in parts for h in range(2)]
                for j, key in enumerate(keys):
                    landed(pe, key)
                    w = wtile(key)
                    if ADA[key]:
                        pe.wait_ge(part_ready, ADA[key])
                    for k in range(DC):
                        q = 32 * (k % 4)
                        last = mm(ps_part[q:q + 32, :], csil[:, k, :], w[:, k, :], k < 4, k >= 4)
                    last.then_inc(tiles_used, 1)
                    if j:
                        turn(keys[j - 1])
                turn(keys[-1])

            def column_sums(dst, src, ready, count, done):
                for k in range(DC):
                    pe.wait_ge(ready, count(k))
                    last = mm(dst, ones[:, :], src[:, k, :], k == 0, k == DC - 1)
                last.then_inc(done, 1)

            def norm_sums(n):
                column_sums(ps_norm, sq, sq_ready[n], lambda k: k + 1, ss_done[n])

            pe.wait_ge(s_cst, 16)
            pe.wait_ge(s_x, 32)
            for k in range(DC):
                for g in range(2):
                    last = nc.tensor.transpose(psx[:, k, g * TG:(g + 1) * TG], xtok[:, g, k * P:(k + 1) * P],
                                               ident)
                if k % 2:
                    last.then_inc(s_xt, 1)
            pe.wait_ge(s_rows, 16 * 9)
            pe.wait_ge(s_rows_conv, 16 * 7)
            nc.tensor.transpose(ps[:, 4, 0:V_ROWS], rows_v[:, :], ident[0:V_ROWS, 0:V_ROWS])
            nc.tensor.transpose(ps[:, 4, 128:224], rows_b[:, :], ident[0:96, 0:96])
            for k in range(DC):
                nc.tensor.transpose(ps[:, 5, k * TAPS:(k + 1) * TAPS], rows_dw[:, k * P:(k + 1) * P],
                                    ident[0:TAPS, 0:TAPS])
            rv = rows_r[:, :].rearrange("r (p e) -> r e p", e=4)
            for e in range(4):
                nc.tensor.transpose(ps[:, 6, e * 80:(e + 1) * 80], rv[:, e, :], ident[0:80, 0:80])
            pe.wait_ge(s_fill, 2)
            mm(ps[:, 4, 256:256 + NH], ones[0:1, :],
               sinkrow[0:1, :].rearrange("o (i r) -> o r i", r=2)).then_inc(s_vt, 1)

            pe.wait_ge(s_csil, 1)
            pe.wait_ge(s_prep, 1)
            norm_sums(0)
            ada(0, (0, 1))

            def project(key, out, ready=None):
                landed(pe, key)
                w = wtile(key)
                for m in range(4):
                    for k in range(DC):
                        if ready is not None and m == 0:
                            pe.wait_ge(ready, k + 1)
                        last = mm(out(m), w[:, k, m * P:(m + 1) * P], hT[:, k, :], k == 0, k == DC - 1)
                last.then_inc(tiles_used, 1)

            project(("in", 0, 0), lambda m: psx[:, m, :], h_ready[0])
            project(("in", 0, 1), lambda m: psx[:, 4 + m, :])
            landed(pe, LAST_IN)
            w = ring[:, TILE[LAST_IN] % SLOTS, 0:DC * 2 * P].rearrange("p (k n) -> p k n", k=DC)
            for k in range(DC):
                mm(ps[:, 4, 0:NT], w[:, k, 0:P], hT[:, k, :], k == 0, k == DC - 1)
            for k in range(DC):
                mm(ps[:, 5, 0:2 * P], hT[:, k, 0:TG], w[:, k, 0:2 * P], k == 0, k == DC - 1)
            for k in range(DC):
                last = mm(ps[:, 4, NT:NT + P], hT[:, k, TG:NT], w[:, k, P:2 * P], k == 0, k == DC - 1)
            last.then_inc(tiles_used, 1)
            pe.wait_ge(s_kv, 48)
            nc.tensor.transpose(ps[:, 4, NT + P:NT + 2 * P], cktok[:, :], ident).then_inc(qkv_done, 1)
            ada(0, (2, 3))
            pe.wait_ge(qraw_ready, 2)
            mm(ps[:, 2, :], rot, qT[:, :, TG:NT])
            mm(ps[:, 4, 0:P], rot, kT[:, 0, TG:NT]).then_inc(rot_done, 1)
            pe.wait_ge(a_ready, 1)
            pe.wait_ge(kv_ready, 1)
            pe.wait_ge(qk_ready, 2)
            for r in range(2):
                lo, hi = 64 * r, 64 * r + 64
                for i in range(4):
                    kv = (2 * i + r) // 4
                    mm(ps[:, r, i * P:(i + 1) * P], qT[lo:hi, i, 0:TG], kT[lo:hi, int(kv != r), 0:TG])
            nc_last = None
            for r in range(2):
                lo, hi = 64 * r, 64 * r + 64
                for i in range(4):
                    kv = (2 * i + r) // 4
                    at = (i % 2) * 2 * P
                    b = 2 + 2 * r + i // 2
                    mm(ps[:, b, at:at + P], qT[lo:hi, i, TG:NT], kT[lo:hi, int(kv != r), TG:NT])
                    nc_last = mm(ps[:, b, at + P:at + 2 * P], qT[lo:hi, i, TG:NT], ckT[lo:hi, int(kv != r), :])
            nc_last.then_inc(scores_done, 1)
            pe.wait_ge(mod_taken, 2)
            ada(0, (4, 5))
            for n in range(24):
                if n % 8 == 0:
                    pe.wait_ge(probs_ready, n // 8 + 1)
                last = nc.tensor.transpose(ps[:, n // 4, (n % 4) * P:(n % 4 + 1) * P], probs[:, n, :], ident)
                if n % 4 == 3:
                    last.then_inc(pt_done, 1)
            pe.wait_ge(pt_ready, 6)
            for r in range(2):
                for i in range(4):
                    h = r * 4 + i
                    kv = (2 * i + r) // 4
                    v = slice(64 * kv, 64 * kv + 64)
                    mm(psx[64 * r:64 * r + 64, i, 0:TG], kvctx[:, P + 64 * kv:P + 64 * kv + 64], probsT[:, h, :])
                    mm(psx[64 * r:64 * r + 64, i, TG:NT], vlat[:, v], probsT[:, 8 + 2 * h, :], True, False)
                    last = mm(psx[64 * r:64 * r + 64, i, TG:NT], cvtok[:, v], probsT[:, 9 + 2 * h, :], False, True)
            last.then_inc(pv_done, 1)
            pe.wait_ge(pooled_ready, 1)
            for m in range(4):
                last = mm(psx[:, 4 + m, :], poolw[:, m, :], apad[:, m, :, APAD:APAD + TG])
            last.then_inc(pool_done, 1)
            pe.wait_ge(mix_ready, 2)
            for n in range(2):
                key = ("out", 0, n)
                landed(pe, key)
                w = wtile(key)
                for m in range(4):
                    for k in range(DC):
                        last = mm(psx[:, 4 * n + m, :], w[:, k, m * P:(m + 1) * P], mixT[:, k, :],
                                  k == 0, k == DC - 1)
                    if m == 1:
                        last.then_inc(y_done[0], 1)
                last.then_inc(tiles_used, 1)
            norm_sums(1)

            def moe(l, n):
                for k in range(DC):
                    pe.wait_ge(h_ready[n], k + 1)
                for g in range(2):
                    for k in range(DC):
                        last = mm(ps_logit[:, g, 0:20], hT[:, k, g * TG:(g + 1) * TG],
                                  wr[:, l, k, :], k == 0, k == DC - 1)
                last.then_inc(route_done, 1)
                for g in range(2):
                    for k in range(DC):
                        last = nc.tensor.transpose(ps[:, 2 * g + k // 4, (k % 4) * P:(k % 4 + 1) * P],
                                                   hT[:, k, g * TG:(g + 1) * TG], ident)
                        if k % 4 == 3:
                            last.then_inc(htok_done, 1)
                pe.wait_ge(mask_ready, l + 1)
                mm(ps_rank[:, 0, :], upper, mask[:, 0, :])
                mm(ps_rank[:, 1, :], upper, mask[:, 1, :], True, False)
                mm(ps_rank[:, 1, :], ones[:, :], mask[:, 0, :], False, True)
                mm(ps_rank[:, 2, :], ones[:, :], mask[:, 0, :], True, False)
                mm(ps_rank[:, 2, :], ones[:, :], mask[:, 1, :], False, True).then_inc(rank_done, 1)
                pe.wait_ge(htok_ready, 4 * l + 4)
                for b in range(4):
                    mm(ps[:, b, :], zrow[0:1, 0:P], zrow[0:1, :])
                pe.wait_ge(gate_ready, l + 1)
                first = TILE["w1", l, 0]
                tiles = [first + j for j in range(6)]
                w1, w3, w2 = ([ring[:, tiles[2 * j + u] % SLOTS, :].rearrange("p (k n) -> p k n", k=k)
                               for u in range(2)] for j, k in ((0, DC), (1, DC), (2, FC)))

                with pe.Fori(0, PAIRS) as i:
                    n = i + l * PAIRS
                    def tile_landed(j):
                        pe.wait_ge(slot_full[tiles[j] % SLOTS], i * 16 + 16 * (tiles[j] // SLOTS + 1))

                    dense = pe.value_load(overflow[0:1, bass.ds(i, 1)], min_val=0, max_val=1)
                    with pe.If(dense == 0):
                        pe.wait_ge(pick_ready, n + (l + 1))
                        for g in range(2):
                            last = nc.tensor.transpose(ps[:, 7, g * TG:(g + 1) * TG], pick_gate[:, g, :], ident)
                        last.then_inc(spread_done, 1)
                        for k in range(DC):
                            for g in range(2):
                                last = mm(ps[:, 4 + k // 4, (k % 4) * P:(k % 4 + 1) * P],
                                          htok[:, g, k * P:(k + 1) * P], pick[:, g, :], g == 0, g == 1)
                            if k % 4 == 3:
                                last.then_inc(gather_done, 1)
                        for w, bank, j in ((w1, 6, 0), (w3, 7, 2)):
                            tile_landed(j)
                            tile_landed(j + 1)
                            if j == 0:
                                pe.wait_ge(hsel_lo, n + 1)
                            else:
                                pe.wait_ge(spread_ready, n + 1)
                            for k in range(DC):
                                if j == 0 and k == 4:
                                    pe.wait_ge(hsel_hi, n + 1)
                                for u in range(2):
                                    c = slice(CAP * u, CAP * u + CAP)
                                    last = mm(ps[c, bank, :], hsel[:, k, c], w[u][:, k, :], k == 0, k == DC - 1)
                            last.then_inc(tiles_used, 2)
                        for f in range(FC):
                            if f % 2 == 0:
                                pe.wait_ge(hid_ready, n * 2 + (f // 2 + 1))
                            last = nc.tensor.transpose(ps[:, 6 + f // 2, (f % 2) * P:(f % 2 + 1) * P],
                                                       hid[:, f * P:(f + 1) * P], ident)
                            if f % 2:
                                last.then_inc(turn_done, 1)
                        tile_landed(4)
                        tile_landed(5)
                        for h in range(2):
                            for f in range(FC):
                                if h == 0 and f % 2 == 0:
                                    pe.wait_ge((hidT_lo, hidT_hi)[f // 2], n + 1)
                                for u in range(2):
                                    c = slice(CAP * u, CAP * u + CAP)
                                    last = mm(ps[c, 4 + h, :], hidT[:, f, c], w2[u][:, f, h * 512:(h + 1) * 512],
                                              f == 0, f == FC - 1)
                            if h == 0:
                                last.then_inc(ysel_done, 1)
                        last.then_inc(tiles_used, 2)
                        pe.wait_ge(ysel_lo, n + 1)
                        for m in range(DC):
                            if m == 4:
                                pe.wait_ge(ysel_hi, n + 1)
                                pe.sem_inc(gatebc_done, 1)
                                pe.sem_inc(dense_done, 2 * FC)
                            last = mm(psx[:, m, :], ysel[:, m * P:(m + 1) * P], spread, False, True)
                        last.then_inc(pair_done, 1)
                    with pe.Else():
                        pe.wait_ge(gdiag_ready, n + 1)
                        mm(ps[:, 4, :], ones[:, :], gate_diag).then_inc(gatebc_done, 1)
                        pe.wait_ge(gatebc_ready, n + 1)
                        for u in range(2):
                            tile_landed(u)
                            tile_landed(2 + u)
                            for m in range(FC):
                                for w, at in ((w1[u], 0), (w3[u], NT)):
                                    for k in range(DC):
                                        last = mm(ps[:, 4 + m, at:at + NT], w[:, k, m * P:(m + 1) * P],
                                                  hT[:, k, :], k == 0, k == DC - 1)
                                last.then_inc(dense_done, 1)
                            tile_landed(4 + u)
                            for f in range(FC):
                                pe.wait_ge(dense_act_ready, n * 2 * FC + (FC * u + f + 1))
                                for m in range(DC):
                                    last = mm(psx[:, m, :], w2[u][:, f, m * P:(m + 1) * P], dense_act[:, f, :],
                                              False, True)
                                    if f == m == 0:
                                        last.then_inc(tiles_used, 1 + 2 * u)
                        last.then_inc(pair_done, 1)
                        pe.sem_inc(spread_done, 1)
                        pe.sem_inc(gather_done, 2)
                        pe.sem_inc(turn_done, 2)
                        pe.sem_inc(ysel_done, 1)
                        pe.wait_ge(pair_done, n + 1)
                        pe.sem_inc(tiles_used, 2)

            moe(0, 1)
            ada(1, (0, 1))
            norm_sums(2)

            for h in range(2):
                for half, j in ((0, 0), (1, 2)):
                    key = ("cw1", 1, h + j)
                    landed(pe, key)
                    w = wtile(key)
                    for m in range(4):
                        b = (4 * h + m) % 6
                        if half == 0 and 4 * h + m >= 6:
                            pe.wait_ge(u_ready, 4 * h + m - 5)
                        for k in range(DC):
                            if h == 0 and half == 0 and m == 0:
                                pe.wait_ge(h_ready[2], k + 1)
                            last = mm(ps[:, b, half * NT:(half + 1) * NT], w[:, k, m * P:(m + 1) * P],
                                      hT[:, k, :], k == 0, k == DC - 1)
                        if half and m < 3:
                            last.then_inc(glu_done, 1)
                    last.then_inc(tiles_used, 1)
            pe.wait_ge(u_ready, DC)
            for j, k in enumerate(PE_CHUNKS):
                for t in range(TAPS + 1):
                    n = j * (TAPS + 1) + t
                    pe.wait_ge(diag_ready, n + 1)
                    rows = upad[:, k, :, t:t + TG] if t < TAPS else ones[:, 0:1].unsqueeze(2).to_broadcast([P, 2, TG])
                    last = mm(ps[:, j, 0:NT], diag[:, n % DIAGS, :], rows, t == 0, t == TAPS)
                    if t < TAPS:
                        last.then_inc(diag_used, 1)
                last.then_inc(dconv_done, 1)
            ada(1, (2, 3, 4, 5))
            pe.wait_ge(conv_ready, 1)
            pe.wait_ge(dconv_ready, len(PE_CHUNKS))
            column_sums(ps[:, 5, 0:NT], conv, conv_ready, lambda k: 1, mean_done)
            column_sums(ps[:, 4, 0:NT], sq, csq_ready, lambda k: k + 1, var_done)
            for n in range(2):
                key = ("cw2", 1, n)
                landed(pe, key)
                w = wtile(key)
                for m in range(4):
                    for k in range(DC):
                        if n == 0 and m == 0:
                            pe.wait_ge(cs_ready, k + 1)
                        last = mm(psx[:, 4 * n + m, :], w[:, k, m * P:(m + 1) * P], hT[:, k, :],
                                  k == 0, k == DC - 1)
                    if m == 1:
                        last.then_inc(y_done[2], 1)
                last.then_inc(tiles_used, 1)
            norm_sums(3)
            moe(1, 3)
            norm_sums(4)
            pe.wait_ge(hpre_ready[4], DC)
            for g in range(2):
                for k in range(DC):
                    last = nc.tensor.transpose(ps[:, 2 * g + k // 4, (k % 4) * P:(k % 4 + 1) * P],
                                               hT[:, k, g * TG:(g + 1) * TG], ident)
                last.then_inc(out_t, 1)

        @block.scalar
        def _(act):
            def vrow(at, src):
                n = src.shape[0] // P
                act.dma_start(rows_v[at:at + n, :], src.rearrange("(r p) -> r p", p=P)).then_inc(s_rows, 16)

            act.dma_start(cst[:, :], shape_consts).then_inc(s_cst, 16)
            vrow(V_CCTX, c_ctx)
            vrow(V_C, c[0])
            act.dma_start(rows_v[V_NMIX:V_NMIX + 16, :],
                          norm_mix_g.rearrange("l (r p) -> (l r) p", p=P)).then_inc(s_rows, 16)
            act.dma_start(rows_v[V_NFFN:V_NFFN + 16, :],
                          norm_ffn_g.rearrange("l (r p) -> (l r) p", p=P)).then_inc(s_rows, 16)
            vrow(V_FIN, final_g)
            act.dma_start(rows_b[:, :], b_ada.rearrange("l (r p) -> (l r) p", p=P)).then_inc(s_rows, 16)
            act.dma_start(rows_r[0:64, :],
                          router_exp.rearrange("l g (c p) e -> (l g c) (p e)", p=P)).then_inc(s_rows, 16)
            act.dma_start(rows_r[64:80, :],
                          router_grp.rearrange("l (c p) e -> (l c) (p e)", p=P)).then_inc(s_rows, 16)
            act.dma_start(sinkrow[:, :], attn_sink).then_inc(s_rows, 16)
            act.sem_inc(small_issued, 1)

            act.wait_ge(s_vec, 1)
            act.wait_ge(s_fill, 1)
            nc.scalar.activation(csil[:, :, 0:2].rearrange("p k g -> p g k"), vec[:, V_CCTX:V_CCTX + 2 * DC].rearrange("p (g k) -> p g k", g=2),
                                 ACT.Silu).then_inc(s_csil, 1)

            def norm_act(n, shift, meanwhile=None):
                for k in range(DC):
                    act.wait_ge(x_ready[n], k + 1)
                    nc.scalar.activation(sq[:, k, :], xT[:, k, :], ACT.Square).then_inc(sq_ready[n], 1)
                act.wait_ge(ss_done[n], 1)
                nc.scalar.activation(root[:, :], ps_norm, ACT.Sqrt, bias=eps[:, 0:1],
                                     scale=1.0 / D).then_inc(root_ready[n], 1)
                if meanwhile is not None:
                    meanwhile()
                if shift is None:
                    return
                for k in range(DC):
                    act.wait_ge(hpre_ready[n], k + 1)
                    for g in range(2):
                        last = nc.scalar.activation(hT[:, k, g * TG:(g + 1) * TG], hT[:, k, g * TG:(g + 1) * TG],
                                                    ACT.Identity, bias=mod[:, shift[0], shift[1] + k, g:g + 1])
                    last.then_inc(h_ready[n], 1)

            def take_part(keys):
                for key in keys:
                    n = ADA[key]
                    used(act, key)
                    if n >= 2:
                        act.wait_ge(mod_done, n - 1)
                    nc.scalar.activation(part[:, n % 2, :], ps_part, ACT.Copy).then_inc(part_ready, 1)

            act.wait_ge(s_fill, 2)
            norm_act(0, (0, 0), lambda: take_part(ada_keys(0, (0, 1))))
            used(act, ("in", 0, 0))
            act.wait_ge(s_fill, 3)
            nc.scalar.activation(apad[:, :, :, APAD:APAD + TG],
                                 psx[:, 0:4, :].rearrange("p c (g t) -> p c g t", g=2), ACT.Copy).then_inc(a_ready, 1)
            act.wait_ge(qkv_done, 1)
            nc.scalar.activation(kvctx[:, :], ps[:, 5, 0:2 * P], ACT.Copy).then_inc(kv_ready, 1)
            act.wait_ge(kv_ready, 1)
            act.dma_start(state_k[0, 0].rearrange("t h d -> t (h d)"), kvctx[:, 0:P]).then_inc(s_out, 16)
            act.dma_start(state_v[0, 0].rearrange("t h d -> t (h d)"), kvctx[:, P:2 * P]).then_inc(s_out, 16)
            take_part(ada_keys(0, (2, 3)))
            act.wait_ge(nmax_ready, 1)
            for h in range(NH):
                nc.scalar.activation(probs[:, h, :], ps[:, h // 4, (h % 4) * P:(h % 4 + 1) * P], ACT.Exp,
                                     bias=nmax[:, 0, h:h + 1], scale=SCALE,
                                     accum_out=rsum[:, 0, h:h + 1]).then_inc(exp_ready, 1)
            for h in range(NH):
                nc.scalar.activation(probs[:, 8 + 2 * h:10 + 2 * h, :],
                                     ps[:, 2 + h // 2, (h % 2) * NT:(h % 2 + 1) * NT].rearrange(
                                         "p (s k) -> p s k", s=2), ACT.Exp,
                                     bias=nmax[:, 1, h:h + 1], scale=SCALE,
                                     accum_out=rsum[:, 1, h:h + 1]).then_inc(exp_ready, 1)
            act.wait_ge(nmax_ready, 2)
            nc.scalar.activation(esink[:, :, :], esink[:, :, :], ACT.Exp).then_inc(exp_ready, 1)
            take_part(ada_keys(0, (4, 5)))
            for b in (1, 3, 5):
                act.wait_ge(pt_done, b + 1)
                nc.scalar.activation(probsT[:, 4 * b:4 * b + 4, :], ps[:, b, :], ACT.Copy).then_inc(pt_ready, 1)
            act.wait_ge(pv_done, 1)
            nc.scalar.activation(mixT[:, 4:8, :], psx[:, 0:4, :], ACT.Copy).then_inc(mix_ready, 1)
            norm_act(1, (0, 24))

            def moe_act(l):
                act.wait_ge(gexp_in, l + 1)
                nc.scalar.activation(rs[:, 2:4, :], rs[:, 0:2, :], ACT.Exp).then_inc(gexp_out, 1)
                nc.scalar.activation(rg[:, 1], rg[:, 0], ACT.Exp).then_inc(gexp_out, 1)
                for b in range(4):
                    act.wait_ge(htok_done, 4 * l + b + 1)
                    nc.scalar.activation(htok[:, b // 2, (b % 2) * 512:(b % 2 + 1) * 512], ps[:, b, :],
                                         ACT.Copy).then_inc(htok_ready, 1)
                act.wait_ge(gate_ready, l + 1)
                first = TILE["w1", l, 0]
                with act.Fori(0, PAIRS) as i:
                    n = i + l * PAIRS
                    dense = act.value_load(overflow[0:1, bass.ds(i, 1)], min_val=0, max_val=1)
                    with act.If(dense == 0):
                        act.wait_ge(gather_done, n * 2 + 1)
                        nc.scalar.activation(hsel[:, 0:4, :], ps[:, 4, :].rearrange("p (k j) -> p k j", k=4),
                                             ACT.Copy).then_inc(hsel_lo, 1)
                        act.wait_ge(tiles_used, i * 6 + (first + 2))
                        nc.scalar.activation(sil, ps[:, 6, :], ACT.Silu).then_inc(sil_ready, 1)
                        act.wait_ge(turn_done, n * 2 + 1)
                        nc.scalar.activation(hidT[:, 0:2, :], ps[:, 6, 0:2 * P].rearrange("p (f j) -> p f j", f=2),
                                             ACT.Copy).then_inc(hidT_lo, 1)
                        act.wait_ge(ysel_done, n + 1)
                        nc.scalar.activation(ysel[:, 0:512], ps[:, 4, :], ACT.Copy).then_inc(ysel_lo, 1)
                        act.sem_inc(dense_sil_ready, 2 * FC)
                    with act.Else():
                        for u in range(2):
                            for m in range(FC):
                                act.wait_ge(dense_done, n * 2 * FC + (FC * u + m + 1))
                                if u:
                                    act.wait_ge(dense_act_ready, n * 2 * FC + (m + 1))
                                nc.scalar.activation(dense_sil[:, m, :], ps[:, 4 + m, 0:NT],
                                                     ACT.Silu).then_inc(dense_sil_ready, 1)
                        act.sem_inc(hsel_lo, 1)
                        act.sem_inc(sil_ready, 1)
                        act.sem_inc(hidT_lo, 1)
                        act.sem_inc(ysel_lo, 1)

            moe_act(0)
            take_part(ada_keys(1, (0, 1)))
            norm_act(2, (1, 0))
            for m in range(DC):
                if m % 4 == 3:
                    used(act, ("cw1", 1, 2 + m // 4))
                else:
                    act.wait_ge(glu_done, 3 * (m // 4) + m % 4 + 1)
                nc.scalar.activation(sq[:, m, :], ps[:, m % 6, NT:2 * NT], ACT.Sigmoid,
                                     bias=vec[:, V_CB1 + DC + m:V_CB1 + DC + m + 1]).then_inc(sig_ready, 1)
            for j, k in enumerate(PE_CHUNKS):
                for t in range(TAPS + 1):
                    n = j * (TAPS + 1) + t
                    if n >= DIAGS:
                        before = n - DIAGS
                        if before % (TAPS + 1) == TAPS:
                            act.wait_ge(dconv_done, before // (TAPS + 1) + 1)
                        else:
                            act.wait_ge(diag_used, before - before // (TAPS + 1) + 1)
                    tap = dw[:, k, t:t + 1] if t < TAPS else vec[:, V_DWB + k:V_DWB + k + 1]
                    nc.scalar.activation(diag[:, n % DIAGS, :], ident, ACT.Copy, scale=tap).then_inc(diag_ready, 1)
            for j, k in enumerate(PE_CHUNKS):
                act.wait_ge(dconv_done, j + 1)
                nc.scalar.activation(conv[:, k, :], ps[:, j, 0:NT], ACT.Copy).then_inc(dconv_ready, 1)
            take_part(ada_keys(1, (2, 3, 4, 5)))
            act.wait_ge(mean_done, 1)
            nc.scalar.activation(mean[:, :], ps[:, 5, 0:NT], ACT.Copy, scale=1.0 / D).then_inc(mean_ready, 1)
            for k in range(DC):
                act.wait_ge(cent_ready, k + 1)
                nc.scalar.activation(sq[:, k, :], conv[:, k, :], ACT.Square).then_inc(csq_ready, 1)
            act.wait_ge(var_done, 1)
            nc.scalar.activation(root[:, :], ps[:, 4, 0:NT], ACT.Sqrt, bias=eps[:, 0:1],
                                 scale=1.0 / D).then_inc(croot_ready, 1)
            for k in range(DC):
                act.wait_ge(cn_ready, k + 1)
                nc.scalar.activation(hT[:, k, :], conv[:, k, :], ACT.Silu, bias=vec[:, V_LNB + k:V_LNB + k + 1],
                                     scale=vec[:, V_LNG + k:V_LNG + k + 1]).then_inc(cs_ready, 1)
            for k in range(DC):
                product(act, y_done[2], "cw2", 1, k)
                nc.scalar.activation(sq[:, k, :], psx[:, k, :], ACT.Identity,
                                     bias=vec[:, V_CB2 + k:V_CB2 + k + 1]).then_inc(yb_ready, 1)
            norm_act(3, (1, 24))
            moe_act(1)
            norm_act(4, None)
            for g in range(2):
                act.wait_ge(out_t, g + 1)
                nc.scalar.activation(xtok[:, g, 0:512], ps[:, 2 * g, :], ACT.Copy).then_inc(out_ready[g], 1)

        @block.gpsimd
        def _(pool):
            def vrow(at, src):
                n = src.shape[0] // P
                pool.dma_start(rows_v[at:at + n, :], src.rearrange("(r p) -> r p", p=P)).then_inc(s_rows_conv, 16)

            vrow(V_CB1, conv_b1[0])
            vrow(V_DWB, conv_dw_b[0])
            vrow(V_LNG, conv_ln_g[0])
            vrow(V_LNB, conv_ln_b[0])
            vrow(V_CB2, conv_b2[0])
            vrow(V_PSC, pool_scale[0])
            pool.dma_start(rows_dw[:, :], conv_dw[0]).then_inc(s_rows_conv, 16)
            pool.dma_start(cktok[:, :], cache_k[0, 0].rearrange("t h d -> t (h d)")).then_inc(s_kv, 16)
            pool.dma_start(cvtok[:, :], cache_v[0, 0].rearrange("t h d -> t (h d)")).then_inc(s_kv, 16)
            pool.dma_start(poolw[:, :, :], pool_w[0].rearrange("g c d -> c g d")).then_inc(s_kv, 16)
            pool.sem_inc(small_issued, 1)
            nc.gpsimd.memset(csil[:, :, :], 0.0).then_inc(s_fill, 1)
            nc.gpsimd.memset(ones[:, :], 1.0)
            nc.gpsimd.memset(eps[:, :], EPS)
            nc.gpsimd.memset(gate[:, :, :], 0.0)
            nc.gpsimd.memset(slot[:, :, :], -1.0)
            nc.gpsimd.memset(zrow[:, :], 0.0).then_inc(s_fill, 1)
            nc.gpsimd.memset(apad[:, :, :, :], 0.0).then_inc(s_fill, 1)
            pool.wait_ge(a_ready, 1)
            src, at = apad, 0
            for n in range(4):
                step = 1 << n
                length = AL - 2 * step + 1
                dst = asum[:, n % 2]
                nc.gpsimd.tensor_tensor(dst[:, n:4, :, 0:length], src[:, n:4, :, 0:length],
                                        src[:, n:4, :, step:step + length], ALU.add).then_inc(s_pool, 1)
                pool.wait_ge(s_pool, 3 * n + 1)
                lo = APAD - WINDOWS[n] // 2
                nc.gpsimd.tensor_tensor(mean4[:, :, :], dst[:, n, :, lo:lo + TG],
                                        icnt[:, n:n + 1, :].to_broadcast([P, 2, TG]), ALU.mult).then_inc(s_pool, 1)
                pool.wait_ge(s_pool, 3 * n + 2)
                last = nc.gpsimd.tensor_tensor(apad[:, n, :, APAD:APAD + TG], mean4[:, :, :],
                                               apad[:, n, :, APAD:APAD + TG], ALU.subtract).then_inc(s_pool, 1)
                pool.wait_ge(s_pool, 3 * n + 3)
                src = dst
            pool.sem_inc(pooled_ready, 1)

        @block.vector
        def _(dve):
            chain = [0]
            V = nc.vector

            def link(ins):
                chain[0] += 1
                ins.then_inc(s_dve, 1)
                dve.wait_ge(s_dve, chain[0])

            def take_mod(l, p0, p1):
                dve.wait_ge(mod_done, ADA["ada", l, 2 * p1 - 1] + 1)
                a, b = 8 * p0, 8 * p1
                link(V.tensor_tensor(mod[:, l, a:b, :], ps_ada[:, a:b, :],
                                     bias[:, l, a:b].unsqueeze(2).to_broadcast([P, b - a, 2]), ALU.add))
                for which, p, v in ((0, 1, V_NMIX), (1, 4, V_NFFN)):
                    if p0 <= p < p1:
                        g = vec[:, v + DC * l:v + DC * (l + 1)].unsqueeze(2).to_broadcast([P, DC, 2])
                        link(V.scalar_tensor_tensor(out=gain[:, l, which], in0=mod[:, l, 8 * p:8 * p + 8, :],
                                                    scalar=1.0, in1=g, op0=ALU.add, op1=ALU.mult))
                dve.sem_inc(mod_taken, 1)

            def norm_dve(n, g_of):
                dve.wait_ge(root_ready[n], 1)
                link(V.reciprocal(rstd[:, :], root[:, :]))
                for k in range(DC):
                    for g in range(2):
                        t = slice(g * TG, (g + 1) * TG)
                        last = V.scalar_tensor_tensor(out=hT[:, k, t], in0=xT[:, k, t], scalar=g_of(k, g),
                                                      in1=rstd[:, t], op0=ALU.mult, op1=ALU.mult)
                    last.then_inc(hpre_ready[n], 1)

            def residual(n, y, l, part, ready):
                for k in range(DC):
                    ready(k)
                    for g in range(2):
                        t = slice(g * TG, (g + 1) * TG)
                        last = V.scalar_tensor_tensor(out=xT[:, k, t], in0=y[:, k, t],
                                                      scalar=mod[:, l, 8 * part + k, g:g + 1],
                                                      in1=xT[:, k, t], op0=ALU.mult, op1=ALU.add)
                    last.then_inc(x_ready[n], 1)

            for k in range(DC):
                dve.wait_ge(s_xt, k // 2 + 1)
                V.tensor_copy(xT[:, k, :], psx[:, k, :]).then_inc(x_ready[0], 1)
            dve.wait_ge(s_vt, 1)
            V.tensor_copy(vec[:, :], ps[:, 4, 0:V_ROWS]).then_inc(s_vec, 1)
            V.tensor_copy(bias[:, :, :], ps[:, 4, 128:224].rearrange("p (l m) -> p l m", l=2))
            V.tensor_copy(dw[:, :, :], ps[:, 5, 0:DC * TAPS].rearrange("p (c t) -> p c t", c=DC))
            V.tensor_copy(sink[:, :], ps[:, 4, 256:256 + NH])
            pr = ps[:, 6, 0:320].rearrange("p (e r) -> p e r", e=4)
            for l in range(2):
                for g in range(4):
                    V.tensor_copy(wr[:, l, :, 4 * g:4 * g + 4],
                                  pr[:, :, 32 * l + 8 * g:32 * l + 8 * g + 8].rearrange("p e c -> p c e"))
                last = V.tensor_copy(wr[:, l, :, 16:20], pr[:, :, 64 + 8 * l:72 + 8 * l].rearrange("p e c -> p c e"))
            last.then_inc(s_prep, 1)
            dve.wait_ge(s_prep, 1)
            take_mod(0, 0, 2)
            norm_dve(0, lambda k, g: gain[:, 0, 0, k, g:g + 1])

            dve.wait_ge(qkv_done, 1)
            V.tensor_copy(qT, psx[:, 4:8, :]).then_inc(qraw_ready, 1)
            V.tensor_copy(kT[:, 0, :], ps[:, 4, 0:NT])
            V.tensor_copy(vlat[:, :], ps[:, 4, NT:NT + P])
            V.tensor_copy(ckT[:, 0, :], ps[:, 4, NT + P:NT + 2 * P]).then_inc(qraw_ready, 1)
            dve.wait_ge(qraw_ready, 2)
            V.tensor_copy(kT[0:64, 1, 0:TG], kT[64:128, 0, 0:TG])
            V.tensor_copy(kT[64:128, 1, 0:TG], kT[0:64, 0, 0:TG])
            V.tensor_copy(ckT[0:64, 1, :], ckT[64:128, 0, :])
            V.tensor_copy(ckT[64:128, 1, :], ckT[0:64, 0, :])
            V.tensor_tensor(rt[:, 0:4, :], qT[:, :, TG:NT], cos.unsqueeze(1).to_broadcast([P, 4, TG]), ALU.mult)
            link(V.tensor_tensor(rt[:, 4, :], kT[:, 0, TG:NT], cos, ALU.mult))
            dve.wait_ge(rot_done, 1)
            V.tensor_tensor(rt2[:, 0:4, :], ps[:, 2, :].rearrange("p (c t) -> p c t", c=4),
                            sin.unsqueeze(1).to_broadcast([P, 4, TG]), ALU.mult)
            link(V.tensor_tensor(rt2[:, 4, :], ps[:, 4, 0:P], sin, ALU.mult))
            V.tensor_tensor(qT[:, :, TG:NT], rt[:, 0:4, :], rt2[:, 0:4, :], ALU.add).then_inc(qk_ready, 1)
            link(V.tensor_tensor(kT[:, 0, TG:NT], rt[:, 4, :], rt2[:, 4, :], ALU.add))
            V.tensor_copy(kT[0:64, 1, TG:NT], kT[64:128, 0, TG:NT])
            V.tensor_copy(kT[64:128, 1, TG:NT], kT[0:64, 0, TG:NT]).then_inc(qk_ready, 1)
            take_mod(0, 2, 4)

            dve.wait_ge(scores_done, 1)
            V.tensor_reduce(smax[:, 0, :], ps[:, 0:2, :].rearrange("p b (h k) -> p (b h) k", h=4), AX.X, ALU.max)
            link(V.tensor_reduce(smax[:, 1, :], ps[:, 2:6, :].rearrange("p b (h k) -> p (b h) k", h=2), AX.X, ALU.max))
            link(V.scalar_tensor_tensor(out=nmax[:, :, :], in0=smax[:, :, :], scalar=SCALE,
                                        in1=sink[:, :].unsqueeze(1).to_broadcast([P, 2, NH]),
                                        op0=ALU.mult, op1=ALU.max))
            V.tensor_scalar(nmax[:, :, :], nmax[:, :, :], -1.0, None, ALU.mult).then_inc(nmax_ready, 1)
            dve.wait_ge(nmax_ready, 1)
            V.tensor_tensor(esink[:, :, :], nmax[:, :, :], sink[:, :].unsqueeze(1).to_broadcast([P, 2, NH]),
                            ALU.add).then_inc(nmax_ready, 1)
            dve.wait_ge(exp_ready, 17)
            link(V.tensor_tensor(rden[:, :, :], rsum[:, :, :], esink[:, :, :], ALU.add))
            link(V.reciprocal(rden[:, :, :], rden[:, :, :]))
            for h in range(NH):
                last = V.tensor_scalar(probs[:, h, :], probs[:, h, :], rden[:, 0, h:h + 1], None, ALU.mult)
            last.then_inc(probs_ready, 1)
            for h in range(NH):
                last = V.tensor_scalar(probs[:, 8 + 2 * h:10 + 2 * h, :], probs[:, 8 + 2 * h:10 + 2 * h, :],
                                       rden[:, 1, h:h + 1], None, ALU.mult)
                if h % 4 == 3:
                    last.then_inc(probs_ready, 1)
            take_mod(0, 4, 6)
            for b in (0, 2, 4):
                dve.wait_ge(pt_done, b + 1)
                V.tensor_copy(probsT[:, 4 * b:4 * b + 4, :], ps[:, b, :].rearrange("p (n k) -> p n k", n=4)).then_inc(
                    pt_ready, 1)
            dve.wait_ge(pool_done, 1)
            for m in range(4):
                last = V.tensor_scalar(mixT[:, m, :], psx[:, 4 + m, :], vec[:, V_PSC + m:V_PSC + m + 1], None,
                                       ALU.mult)
            last.then_inc(mix_ready, 1)
            residual(1, psx, 0, 2, lambda k: product(dve, y_done[0], "out", 0, k))
            norm_dve(1, lambda k, g: gain[:, 0, 1, k, g:g + 1])

            def first_match(out, eq, a, b):
                link(V.tensor_copy(a, eq))
                link(V.tensor_tensor(a[:, :, 1:4], eq[:, :, 1:4], eq[:, :, 0:3], ALU.add))
                link(V.tensor_copy(b, a))
                link(V.tensor_tensor(b[:, :, 2:4], a[:, :, 2:4], a[:, :, 0:2], ALU.add))
                link(V.scalar_tensor_tensor(out=out, in0=b, scalar=1.0, in1=eq, op0=ALU.is_equal, op1=ALU.mult))

            def wide(v, n=4):
                return v.unsqueeze(2).to_broadcast([P, 2, n])

            def route(l):
                dve.wait_ge(route_done, l + 1)
                link(V.tensor_copy(lg[:, :, :], ps_logit[:, :, 0:20]))
                gl = lg[:, :, 16:20]
                gmax, m1, m2, gsum, t0 = rs[:, 4], rs[:, 5], rs[:, 6], rs[:, 7], rs[:, 8]
                link(V.tensor_reduce(gmax, gl, AX.X, ALU.max))
                link(V.tensor_tensor(rg[:, 0], gl, wide(gmax), ALU.subtract))
                link(V.tensor_tensor(rg[:, 2], gl, wide(gmax), ALU.is_equal))
                first_match(rg[:, 3], rg[:, 2], rg[:, 4], rg[:, 5])
                sel = rg[:, 3].unsqueeze(3).to_broadcast([P, 2, 4, 4])
                r4 = r1[:, :, :].rearrange("p g (a e) -> p g a e", a=4)
                link(V.tensor_tensor(r4, lg[:, :, 0:16].rearrange("p g (a e) -> p g a e", a=4), sel, ALU.mult))
                link(V.tensor_reduce(rg[:, 6], r4.rearrange("p g a e -> p g e a"), AX.X, ALU.add))
                link(V.tensor_reduce(m1, rg[:, 6], AX.X, ALU.max))
                link(V.tensor_tensor(rg[:, 2], rg[:, 6], wide(m1), ALU.is_equal))
                first_match(rg[:, 7], rg[:, 2], rg[:, 4], rg[:, 5])
                link(V.scalar_tensor_tensor(out=rg[:, 8], in0=rg[:, 7], scalar=-1e30, in1=rg[:, 6],
                                            op0=ALU.mult, op1=ALU.add))
                link(V.tensor_reduce(m2, rg[:, 8], AX.X, ALU.max))
                link(V.tensor_tensor(rg[:, 2], rg[:, 8], wide(m2), ALU.is_equal))
                first_match(rg[:, 9], rg[:, 2], rg[:, 4], rg[:, 5])
                link(V.tensor_tensor(rg[:, 11], rg[:, 7], rg[:, 9], ALU.add))
                V.tensor_tensor(mask[:, :, :].rearrange("p g (a e) -> p g a e", a=4), sel,
                                rg[:, 11].unsqueeze(2).to_broadcast([P, 2, 4, 4]), ALU.mult).then_inc(mask_ready, 1)
                V.tensor_tensor(rs[:, 0], m1, m1, ALU.subtract)
                V.tensor_tensor(rs[:, 1], m2, m1, ALU.subtract).then_inc(gexp_in, 1)
                dve.wait_ge(gexp_out, 2 * l + 2)
                link(V.tensor_reduce(gsum, rg[:, 1], AX.X, ALU.add))
                link(V.tensor_tensor(t0, rs[:, 2], rs[:, 3], ALU.add))
                link(V.tensor_tensor(t0, t0, gsum, ALU.mult))
                link(V.reciprocal(t0, t0))
                link(V.tensor_tensor(rs[:, 9], rs[:, 2], t0, ALU.mult))
                link(V.tensor_tensor(rs[:, 10], rs[:, 3], t0, ALU.mult))
                link(V.tensor_tensor(rg[:, 7], rg[:, 7], wide(rs[:, 9]), ALU.mult))
                link(V.tensor_tensor(rg[:, 9], rg[:, 9], wide(rs[:, 10]), ALU.mult))
                link(V.tensor_tensor(rg[:, 10], rg[:, 7], rg[:, 9], ALU.add))
                link(V.tensor_tensor(gate[:, :, 0:NE].rearrange("p g (a e) -> p g a e", a=4), sel,
                                     rg[:, 10].unsqueeze(2).to_broadcast([P, 2, 4, 4]), ALU.mult))
                dve.wait_ge(rank_done, l + 1)
                link(V.scalar_tensor_tensor(out=slot[:, :, 0:NE], in0=ps_rank[:, 0:2, :], scalar=1.0,
                                            in1=mask[:, :, :], op0=ALU.add, op1=ALU.mult))
                V.tensor_scalar(slot[:, :, 0:NE], slot[:, :, 0:NE], -1.0, None, ALU.add)
                link(V.tensor_reduce(crowd[:, :], ps_rank[:, 2, :].rearrange("p (i u) -> p i u", u=2), AX.X, ALU.max))
                V.tensor_scalar(overflow[:, :], crowd[:, :], LIMIT, None, ALU.is_gt).then_inc(gate_ready, 1)
                dve.wait_ge(gate_ready, l + 1)

            def choose(l, i):
                shape = [P, 2, 2, CAP]
                e = slice(0, 2) if i is None else bass.ds(i * 2 + 2, 2)
                first = V.tensor_tensor(pick.rearrange("p g (u j) -> p g u j", u=2),
                                        iota.unsqueeze(1).unsqueeze(1).to_broadcast(shape),
                                        slot[:, :, e].unsqueeze(3).to_broadcast(shape), ALU.is_equal)
                first.then_inc(picked, 1)
                dve.wait_ge(picked, l * (PAIRS + 1) + 1 if i is None else i + (l * (PAIRS + 1) + 2))
                V.tensor_tensor(pick_gate.rearrange("p g (u j) -> p g u j", u=2),
                                pick.rearrange("p g (u j) -> p g u j", u=2),
                                gate[:, :, e].unsqueeze(3).to_broadcast(shape), ALU.mult).then_inc(pick_ready, 1)

            def experts(l):
                first = TILE["w1", l, 0]
                choose(l, None)
                with dve.Fori(0, PAIRS) as i:
                    n = i + l * PAIRS
                    dense = dve.value_load(overflow[0:1, bass.ds(i, 1)], min_val=0, max_val=1)
                    with dve.If(dense == 0):
                        dve.wait_ge(spread_done, n + 1)
                        V.tensor_copy(spread, ps[:, 7, 0:NT]).then_inc(spread_ready, 1)
                        dve.wait_ge(gather_done, n * 2 + 2)
                        V.tensor_copy(hsel[:, 4:8, :], ps[:, 5, :].rearrange("p (k j) -> p k j", k=4)).then_inc(
                            hsel_hi, 1)
                        dve.wait_ge(sil_ready, n + 1)
                        dve.wait_ge(tiles_used, i * 6 + (first + 4))
                        for h in range(2):
                            c = slice(h * 2 * P, (h + 1) * 2 * P)
                            V.tensor_tensor(hid[:, c], sil[:, c], ps[:, 7, c], ALU.mult).then_inc(hid_ready, 1)
                        dve.wait_ge(turn_done, n * 2 + 2)
                        V.tensor_copy(hidT[:, 2:4, :], ps[:, 7, 0:2 * P].rearrange("p (f j) -> p f j", f=2)).then_inc(
                            hidT_hi, 1)
                        choose(l, i)
                        dve.wait_ge(tiles_used, i * 6 + (first + 6))
                        V.tensor_copy(ysel[:, 512:1024], ps[:, 5, :]).then_inc(ysel_hi, 1)
                        dve.sem_inc(gdiag_ready, 1)
                        dve.sem_inc(gatebc_ready, 1)
                        dve.sem_inc(dense_act_ready, 2 * FC)
                        dve.sem_inc(gated, 2 * FC)
                    with dve.Else():
                        shape = [P, 2, 2, TG]
                        V.tensor_tensor(gate_diag.rearrange("p (u g) t -> p u g t", u=2),
                                        ident.unsqueeze(1).unsqueeze(1).to_broadcast(shape),
                                        gate[:, :, bass.ds(i * 2, 2)].rearrange("p g u -> p u g").unsqueeze(
                                            3).to_broadcast(shape), ALU.mult).then_inc(gdiag_ready, 1)
                        dve.wait_ge(gatebc_done, n + 1)
                        V.tensor_copy(gatebc, ps[:, 4, :].rearrange("p (u t) -> p u t", u=2)).then_inc(
                            gatebc_ready, 1)
                        dve.wait_ge(gatebc_ready, n + 1)
                        for u in range(2):
                            for m in range(FC):
                                turn = FC * u + m + 1
                                dve.wait_ge(dense_sil_ready, n * 2 * FC + turn)
                                V.tensor_tensor(dense_sil[:, m, :], dense_sil[:, m, :], gatebc[:, u, :],
                                                ALU.mult).then_inc(gated, 1)
                                dve.wait_ge(gated, n * 2 * FC + turn)
                                V.tensor_tensor(dense_act[:, m, :], dense_sil[:, m, :], ps[:, 4 + m, NT:2 * NT],
                                                ALU.mult).then_inc(dense_act_ready, 1)
                        choose(l, i)
                        dve.sem_inc(spread_ready, 1)
                        dve.sem_inc(hsel_hi, 1)
                        dve.sem_inc(hid_ready, 2)
                        dve.sem_inc(hidT_hi, 1)
                        dve.sem_inc(ysel_hi, 1)
                dve.wait_ge(pair_done, (l + 1) * PAIRS)

            route(0)
            experts(0)
            residual(2, psx, 0, 5, lambda k: None)
            take_mod(1, 0, 2)
            norm_dve(2, lambda k, g: gain[:, 1, 0, k, g:g + 1])

            link(V.memset(upad[:, :, :, :], 0.0))
            cv = [conv[:, k, :].rearrange("p (g t) -> p g t", g=2) for k in range(DC)]

            def glu(m):
                dve.wait_ge(sig_ready, m + 1)
                V.scalar_tensor_tensor(out=upad[:, m, :, HALF:HALF + TG],
                                       in0=ps[:, m % 6, 0:NT].rearrange("p (g t) -> p g t", g=2),
                                       scalar=vec[:, V_CB1 + m:V_CB1 + m + 1],
                                       in1=sq[:, m, :].rearrange("p (g t) -> p g t", g=2),
                                       op0=ALU.add, op1=ALU.mult).then_inc(u_ready, 1)

            def convolve(a, b):
                dve.wait_ge(u_ready, b)
                base, n = TAPS * a, b - a
                for k in range(a, b):
                    V.tensor_scalar(cv[k], upad[:, k, :, 0:TG], dw[:, k, 0:1], vec[:, V_DWB + k:V_DWB + k + 1],
                                    ALU.mult, ALU.add).then_inc(tap_done, 1)
                with dve.Fori(1, TAPS) as t:
                    for k in range(a, b):
                        dve.wait_ge(tap_done, t * n + (base + k - a + 1 - n))
                        V.scalar_tensor_tensor(out=cv[k], in0=upad[:, k, :, bass.ds(t, TG)],
                                               scalar=dw[:, k, bass.ds(t, 1)], in1=cv[k],
                                               op0=ALU.mult, op1=ALU.add).then_inc(tap_done, 1)
                dve.wait_ge(tap_done, TAPS * b)

            for m in range(4):
                glu(m)
            convolve(0, 4)
            for m in range(4, DC):
                glu(m)
            convolve(4, DVE_CHUNKS)
            dve.sem_inc(conv_ready, 1)
            take_mod(1, 2, 6)
            dve.wait_ge(mean_ready, 1)
            for k in range(DC):
                V.tensor_tensor(conv[:, k, :], conv[:, k, :], mean[:, :], ALU.subtract).then_inc(cent_ready, 1)
            dve.wait_ge(croot_ready, 1)
            link(V.reciprocal(rstd[:, :], root[:, :]))
            for k in range(DC):
                V.tensor_tensor(conv[:, k, :], conv[:, k, :], rstd[:, :], ALU.mult).then_inc(cn_ready, 1)
            residual(3, sq, 1, 2, lambda k: dve.wait_ge(yb_ready, k + 1))
            norm_dve(3, lambda k, g: gain[:, 1, 1, k, g:g + 1])
            route(1)
            experts(1)
            residual(4, psx, 1, 5, lambda k: None)
            norm_dve(4, lambda k, g: vec[:, V_FIN + k:V_FIN + k + 1])
            for g in range(2):
                dve.wait_ge(out_t, g + 1)
                V.tensor_copy(xtok[:, g, 512:1024], ps[:, 2 * g + 1, :]).then_inc(out_ready[g], 1)


def shape_constants():
    t = np.zeros((P, C_W), np.float32)
    t[:, C_ID:C_ID + P] = np.eye(P, dtype=np.float32)
    axis, half = HD // 2, HD // 4
    for d in range(P):
        j = d % axis
        if j < half:
            t[d + half, C_ROT + d] = -1.0
        else:
            t[d - half, C_ROT + d] = 1.0
    inv = (10000.0 ** (-np.arange(0, axis, 2, dtype=np.float32) / axis)).astype(np.float32)
    tok = np.arange(TG)
    pos = {0: (tok // 64).astype(np.float32), 1: (tok % 64).astype(np.float32)}
    for d in range(P):
        ang = pos[(d % HD) // axis] * inv[d % half]
        t[d, C_COS:C_COS + TG] = np.cos(ang)
        t[d, C_SIN:C_SIN + TG] = np.sin(ang)
    for j in range(4):
        t[32 * j, C_SEL] = t[32 * j + 1, C_SEL + 1] = 1.0
    t[:, C_IOTA:C_IOTA + CAP] = np.arange(CAP, dtype=np.float32)
    t[:, C_UPPER:C_UPPER + P] = np.triu(np.ones((P, P), np.float32), 1)
    for w, size in enumerate(WINDOWS):
        lo, hi = size // 2, size - size // 2 - 1
        count = np.clip(tok + hi + 1, 0, TG) - np.clip(tok - lo, 0, TG)
        t[:, C_CNT + w * P:C_CNT + (w + 1) * P] = (1.0 / count).astype(np.float32)
    return t


INPUTS = ("x_prompt", "x_sample", "cache_k", "cache_v", "c", "c_ctx", "w_ada", "b_ada", "norm_mix_g",
          "norm_ffn_g", "w_in_ab", "pool_w", "pool_scale", "attn_sink", "w_out_ab", "conv_w1", "conv_b1",
          "conv_dw", "conv_dw_b", "conv_ln_g", "conv_ln_b", "conv_w2", "conv_b2", "router_grp", "router_exp",
          "moe_w1", "moe_w3", "moe_w2", "final_g")
OUTPUTS = (("y_prompt", (1, TG, D)), ("y_sample", (1, TG, D)), ("state_k", (1, 1, TG, 2, HD)),
           ("state_v", (1, 1, TG, 2, HD)))


def kernel(**inputs):
    import concourse.bacc as bacc
    from concourse.bass_utils import run_bass_kernel_spmd

    nc = bacc.Bacc("TRN2", target_bir_lowering=False, num_devices=1)
    arrays, args = {}, []
    for name in INPUTS:
        a = np.ascontiguousarray(inputs[name])
        arrays[f"in_{name}"] = a
        args.append(nc.dram_tensor(f"in_{name}", a.shape, mybir.dt.from_np(a.dtype), kind="ExternalInput").ap())
    arrays["in_shape_consts"] = shape_constants()
    args.append(nc.dram_tensor("in_shape_consts", (P, C_W), F32, kind="ExternalInput").ap())
    for name, shape in OUTPUTS:
        args.append(nc.dram_tensor(f"out_{name}", shape, F32, kind="ExternalOutput").ap())
    backbone(nc, *args)
    result = run_bass_kernel_spmd(nc, [arrays], core_ids=[0])
    return tuple(result.results[0][f"out_{name}"] for name, _ in OUTPUTS)
```

```python
from contextlib import ExitStack

import numpy as np

import concourse.bass as bass
from concourse import mybir

P = 128
ALU = mybir.AluOpType
ACT = mybir.ActivationFunctionType
F32 = mybir.dt.float32
AX = mybir.AxisListType

D = 1024
DC = D // P
TG = 128
NT = 2 * TG
HD = 64
NH = 8
NE = 16
FF = 512
FC = FF // P
EPS = 1e-6
SCALE = HD ** -0.5
TAPS = 31
HALF = TAPS // 2
UL = TG + 2 * HALF
WINDOWS = (2, 4, 8, 16)
APAD = 8
AL = TG + 2 * APAD
PE_CHUNKS = (6, 7)
AP_CHUNK = 5
DVE_CHUNKS = ((0, 1, 2), (3, 4))
UNROLL = 10
DIAGS = 16
BLOCK = 8
SLOTS = 6
PAIRS = NE // 2
CAP = 64
LIMITS = (CAP + 0.5, 2 * CAP + 0.5)
TW = 512

C_ID, C_ROT, C_COS, C_SIN, C_CNT, C_SEL, C_IOTA, C_UPPER, C_FIRST = 0, 128, 256, 384, 512, 1024, 1036, 1164, 1292
C_W = 1296

V_NMIX, V_NFFN, V_FIN, V_CB1, V_DWB, V_LNG, V_LNB, V_CB2, V_PSC, V_CCTX, V_C = (
    0, 16, 32, 40, 56, 64, 72, 80, 88, 92, 100)
V_ROWS = 108


def ada_keys(l, *parts):
    return [("ada", l, 2 * p + h) for p in parts for h in range(2)]


ADA_SCALE_0, ADA_SHIFT_0 = ada_keys(0, 1), ada_keys(0, 0)
ADA_PROJ_0 = ada_keys(0, 2, 3)
ADA_SOFTMAX_0 = ada_keys(0, 4)
ADA_ROOT = (ada_keys(0, 5), ada_keys(1, 5))
ADA_ROUTE_0 = ada_keys(1, 0, 1)
ADA_CONV = ada_keys(1, 2, 3)
ADA_LAYERNORM = ada_keys(1, 4)
ADA_GROUPS = (ADA_SCALE_0, ADA_SHIFT_0, ADA_PROJ_0, ADA_SOFTMAX_0, ADA_ROOT[0], ADA_ROUTE_0, ADA_CONV,
              ADA_LAYERNORM, ADA_ROOT[1])
ADA = {key: n for n, keys in enumerate(ADA_GROUPS) for key in keys}
ADA_MOST = max(len(keys) for keys in ADA_GROUPS)


def weight_stream():
    moe = lambda l: [(k, l, 2 * i + u) for i in range(PAIRS) for k in ("w1", "w3", "w2") for u in range(2)]
    return (ADA_SCALE_0 + ADA_SHIFT_0 + [("in", 0, n) for n in range(3)] + ADA_PROJ_0 + ADA_SOFTMAX_0
            + [("out", 0, n) for n in range(2)] + ADA_ROOT[0] + ADA_ROUTE_0 + moe(0)
            + [("cw1", 1, n) for n in (0, 2, 1, 3)] + ADA_CONV + ADA_LAYERNORM
            + [("cw2", 1, n) for n in range(2)] + ADA_ROOT[1] + moe(1))


STREAM = weight_stream()
TILE = {key: n for n, key in enumerate(STREAM)}
SPARE = SLOTS


def place_tiles():
    slots = []
    for n, key in enumerate(STREAM):
        experts = [TILE["w1", l, 0] for l in range(2)]
        if key[0] in ("w1", "w3", "w2"):
            pair, tile = divmod(n - experts[key[1]], SLOTS)
            slots.append(SPARE if tile == 0 and pair % 2 else tile)
            continue
        back = min(e for e in experts if e > n) - 1 - n
        if n < experts[0] and back > SLOTS:
            slots.append((SLOTS - 1 - (back - SLOTS - 1)) % SLOTS)
        else:
            slots.append(SLOTS - back % (SLOTS + 1))
    turns = [slots[:n + 1].count(s) for n, s in enumerate(slots)]
    before = [max((m for m in range(n) if slots[m] == s), default=None) for n, s in enumerate(slots)]
    before[slots.index(SPARE)] = TILE["out", 0, 0]
    return slots, turns, before


SLOT, TURN, BEFORE = place_tiles()


def backbone(nc, x_prompt, x_sample, cache_k, cache_v, c, c_ctx, w_ada, b_ada, norm_mix_g, norm_ffn_g,
             w_in_ab, pool_w, pool_scale, attn_sink, w_out_ab, conv_w1, conv_b1, conv_dw, conv_dw_b,
             conv_ln_g, conv_ln_b, conv_w2, conv_b2, router_grp, router_exp, moe_w1, moe_w3, moe_w2,
             final_g, shape_consts, y_prompt, y_sample, state_k, state_v):
    with ExitStack() as ctx:
        def sb(name, shape, dt=F32):
            return ctx.enter_context(nc.sbuf_tensor(name, shape, dt))

        def sem(name):
            return ctx.enter_context(nc.semaphore(name))

        ps = ctx.enter_context(nc.psum_tensor("ps", [P, 8, 512], F32))
        psx = ps[:, 0:4, :].rearrange("p b (h t) -> p (b h) t", h=2)
        ps_part = ps[:, 7, :]
        ps_ada = ps[:, 6, 384:480].rearrange("p (m g) -> p m g", g=2)
        ps_ada4 = ps[:, 6, 384:480].rearrange("p (n m g) -> p m n g", m=4, g=2)
        ps_norm = ps[:, 5, 0:NT]
        ps_rank = ps[:, 5, NT + 64:NT + 112].rearrange("p (s e) -> p s e", s=3)
        ps_logit = ps[:, 4:6, NT:NT + 32]

        ring = sb("ring", [P, SLOTS, DC * TW])
        cst = sb("cst", [P, C_W])
        ones = sb("ones", [P, P])
        zrow = sb("zrow", [1, 512])
        xtok = sb("xtok", [P, 2, D])
        diag = xtok[:, :, :].rearrange("p g d -> p (g d)").rearrange("p (n q) -> p n q", q=P)
        xT = sb("xT", [P, DC, NT])
        hT = sb("hT", [P, DC, NT])
        sq = sb("sq", [P, DC, NT])
        vec = sb("vec", [P, V_ROWS])
        bias = sb("bias", [P, 2, 48])
        dw = sb("dw", [P, DC, TAPS])
        wr = sb("wr", [P, 2, DC, 20])
        sinkrow = sb("sinkrow", [1, NH])
        sink = sb("sink", [P, NH])
        csil = sb("csil", [P, DC, 30 + 2 * ADA_MOST])
        part = sb("part", [P, 2, TW])
        mod = sb("mod", [P, 2, 48, 2])
        gain = sb("gain", [P, 2, 2, DC, 2])
        rstd = sb("rstd", [P, NT])
        root = sb("root", [P, NT])
        mean = sb("mean", [P, NT])
        mixT = hT
        spare = sb("spare", [P, DC * TW])
        poolw = spare[:, 0:4 * P].rearrange("p (n q) -> p n q", n=4)
        apad = spare[:, 4 * P:4 * P + 8 * AL].rearrange("p (n g t) -> p n g t", n=4, g=2)
        asum = spare[:, 4 * P + 8 * AL:4 * P + 24 * AL].rearrange("p (s n g t) -> p s n g t", s=2, n=4, g=2)
        stage = sb("stage", [P, 4 * NT + 10 * TG])
        qT = stage[:, 0:4 * NT].rearrange("p (c t) -> p c t", c=4)
        rt, rt2 = (stage[:, 4 * NT + 5 * TG * n:4 * NT + 5 * TG * (n + 1)].rearrange(
            "p (c t) -> p c t", c=5) for n in range(2))
        dense_sil = stage[:, 0:4 * NT].rearrange("p (c t) -> p c t", c=4)
        dense_act = stage[:, 4 * NT:8 * NT].rearrange("p (c t) -> p c t", c=4)
        kT = sb("kT", [P, 2, NT])
        ckT = sb("ckT", [P, 2, TG])
        cktok = sb("cktok", [P, P])
        cvtok = sb("cvtok", [P, P])
        kvctx = sb("kvctx", [P, 2 * P])
        vlat = sb("vlat", [P, P])
        smax = sb("smax", [P, 2, NH])
        nmax = sb("nmax", [P, 2, NH])
        rsum = sb("rsum", [P, 2, NH])
        esink = sb("esink", [P, 2, NH])
        rden = sb("rden", [P, 2, NH])
        work = sb("work", [P, 6144])
        rows_v = work[0:V_ROWS, 0:P]
        rows_b = work[0:96, P:2 * P]
        rows_r = work[0:80, 2 * P:6 * P]
        rows_dw = work[0:TAPS, 6 * P:6 * P + D]
        probs = work[:, 0:3072].rearrange("p (n k) -> p n k", k=TG)
        probsT = work[:, 3072:6144].rearrange("p (n k) -> p n k", k=TG)
        upad = work[:, 0:DC * 2 * UL].rearrange("p (c g t) -> p c g t", c=DC, g=2)
        conv = work[:, 2560:2560 + DC * NT].rearrange("p (c t) -> p c t", c=DC)
        pick = work[:, 0:2 * P].rearrange("p (g j) -> p g j", g=2)
        pick_gate = work[:, 2 * P:4 * P].rearrange("p (g j) -> p g j", g=2)
        spread = work[:, 4 * P:6 * P]
        hsel = work[:, 6 * P:14 * P].rearrange("p (k j) -> p k j", k=DC)
        sil = work[:, 14 * P:18 * P]
        hid = work[:, 18 * P:22 * P]
        hidT = work[:, 22 * P:26 * P].rearrange("p (f j) -> p f j", f=FC)
        ysel = work[:, 26 * P:34 * P]
        gate_diag = work[:, 34 * P:38 * P].rearrange("p (n t) -> p n t", n=4)
        gatebc = work[:, 38 * P:42 * P].rearrange("p (u t) -> p u t", u=2)
        htok = xtok
        eps = sb("eps", [P, 1])
        early = sb("early", [P, 1])
        mean4 = sb("mean4", [P, 2, TG])
        lg = sb("lg", [P, 2, 20])
        r1 = sb("r1", [P, 2, 16])
        rg = sb("rg", [P, 12, 2, 4])
        rs = sb("rs", [P, 12, 2])
        gate = sb("gate", [P, 2, NE + 2])
        slot = sb("slot", [P, 2, NE + 2])
        mask = sb("mask", [P, 2, NE])
        crowd = sb("crowd", [P, PAIRS])
        over = sb("over", [P, PAIRS])
        path = sb("path", [P, PAIRS], mybir.dt.int32)

        ident = cst[:, C_ID:C_ID + P]
        rot = cst[:, C_ROT:C_ROT + P]
        cos = cst[:, C_COS:C_COS + P]
        sin = cst[:, C_SIN:C_SIN + P]
        sel = cst[:, C_SEL:C_SEL + 2 * ADA_MOST]
        first = cst[:, C_FIRST:C_FIRST + 4]
        iota = cst[:, C_IOTA:C_IOTA + 2 * CAP]
        upper = cst[:, C_UPPER:C_UPPER + P]
        icnt = cst[:, C_CNT:C_CNT + 4 * P].rearrange("p (w t) -> p w t", w=4)

        slot_full = [sem(f"slot_full{s}") for s in range(SLOTS + 1)]
        tiles_used = sem("tiles_used")
        s_x = sem("s_x")
        s_cst = sem("s_cst")
        s_rows = sem("s_rows")
        s_rows_conv = sem("s_rows_conv")
        s_rows_dw = sem("s_rows_dw")
        dw_turned = sem("dw_turned")
        dw_ready = sem("dw_ready")
        s_kv = sem("s_kv")
        s_fill = sem("s_fill")
        s_xt = sem("s_xt")
        s_vt = sem("s_vt")
        s_prep = sem("s_prep")
        s_vec = sem("s_vec")
        s_csil = sem("s_csil")
        small_issued = sem("small_issued")
        part_done = sem("part_done")
        part_ready = sem("part_ready")
        mod_done = sem("mod_done")
        diag_ready = sem("diag_ready")
        diag_used = sem("diag_used")
        dconv_done = sem("dconv_done")
        dconv_ready = sem("dconv_ready")
        mod_taken = sem("mod_taken")
        x_ready = [sem(f"x_ready{n}") for n in range(5)]
        sq_ready = [sem(f"sq_ready{n}") for n in range(5)]
        ss_done = [sem(f"ss_done{n}") for n in range(5)]
        root_ready = [sem(f"root_ready{n}") for n in range(5)]
        hpre_ready = [sem(f"hpre_ready{n}") for n in range(5)]
        h_ready = [sem(f"h_ready{n}") for n in range(5)]
        y_done = [sem(f"y_done{n}") for n in range(4)]
        s_dve = sem("s_dve")
        s_act = sem("s_act")
        s_pool = sem("s_pool")
        qkv_done = sem("qkv_done")
        a_ready = sem("a_ready")
        qraw_ready = sem("qraw_ready")
        rot_done = sem("rot_done")
        qk_ready = sem("qk_ready")
        kv_ready = sem("kv_ready")
        scores_done = sem("scores_done")
        nmax_ready = sem("nmax_ready")
        exp_ready = sem("exp_ready")
        probs_ready = sem("probs_ready")
        pt_done = sem("pt_done")
        pt_ready = sem("pt_ready")
        pv_done = sem("pv_done")
        pooled_ready = sem("pooled_ready")
        pool_done = sem("pool_done")
        mix_ready = sem("mix_ready")
        glu_done = sem("glu_done")
        sig_ready = sem("sig_ready")
        u_ready = sem("u_ready")
        value_ready = sem("value_ready")
        product_ready = sem("product_ready")
        sum_done = sem("sum_done")
        gated_u_ready = sem("gated_u_ready")
        tap_done = sem("tap_done")
        conv_ready = sem("conv_ready")
        mean_done = sem("mean_done")
        mean_ready = sem("mean_ready")
        cent_ready = sem("cent_ready")
        csq_ready = sem("csq_ready")
        var_done = sem("var_done")
        croot_ready = sem("croot_ready")
        cn_ready = sem("cn_ready")
        cs_ready = sem("cs_ready")
        yb_ready = sem("yb_ready")
        route_done = sem("route_done")
        gexp_in = sem("gexp_in")
        gexp_out = sem("gexp_out")
        gate_ready = sem("gate_ready")
        mask_ready = sem("mask_ready")
        rank_done = sem("rank_done")
        htok_done = sem("htok_done")
        htok_ready = sem("htok_ready")
        pick_ready = [sem(f"pick_ready_round{r}") for r in range(2)]
        spread_done = [sem(f"spread_done_round{r}") for r in range(2)]
        spread_ready = [sem(f"spread_ready_round{r}") for r in range(2)]
        gather_done = [sem(f"gather_done_round{r}") for r in range(2)]
        hsel_lo = [sem(f"hsel_lo_round{r}") for r in range(2)]
        hsel_hi = [sem(f"hsel_hi_round{r}") for r in range(2)]
        sil_ready = [sem(f"sil_ready_round{r}") for r in range(2)]
        hid_ready = [sem(f"hid_ready_round{r}") for r in range(2)]
        turn_done = [sem(f"turn_done_round{r}") for r in range(2)]
        hidT_lo = [sem(f"hidT_lo_round{r}") for r in range(2)]
        hidT_hi = [sem(f"hidT_hi_round{r}") for r in range(2)]
        hid_done = [sem(f"hid_done_round{r}") for r in range(2)]
        ysel_done = [sem(f"ysel_done_round{r}") for r in range(2)]
        ysel_lo = [sem(f"ysel_lo_round{r}") for r in range(2)]
        ysel_hi = [sem(f"ysel_hi_round{r}") for r in range(2)]
        pair_done = sem("pair_done")
        gdiag_ready = sem("gdiag_ready")
        gatebc_done = sem("gatebc_done")
        gatebc_ready = sem("gatebc_ready")
        dense_done = sem("dense_done")
        dense_sil_ready = sem("dense_sil_ready")
        dense_act_ready = sem("dense_act_ready")
        picked = [sem(f"picked_round{r}") for r in range(2)]
        gated = sem("gated")
        out_t = sem("out_t")
        out_ready = [sem(f"out_ready{g}") for g in range(2)]
        s_out = sem("s_out")

        def place(n):
            return spare if SLOT[n] == SPARE else ring[:, SLOT[n], :]

        def wtile(key):
            w = place(TILE[key])
            return w.rearrange("p (k n) -> p k n", k=FC if key[0] == "w2" else DC)

        def landed(eng, key):
            n = TILE[key]
            eng.wait_ge(slot_full[SLOT[n]], 16 * TURN[n])

        def used(eng, key):
            eng.wait_ge(tiles_used, TILE[key] + 1)

        def product(eng, done, kind, l, k):
            if k % 4 < 2:
                eng.wait_ge(done, k // 4 + 1)
            else:
                used(eng, (kind, l, k // 4))

        SOURCE = {
            "ada": lambda l, n: w_ada[l, :, n * TW:(n + 1) * TW],
            "in": lambda l, n: w_in_ab[0, :, n * TW:min((n + 1) * TW, 1280)],
            "out": lambda l, n: w_out_ab[0, :, n * TW:(n + 1) * TW],
            "cw1": lambda l, n: conv_w1[0, :, n * TW:(n + 1) * TW],
            "cw2": lambda l, n: conv_w2[0, :, n * TW:(n + 1) * TW],
        }
        LAST_IN = ("in", 0, 2)

        block = ctx.enter_context(nc.Block())

        @block.sync
        def _(sp):
            def load(key):
                n = TILE[key]
                src = SOURCE[key[0]](key[1], key[2])
                width = src.shape[1]
                dst = place(n)[:, 0:DC * width].rearrange("p (k n) -> p k n", k=DC)
                if BEFORE[n] is not None:
                    sp.wait_ge(tiles_used, BEFORE[n] + 1)
                sp.dma_start(dst, src.rearrange("(k p) n -> p k n", p=P)).then_inc(slot_full[SLOT[n]], 16)

            for g, x in enumerate((x_prompt, x_sample)):
                sp.dma_start(xtok[:, g, :], x[0]).then_inc(s_x, 16)
            sp.wait_ge(small_issued, 2)
            for key in STREAM[:TILE["w1", 0, 0]]:
                load(key)

            def load_experts(l):
                first = TILE["w1", l, 0]

                def expert_tile(v, t, expert):
                    n = first + SLOTS * v + t
                    dst = place(n).rearrange("p (k n) -> p k n", k=FC if t >= 4 else DC)
                    src = (moe_w1, moe_w3, moe_w2)[t // 2][l, expert].rearrange("o (k p) n -> p (o k) n", p=P)
                    sp.dma_start(dst, src).then_inc(slot_full[SLOT[n]], 16)

                for v in range(2):
                    for t in range(SLOTS):
                        sp.wait_ge(tiles_used, BEFORE[first + SLOTS * v + t] + 1)
                        e = 2 * v + t % 2
                        expert_tile(v, t, slice(e, e + 1))
                with sp.Fori(1, PAIRS // 2) as h:
                    for v in range(2):
                        for t in range(SLOTS):
                            n = first + SLOTS * v + t - (2 * SLOTS if t == 0 else SLOTS)
                            sp.wait_ge(tiles_used, h * (2 * SLOTS) + (n + 1))
                            expert_tile(v, t, bass.ds(h * 4 + (2 * v + t % 2), 1))

            load_experts(0)
            for key in STREAM[TILE["w2", 0, NE - 1] + 1:TILE["w1", 1, 0]]:
                load(key)
            load_experts(1)
            for g, y in enumerate((y_prompt, y_sample)):
                sp.wait_ge(out_ready[g], 2)
                sp.dma_start(y[0], xtok[:, g, :]).then_inc(s_out, 16)
            sp.wait_ge(s_out, 64)

        @block.tensor
        def _(pe):
            def mm(out, lhsT, rhs, start=True, stop=True):
                return nc.tensor.matmul(out, lhsT, rhs, start=start, stop=stop, skip_group_check=True)

            def ada_rows(keys, j):
                landed(pe, keys[j])
                w = wtile(keys[j])
                if j == 0 and ADA[keys[0]]:
                    pe.wait_ge(part_ready, ADA[keys[0]])
                at = 2 * (ADA_MOST - 1 - j)
                for k in range(DC):
                    q = 32 * (k % 4)
                    last = mm(ps_part[q:q + 32, :], csil[:, k, at:at + 32], w[:, k, :], j == 0 and k < 4, True)
                last.then_inc(tiles_used, 1)

            def ada_turn(keys):
                n, a, b = ADA[keys[0]], keys[0][2], keys[-1][2] + 1
                pe.wait_ge(part_ready, n + 1)
                for m in range(4):
                    last = mm(ps_ada4[:, m, a:b, :], part[:, n % 2, m * P:(m + 1) * P], sel[:, 0:2 * (b - a)])
                last.then_inc(mod_done, 1)

            def ada(keys):
                for j in range(len(keys)):
                    ada_rows(keys, j)
                ada_turn(keys)

            def column_sums(dst, src, ready, count, done):
                for k in range(DC):
                    pe.wait_ge(ready, count(k))
                    last = mm(dst, ones[:, :], src[:, k, :], k == 0, k == DC - 1)
                last.then_inc(done, 1)

            def norm_sum(n, k):
                pe.wait_ge(sq_ready[n], k + 1)
                last = mm(ps_norm, ones[:, :], sq[:, k, :], k == 0, k == DC - 1)
                if k == DC - 1:
                    last.then_inc(ss_done[n], 1)

            def norm_sums(n, start=0):
                for k in range(start, DC):
                    norm_sum(n, k)

            pe.wait_ge(s_cst, 16)
            pe.wait_ge(s_x, 32)
            for k in range(DC):
                for g in range(2):
                    last = nc.tensor.transpose(psx[:, k, g * TG:(g + 1) * TG], xtok[:, g, k * P:(k + 1) * P],
                                               ident)
                if k % 2:
                    last.then_inc(s_xt, 1)
            pe.wait_ge(s_rows, 16 * 9)
            pe.wait_ge(s_rows_conv, 16 * 6)
            nc.tensor.transpose(ps[:, 4, 0:V_ROWS], rows_v[:, :], ident[0:V_ROWS, 0:V_ROWS])
            nc.tensor.transpose(ps[:, 4, 128:224], rows_b[:, :], ident[0:96, 0:96])
            rv = rows_r[:, :].rearrange("r (p e) -> r e p", e=4)
            for e in range(4):
                nc.tensor.transpose(ps[:, 6, e * 80:(e + 1) * 80], rv[:, e, :], ident[0:80, 0:80])
            pe.wait_ge(s_fill, 2)
            mm(ps[:, 4, 256:256 + NH], ones[0:1, :],
               sinkrow[0:1, :].rearrange("o (i r) -> o r i", r=2)).then_inc(s_vt, 1)

            pe.wait_ge(s_csil, 1)
            pe.wait_ge(s_prep, 1)
            norm_sums(0)
            ada(ADA_SCALE_0)
            pe.wait_ge(mod_taken, 1)
            pe.wait_ge(s_rows_dw, 16)
            for k in range(DC):
                last = nc.tensor.transpose(ps[:, 4, k * TAPS:(k + 1) * TAPS], rows_dw[:, k * P:(k + 1) * P],
                                           ident[0:TAPS, 0:TAPS])
            last.then_inc(dw_turned, 1)
            ada(ADA_SHIFT_0)

            def project(key, out, ready=None):
                landed(pe, key)
                w = wtile(key)
                for m in range(4):
                    for k in range(DC):
                        if ready is not None and m == 0:
                            pe.wait_ge(ready, k + 1)
                        last = mm(out(m), w[:, k, m * P:(m + 1) * P], hT[:, k, :], k == 0, k == DC - 1)
                last.then_inc(tiles_used, 1)

            project(("in", 0, 0), lambda m: psx[:, m, :], h_ready[0])
            project(("in", 0, 1), lambda m: psx[:, 4 + m, :])
            landed(pe, LAST_IN)
            pe.wait_ge(dw_ready, 1)
            w = place(TILE[LAST_IN])[:, 0:DC * 2 * P].rearrange("p (k n) -> p k n", k=DC)
            for k in range(DC):
                mm(ps[:, 4, 0:NT], w[:, k, 0:P], hT[:, k, :], k == 0, k == DC - 1)
            for k in range(DC):
                mm(ps[:, 5, 0:2 * P], hT[:, k, 0:TG], w[:, k, 0:2 * P], k == 0, k == DC - 1)
            for k in range(DC):
                last = mm(ps[:, 4, NT:NT + P], hT[:, k, TG:NT], w[:, k, P:2 * P], k == 0, k == DC - 1)
            last.then_inc(tiles_used, 1)
            pe.wait_ge(s_kv, 48)
            nc.tensor.transpose(ps[:, 4, NT + P:NT + 2 * P], cktok[:, :], ident).then_inc(qkv_done, 1)
            ada(ADA_PROJ_0)
            pe.wait_ge(qraw_ready, 2)
            mm(ps[:, 2, :], rot, qT[:, :, TG:NT])
            mm(ps[:, 4, 0:P], rot, kT[:, 0, TG:NT]).then_inc(rot_done, 1)
            pe.wait_ge(a_ready, 1)
            pe.wait_ge(kv_ready, 1)
            pe.wait_ge(qk_ready, 2)
            for i in range(4):
                for r in range(2):
                    lo, hi = 64 * r, 64 * r + 64
                    kv = (2 * i + r) // 4
                    mm(ps[:, r, i * P:(i + 1) * P], qT[lo:hi, i, 0:TG], kT[lo:hi, int(kv != r), 0:TG])
            nc_last = None
            for i in range(4):
                for keys in range(2):
                    for r in range(2):
                        lo, hi = 64 * r, 64 * r + 64
                        kv = (2 * i + r) // 4
                        at = (i % 2) * 2 * P + keys * P
                        k = ckT[lo:hi, int(kv != r), :] if keys else kT[lo:hi, int(kv != r), TG:NT]
                        nc_last = mm(ps[:, 2 + 2 * r + i // 2, at:at + P], qT[lo:hi, i, TG:NT], k)
            nc_last.then_inc(scores_done, 1)
            pe.wait_ge(mod_taken, 3)
            ada(ADA_SOFTMAX_0)
            for n in range(24):
                if n % 8 == 0:
                    pe.wait_ge(probs_ready, n // 8 + 1)
                last = nc.tensor.transpose(ps[:, n // 4, (n % 4) * P:(n % 4 + 1) * P], probs[:, n, :], ident)
                if n % 4 == 3:
                    last.then_inc(pt_done, 1)
            pe.wait_ge(pt_ready, 6)
            for i in range(4):
                for step in range(3):
                    for r in range(2):
                        h = r * 4 + i
                        kv = (2 * i + r) // 4
                        v = slice(64 * kv, 64 * kv + 64)
                        out = psx[64 * r:64 * r + 64, i, :]
                        if step == 0:
                            mm(out[:, 0:TG], kvctx[:, P + 64 * kv:P + 64 * kv + 64], probsT[:, h, :])
                        elif step == 1:
                            mm(out[:, TG:NT], vlat[:, v], probsT[:, 8 + 2 * h, :], True, False)
                        else:
                            last = mm(out[:, TG:NT], cvtok[:, v], probsT[:, 9 + 2 * h, :], False, True)
            last.then_inc(pv_done, 1)
            pe.wait_ge(pooled_ready, 1)
            for m in range(4):
                last = mm(psx[:, 4 + m, :], poolw[:, m, :], apad[:, m, :, APAD:APAD + TG])
            last.then_inc(pool_done, 1)
            pe.wait_ge(mix_ready, 2)
            for n in range(2):
                key = ("out", 0, n)
                landed(pe, key)
                w = wtile(key)
                for m in range(4):
                    for k in range(DC):
                        last = mm(psx[:, 4 * n + m, :], w[:, k, m * P:(m + 1) * P], mixT[:, k, :],
                                  k == 0, k == DC - 1)
                    if m == 1:
                        last.then_inc(y_done[0], 1)
                    if 4 * n + m == DC - 2:
                        for k in range(DC // 2):
                            norm_sum(1, k)
                last.then_inc(tiles_used, 1)
            norm_sums(1, DC // 2)

            def moe(l, n):
                pe.wait_ge(mod_taken, (4, 8)[l])
                for j in range(len(ADA_ROOT[l])):
                    ada_rows(ADA_ROOT[l], j)
                for k in range(DC):
                    pe.wait_ge(h_ready[n], k + 1)
                    for g in range(2):
                        last = mm(ps_logit[:, g, 0:20], hT[:, k, g * TG:(g + 1) * TG],
                                  wr[:, l, k, :], k == 0, k == DC - 1)
                last.then_inc(route_done, 1)
                ada_turn(ADA_ROOT[l])
                for g in range(2):
                    for k in range(DC):
                        last = nc.tensor.transpose(ps[:, 2 * g + k // 4, (k % 4) * P:(k % 4 + 1) * P],
                                                   hT[:, k, g * TG:(g + 1) * TG], ident)
                        if k % 4 == 3:
                            last.then_inc(htok_done, 1)
                if l == 0:
                    ada(ADA_ROUTE_0)
                pe.wait_ge(mask_ready, l + 1)
                mm(ps_rank[:, 0, :], upper, mask[:, 0, :])
                mm(ps_rank[:, 1, :], upper, mask[:, 1, :], True, False)
                mm(ps_rank[:, 1, :], ones[:, :], mask[:, 0, :], False, True)
                mm(ps_rank[:, 2, :], ones[:, :], mask[:, 0, :], True, False)
                mm(ps_rank[:, 2, :], ones[:, :], mask[:, 1, :], False, True).then_inc(rank_done, 1)
                pe.wait_ge(htok_ready, 4 * l + 4)
                for b in range(4):
                    mm(ps[:, b, :], zrow[0:1, 0:P], zrow[0:1, :])
                pe.wait_ge(gate_ready, l + 1)
                pe.wait_ge(mod_taken, (6, 9)[l])
                first = TILE["w1", l, 0]
                with pe.Fori(0, PAIRS // 2) as h:
                    for v in range(2):
                        i = h * 2 + v
                        w1, w3, w2 = ([place(first + SLOTS * v + 2 * j + u).rearrange("p (k n) -> p k n", k=k)
                                       for u in range(2)] for j, k in ((0, DC), (1, DC), (2, FC)))
                        n = i + l * PAIRS

                        def tile_landed(j):
                            t = first + SLOTS * v
                            if j == 0:
                                pe.wait_ge(slot_full[SLOT[t]], h * 16 + 16 * TURN[t])
                            else:
                                pe.wait_ge(slot_full[j], i * 16 + 16 * TURN[first + j])

                        way = pe.value_load(path[0:1, bass.ds(i, 1)], min_val=0, max_val=2)
                        def compact(r, last_round):
                            pe.wait_ge(pick_ready[r], n + (l + 1 if r == 0 else 1))
                            for g in range(2):
                                last = nc.tensor.transpose(ps[:, 7, g * TG:(g + 1) * TG], pick_gate[:, g, :], ident)
                            last.then_inc(spread_done[r], 1)
                            for k in range(DC):
                                for g in range(2):
                                    last = mm(ps[:, 4 + k // 4, (k % 4) * P:(k % 4 + 1) * P],
                                              htok[:, g, k * P:(k + 1) * P], pick[:, g, :], g == 0, g == 1)
                                if k % 4 == 3:
                                    last.then_inc(gather_done[r], 1)
                            for w, bank, j in ((w1, 6, 0), (w3, 7, 2)):
                                tile_landed(j)
                                tile_landed(j + 1)
                                if j == 0:
                                    pe.wait_ge(hsel_lo[r], n + 1)
                                else:
                                    pe.wait_ge(spread_ready[r], n + 1)
                                for k in range(DC):
                                    if j == 0 and k == 4:
                                        pe.wait_ge(hsel_hi[r], n + 1)
                                    for u in range(2):
                                        c = slice(CAP * u, CAP * u + CAP)
                                        last = mm(ps[c, bank, :], hsel[:, k, c], w[u][:, k, :], k == 0, k == DC - 1)
                                    if k == 0 and j == 2 and last_round:
                                        pe.wait_ge(hid_done[r], n * 2 + 1)
                                        pe.sem_inc(tiles_used, 2)
                                last.then_inc(hid_done[r], 1)
                            for f in range(FC):
                                if f == 2 and last_round:
                                    pe.sem_inc(tiles_used, 2)
                                if f % 2 == 0:
                                    pe.wait_ge(hid_ready[r], n * 2 + (f // 2 + 1))
                                last = nc.tensor.transpose(ps[:, 6 + f // 2, (f % 2) * P:(f % 2 + 1) * P],
                                                           hid[:, f * P:(f + 1) * P], ident)
                                if f % 2:
                                    last.then_inc(turn_done[r], 1)
                            tile_landed(4)
                            tile_landed(5)
                            for h in range(2):
                                for f in range(FC):
                                    if h == 0 and f % 2 == 0:
                                        pe.wait_ge((hidT_lo[r], hidT_hi[r])[f // 2], n + 1)
                                    for u in range(2):
                                        c = slice(CAP * u, CAP * u + CAP)
                                        last = mm(ps[c, 4 + h, :], hidT[:, f, c], w2[u][:, f, h * 512:(h + 1) * 512],
                                                  f == 0, f == FC - 1)
                                last.then_inc(ysel_done[r], 1)
                            pe.wait_ge(ysel_lo[r], n + 1)
                            for m in range(DC):
                                if m == 4:
                                    pe.wait_ge(ysel_hi[r], n + 1)
                                last = mm(psx[:, m, :], ysel[:, m * P:(m + 1) * P], spread, False, True)
                                if m == 0 and last_round:
                                    pe.wait_ge(ysel_done[r], n * 2 + 2)
                                    pe.sem_inc(tiles_used, 2)
                            if last_round:
                                last.then_inc(pair_done, 1)

                        with pe.If(way == 0):
                            compact(0, True)
                            pe.sem_inc(spread_done[1], 1)
                            pe.sem_inc(gather_done[1], 2)
                            pe.sem_inc(turn_done[1], 2)
                            pe.sem_inc(ysel_done[1], 2)
                            pe.sem_inc(hid_done[1], 2)
                            pe.sem_inc(gatebc_done, 1)
                            pe.sem_inc(dense_done, 2 * FC)
                        with pe.Else():
                            with pe.If(way == 1):
                                compact(0, False)
                                compact(1, True)
                                pe.sem_inc(gatebc_done, 1)
                                pe.sem_inc(dense_done, 2 * FC)
                            with pe.Else():
                                pe.wait_ge(gdiag_ready, n + 1)
                                mm(ps[:, 4, :], ones[:, :], gate_diag).then_inc(gatebc_done, 1)
                                pe.wait_ge(gatebc_ready, n + 1)
                                for u in range(2):
                                    tile_landed(u)
                                    tile_landed(2 + u)
                                    for m in range(FC):
                                        for w, at in ((w1[u], 0), (w3[u], NT)):
                                            for k in range(DC):
                                                last = mm(ps[:, 4 + m, at:at + NT], w[:, k, m * P:(m + 1) * P],
                                                          hT[:, k, :], k == 0, k == DC - 1)
                                        last.then_inc(dense_done, 1)
                                    tile_landed(4 + u)
                                    for f in range(FC):
                                        pe.wait_ge(dense_act_ready, n * 2 * FC + (FC * u + f + 1))
                                        for m in range(DC):
                                            last = mm(psx[:, m, :], w2[u][:, f, m * P:(m + 1) * P], dense_act[:, f, :],
                                                      False, True)
                                            if f == m == 0:
                                                last.then_inc(tiles_used, 1 + 2 * u)
                                last.then_inc(pair_done, 1)
                                for r in range(2):
                                    pe.sem_inc(spread_done[r], 1)
                                    pe.sem_inc(gather_done[r], 2)
                                    pe.sem_inc(turn_done[r], 2)
                                    pe.sem_inc(ysel_done[r], 2)
                                    pe.sem_inc(hid_done[r], 2)
                                pe.wait_ge(pair_done, n + 1)
                                pe.sem_inc(tiles_used, 2)

            moe(0, 1)
            norm_sums(2)

            for h in range(2):
                for half, j in ((0, 0), (1, 2)):
                    key = ("cw1", 1, h + j)
                    landed(pe, key)
                    w = wtile(key)
                    for m in range(4):
                        b = (4 * h + m) % 6
                        if half == 0 and 4 * h + m >= 6:
                            pe.wait_ge(u_ready, 4 * h + m - 5)
                        for k in range(DC):
                            if h == 0 and half == 0 and m == 0:
                                pe.wait_ge(h_ready[2], k + 1)
                            last = mm(ps[:, b, half * NT:(half + 1) * NT], w[:, k, m * P:(m + 1) * P],
                                      hT[:, k, :], k == 0, k == DC - 1)
                        if half and m < 3:
                            last.then_inc(glu_done, 1)
                    last.then_inc(tiles_used, 1)
            pe.wait_ge(mod_taken, 6)
            for n in range(len(PE_CHUNKS) * (TAPS + 1)):
                j, t = divmod(n, TAPS + 1)
                k = PE_CHUNKS[j]
                if t == 0:
                    pe.wait_ge(gated_u_ready, j + 2)
                    pe.wait_ge(u_ready, 4)
                pe.wait_ge(diag_ready, n + 1)
                rows = upad[:, k, :, t:t + TG] if t < TAPS else ones[:, 0:1].unsqueeze(2).to_broadcast([P, 2, TG])
                last = mm(ps[:, 2 + j, 0:NT], diag[:, n % DIAGS, :], rows, t == 0, t == TAPS)
                last.then_inc(diag_used if t < TAPS else dconv_done, 1)
                b = n // BLOCK
                if n % BLOCK == BLOCK - 1 and b <= len(ADA_CONV):
                    if b < len(ADA_CONV):
                        ada_rows(ADA_CONV, b)
                    else:
                        ada_turn(ADA_CONV)
            pe.wait_ge(conv_ready, 1)
            pe.wait_ge(sum_done, TAPS - 1)
            pe.wait_ge(dconv_ready, len(PE_CHUNKS))
            column_sums(ps[:, 5, 0:NT], conv, conv_ready, lambda k: 1, mean_done)
            ada_rows(ADA_LAYERNORM, 0)
            column_sums(ps[:, 4, 0:NT], sq, csq_ready, lambda k: k + 1, var_done)
            ada_rows(ADA_LAYERNORM, 1)
            for n in range(2):
                key = ("cw2", 1, n)
                landed(pe, key)
                w = wtile(key)
                for m in range(4):
                    for k in range(DC):
                        if n == 0 and m == 0:
                            pe.wait_ge(cs_ready, k + 1)
                        last = mm(psx[:, 4 * n + m, :], w[:, k, m * P:(m + 1) * P], hT[:, k, :],
                                  k == 0, k == DC - 1)
                    if m == 1:
                        last.then_inc(y_done[2], 1)
                    if 4 * n + m == DC - 2:
                        for k in range(DC // 2):
                            norm_sum(3, k)
                last.then_inc(tiles_used, 1)
                if n == 0:
                    pe.wait_ge(mod_taken, 7)
                    ada_turn(ADA_LAYERNORM)
            norm_sums(3, DC // 2)
            moe(1, 3)
            norm_sums(4)
            for g in range(2):
                for k in range(DC):
                    pe.wait_ge(hpre_ready[4], g * DC + k + 1)
                    last = nc.tensor.transpose(ps[:, 2 * g + k // 4, (k % 4) * P:(k % 4 + 1) * P],
                                               hT[:, k, g * TG:(g + 1) * TG], ident)
                    if k % 4 == 3:
                        last.then_inc(out_t, 1)

        @block.scalar
        def _(act):
            def vrow(at, src):
                n = src.shape[0] // P
                act.dma_start(rows_v[at:at + n, :], src.rearrange("(r p) -> r p", p=P)).then_inc(s_rows, 16)

            act.dma_start(cst[:, :], shape_consts).then_inc(s_cst, 16)
            vrow(V_CCTX, c_ctx)
            vrow(V_C, c[0])
            act.dma_start(rows_v[V_NMIX:V_NMIX + 16, :],
                          norm_mix_g.rearrange("l (r p) -> (l r) p", p=P)).then_inc(s_rows, 16)
            act.dma_start(rows_v[V_NFFN:V_NFFN + 16, :],
                          norm_ffn_g.rearrange("l (r p) -> (l r) p", p=P)).then_inc(s_rows, 16)
            vrow(V_FIN, final_g)
            act.dma_start(rows_b[:, :], b_ada.rearrange("l (r p) -> (l r) p", p=P)).then_inc(s_rows, 16)
            act.dma_start(rows_r[0:64, :],
                          router_exp.rearrange("l g (c p) e -> (l g c) (p e)", p=P)).then_inc(s_rows, 16)
            act.dma_start(rows_r[64:80, :],
                          router_grp.rearrange("l (c p) e -> (l c) (p e)", p=P)).then_inc(s_rows, 16)
            act.dma_start(sinkrow[:, :], attn_sink).then_inc(s_rows, 16)
            act.sem_inc(small_issued, 1)

            act.wait_ge(s_vec, 1)
            act.wait_ge(s_fill, 1)
            nc.scalar.activation(csil[:, :, 2 * ADA_MOST - 2:2 * ADA_MOST].rearrange("p k g -> p g k"), vec[:, V_CCTX:V_CCTX + 2 * DC].rearrange("p (g k) -> p g k", g=2),
                                 ACT.Silu).then_inc(s_csil, 1)

            def load_sqrt():
                nc.scalar.activation(early[:, :], eps[:, :], ACT.Sqrt)

            def squares(n, start, stop):
                for k in range(start, stop):
                    act.wait_ge(x_ready[n], k + 1)
                    nc.scalar.activation(sq[:, k, :], xT[:, k, :], ACT.Square).then_inc(sq_ready[n], 1)

            def norm_act(n, shift, meanwhile=None, start=0):
                if start == 0:
                    load_sqrt()
                squares(n, start, DC)
                act.wait_ge(ss_done[n], 1)
                nc.scalar.activation(root[:, :], ps_norm, ACT.Sqrt, bias=eps[:, 0:1],
                                     scale=1.0 / D).then_inc(root_ready[n], 1)
                if meanwhile is not None:
                    meanwhile()
                if shift is None:
                    return
                if n == 0:
                    act.wait_ge(mod_taken, 2)
                for k in range(DC):
                    act.wait_ge(hpre_ready[n], k + 1)
                    for g in range(2):
                        last = nc.scalar.activation(hT[:, k, g * TG:(g + 1) * TG], hT[:, k, g * TG:(g + 1) * TG],
                                                    ACT.Identity, bias=mod[:, shift[0], shift[1] + k, g:g + 1])
                    last.then_inc(h_ready[n], 1)

            def take_part(keys):
                n = ADA[keys[0]]
                used(act, keys[-1])
                if n >= 2:
                    act.wait_ge(mod_done, n - 1)
                nc.scalar.activation(part[:, n % 2, :], ps_part, ACT.Copy).then_inc(part_ready, 1)

            def take_first_parts():
                take_part(ADA_SCALE_0)
                take_part(ADA_SHIFT_0)

            act.wait_ge(s_fill, 2)
            norm_act(0, (0, 0), take_first_parts)
            used(act, ("in", 0, 0))
            act.wait_ge(s_fill, 3)
            nc.scalar.activation(apad[:, :, :, APAD:APAD + TG],
                                 psx[:, 0:4, :].rearrange("p c (g t) -> p c g t", g=2), ACT.Copy).then_inc(a_ready, 1)
            act.wait_ge(qkv_done, 1)
            nc.scalar.activation(kvctx[:, :], ps[:, 5, 0:2 * P], ACT.Copy).then_inc(kv_ready, 1)
            act.wait_ge(kv_ready, 1)
            act.dma_start(state_k[0, 0].rearrange("t h d -> t (h d)"), kvctx[:, 0:P]).then_inc(s_out, 16)
            act.dma_start(state_v[0, 0].rearrange("t h d -> t (h d)"), kvctx[:, P:2 * P]).then_inc(s_out, 16)
            take_part(ADA_PROJ_0)
            act.wait_ge(nmax_ready, 1)
            for h in range(NH):
                nc.scalar.activation(probs[:, h, :], ps[:, h // 4, (h % 4) * P:(h % 4 + 1) * P], ACT.Exp,
                                     bias=nmax[:, 0, h:h + 1], scale=SCALE,
                                     accum_out=rsum[:, 0, h:h + 1]).then_inc(exp_ready, 1)
            for h in range(NH):
                nc.scalar.activation(probs[:, 8 + 2 * h:10 + 2 * h, :],
                                     ps[:, 2 + h // 2, (h % 2) * NT:(h % 2 + 1) * NT].rearrange(
                                         "p (s k) -> p s k", s=2), ACT.Exp,
                                     bias=nmax[:, 1, h:h + 1], scale=SCALE,
                                     accum_out=rsum[:, 1, h:h + 1]).then_inc(exp_ready, 1)
            act.wait_ge(nmax_ready, 2)
            nc.scalar.activation(esink[:, :, :], esink[:, :, :], ACT.Exp).then_inc(exp_ready, 1)
            take_part(ADA_SOFTMAX_0)
            for b in (1, 3, 5):
                act.wait_ge(pt_done, b + 1)
                nc.scalar.activation(probsT[:, 4 * b:4 * b + 4, :], ps[:, b, :], ACT.Copy).then_inc(pt_ready, 1)
            act.wait_ge(pv_done, 1)
            nc.scalar.activation(mixT[:, 4:8, :], psx[:, 0:4, :], ACT.Copy).then_inc(mix_ready, 1)
            norm_act(1, (0, 24))
            take_part(ADA_ROOT[0])

            def moe_act(l):
                for b in range(4):
                    act.wait_ge(htok_done, 4 * l + b + 1)
                    nc.scalar.activation(htok[:, b // 2, (b % 2) * 512:(b % 2 + 1) * 512], ps[:, b, :],
                                         ACT.Copy).then_inc(htok_ready, 1)
                act.wait_ge(gexp_in, l + 1)
                nc.scalar.activation(rs[:, 2:4, :], rs[:, 0:2, :], ACT.Exp).then_inc(gexp_out, 1)
                nc.scalar.activation(rg[:, 1], rg[:, 0], ACT.Exp).then_inc(gexp_out, 1)
                if l == 0:
                    take_part(ADA_ROUTE_0)
                act.wait_ge(gate_ready, l + 1)
                first = TILE["w1", l, 0]
                with act.Fori(0, PAIRS) as i:
                    n = i + l * PAIRS
                    way = act.value_load(path[0:1, bass.ds(i, 1)], min_val=0, max_val=2)
                    def compact(r, last_round):
                        act.wait_ge(gather_done[r], n * 2 + 1)
                        nc.scalar.activation(hsel[:, 0:4, :], ps[:, 4, :].rearrange("p (k j) -> p k j", k=4),
                                             ACT.Copy).then_inc(hsel_lo[r], 1)
                        act.wait_ge(hid_done[r], n * 2 + 1)
                        nc.scalar.activation(sil, ps[:, 6, :], ACT.Silu).then_inc(sil_ready[r], 1)
                        act.wait_ge(turn_done[r], n * 2 + 1)
                        nc.scalar.activation(hidT[:, 0:2, :], ps[:, 6, 0:2 * P].rearrange("p (f j) -> p f j", f=2),
                                             ACT.Copy).then_inc(hidT_lo[r], 1)
                        act.wait_ge(ysel_done[r], n * 2 + 1)
                        nc.scalar.activation(ysel[:, 0:512], ps[:, 4, :], ACT.Copy).then_inc(ysel_lo[r], 1)

                    with act.If(way == 0):
                        compact(0, True)
                        act.sem_inc(hsel_lo[1], 1)
                        act.sem_inc(sil_ready[1], 1)
                        act.sem_inc(hidT_lo[1], 1)
                        act.sem_inc(ysel_lo[1], 1)
                        act.sem_inc(dense_sil_ready, 2 * FC)
                    with act.Else():
                        with act.If(way == 1):
                            compact(0, False)
                            compact(1, True)
                            act.sem_inc(dense_sil_ready, 2 * FC)
                        with act.Else():
                            for u in range(2):
                                for m in range(FC):
                                    act.wait_ge(dense_done, n * 2 * FC + (FC * u + m + 1))
                                    if u:
                                        act.wait_ge(dense_act_ready, n * 2 * FC + (m + 1))
                                    nc.scalar.activation(dense_sil[:, m, :], ps[:, 4 + m, 0:NT],
                                                         ACT.Silu).then_inc(dense_sil_ready, 1)
                            for r in range(2):
                                act.sem_inc(hsel_lo[r], 1)
                                act.sem_inc(sil_ready[r], 1)
                                act.sem_inc(hidT_lo[r], 1)
                                act.sem_inc(ysel_lo[r], 1)

            moe_act(0)
            norm_act(2, (1, 0))
            def sigmoids(a, b):
                for m in range(a, b):
                    if m % 4 == 3:
                        used(act, ("cw1", 1, 2 + m // 4))
                    else:
                        act.wait_ge(glu_done, 3 * (m // 4) + m % 4 + 1)
                    nc.scalar.activation(sq[:, m, :], ps[:, m % 6, NT:2 * NT], ACT.Sigmoid,
                                         bias=vec[:, V_CB1 + DC + m:V_CB1 + DC + m + 1]).then_inc(sig_ready, 1)
                    if m >= AP_CHUNK:
                        act.wait_ge(u_ready, 1)
                        nc.scalar.activation(upad[:, m, :, HALF:HALF + TG],
                                             ps[:, m % 6, 0:NT].rearrange("p (g t) -> p g t", g=2), ACT.Identity,
                                             bias=vec[:, V_CB1 + m:V_CB1 + m + 1]).then_inc(value_ready, 1)

            def diagonals(b):
                for n in range(b * BLOCK, (b + 1) * BLOCK):
                    j, t = divmod(n, TAPS + 1)
                    k = PE_CHUNKS[j]
                    if n >= DIAGS:
                        before = n - DIAGS
                        if before % (TAPS + 1) == TAPS:
                            act.wait_ge(dconv_done, before // (TAPS + 1) + 1)
                        else:
                            act.wait_ge(diag_used, before - before // (TAPS + 1) + 1)
                    tap = dw[:, k, t:t + 1] if t < TAPS else vec[:, V_DWB + k:V_DWB + k + 1]
                    nc.scalar.activation(diag[:, n % DIAGS, :], ident, ACT.Copy, scale=tap).then_inc(diag_ready, 1)

            def products(start, stop):
                k = AP_CHUNK
                for t in range(start, min(stop, TAPS)):
                    rows = upad[:, k, :, t:t + TG]
                    if t == 0:
                        act.wait_ge(gated_u_ready, 1)
                        act.wait_ge(u_ready, 4)
                        nc.scalar.activation(cv5, rows, ACT.Identity, scale=dw[:, k, 0:1],
                                             bias=vec[:, V_DWB + k:V_DWB + k + 1]).then_inc(product_ready, 1)
                    else:
                        if t > 4:
                            act.wait_ge(sum_done, t - 4)
                        nc.scalar.activation(sq[:, t % 4, :].rearrange("p (g t) -> p g t", g=2), rows, ACT.Copy,
                                             scale=dw[:, k, t:t + 1]).then_inc(product_ready, 1)

            cv5 = conv[:, AP_CHUNK, :].rearrange("p (g t) -> p g t", g=2)
            blocks = len(PE_CHUNKS) * (TAPS + 1) // BLOCK
            sigmoids(0, 4)
            diagonals(0)
            diagonals(1)
            sigmoids(4, DC)
            for b in range(blocks):
                if b == len(ADA_CONV):
                    take_part(ADA_CONV)
                if b + 2 < blocks:
                    diagonals(b + 2)
                    products(6 * b, 6 * b + 6)
            for j, k in enumerate(PE_CHUNKS):
                act.wait_ge(dconv_done, j + 1)
                nc.scalar.activation(conv[:, k, :], ps[:, 2 + j, 0:NT], ACT.Copy).then_inc(dconv_ready, 1)
            act.wait_ge(mean_done, 1)
            nc.scalar.activation(mean[:, :], ps[:, 5, 0:NT], ACT.Copy, scale=1.0 / D).then_inc(mean_ready, 1)
            load_sqrt()
            for k in range(DC):
                act.wait_ge(cent_ready, k + 1)
                nc.scalar.activation(sq[:, k, :], conv[:, k, :], ACT.Square).then_inc(csq_ready, 1)
            act.wait_ge(var_done, 1)
            nc.scalar.activation(root[:, :], ps[:, 4, 0:NT], ACT.Sqrt, bias=eps[:, 0:1],
                                 scale=1.0 / D).then_inc(croot_ready, 1)
            for k in range(DC):
                act.wait_ge(cn_ready, k + 1)
                nc.scalar.activation(hT[:, k, :], conv[:, k, :], ACT.Silu, bias=vec[:, V_LNB + k:V_LNB + k + 1],
                                     scale=vec[:, V_LNG + k:V_LNG + k + 1]).then_inc(cs_ready, 1)
            take_part(ADA_LAYERNORM)
            for k in range(DC):
                if k == DC // 2 + 1:
                    load_sqrt()
                    squares(3, 0, DC // 2)
                product(act, y_done[2], "cw2", 1, k)
                nc.scalar.activation(sq[:, k, :], psx[:, k, :], ACT.Identity,
                                     bias=vec[:, V_CB2 + k:V_CB2 + k + 1]).then_inc(yb_ready, 1)
            norm_act(3, (1, 24), start=DC // 2)
            take_part(ADA_ROOT[1])
            moe_act(1)
            norm_act(4, None)
            for b in range(3):
                act.wait_ge(out_t, b + 1)
                nc.scalar.activation(xtok[:, b // 2, (b % 2) * 512:(b % 2 + 1) * 512], ps[:, b, :],
                                     ACT.Copy).then_inc(out_ready[b // 2], 1)

        @block.gpsimd
        def _(pool):
            def vrow(at, src):
                n = src.shape[0] // P
                pool.dma_start(rows_v[at:at + n, :], src.rearrange("(r p) -> r p", p=P)).then_inc(s_rows_conv, 16)

            vrow(V_CB1, conv_b1[0])
            vrow(V_DWB, conv_dw_b[0])
            vrow(V_LNG, conv_ln_g[0])
            vrow(V_LNB, conv_ln_b[0])
            vrow(V_CB2, conv_b2[0])
            vrow(V_PSC, pool_scale[0])
            pool.dma_start(rows_dw[:, :], conv_dw[0]).then_inc(s_rows_dw, 16)
            pool.dma_start(cktok[:, :], cache_k[0, 0].rearrange("t h d -> t (h d)")).then_inc(s_kv, 16)
            pool.dma_start(cvtok[:, :], cache_v[0, 0].rearrange("t h d -> t (h d)")).then_inc(s_kv, 16)
            pool.dma_start(poolw[:, :, :], pool_w[0].rearrange("g c d -> c g d")).then_inc(s_kv, 16)
            pool.sem_inc(small_issued, 1)
            nc.gpsimd.memset(csil[:, :, :], 0.0).then_inc(s_fill, 1)
            nc.gpsimd.memset(ones[:, :], 1.0)
            nc.gpsimd.memset(eps[:, :], EPS)
            nc.gpsimd.memset(gate[:, :, :], 0.0)
            nc.gpsimd.memset(slot[:, :, :], -1.0)
            nc.gpsimd.memset(zrow[:, :], 0.0).then_inc(s_fill, 1)
            nc.gpsimd.memset(apad[:, :, :, :], 0.0).then_inc(s_fill, 1)
            pool.wait_ge(a_ready, 1)
            src, at = apad, 0
            for n in range(4):
                step = 1 << n
                length = AL - 2 * step + 1
                dst = asum[:, n % 2]
                nc.gpsimd.tensor_tensor(dst[:, n:4, :, 0:length], src[:, n:4, :, 0:length],
                                        src[:, n:4, :, step:step + length], ALU.add).then_inc(s_pool, 1)
                pool.wait_ge(s_pool, 3 * n + 1)
                lo = APAD - WINDOWS[n] // 2
                nc.gpsimd.tensor_tensor(mean4[:, :, :], dst[:, n, :, lo:lo + TG],
                                        icnt[:, n:n + 1, :].to_broadcast([P, 2, TG]), ALU.mult).then_inc(s_pool, 1)
                pool.wait_ge(s_pool, 3 * n + 2)
                last = nc.gpsimd.tensor_tensor(apad[:, n, :, APAD:APAD + TG], mean4[:, :, :],
                                               apad[:, n, :, APAD:APAD + TG], ALU.subtract).then_inc(s_pool, 1)
                pool.wait_ge(s_pool, 3 * n + 3)
                src = dst
            pool.sem_inc(pooled_ready, 1)
            for j, k in enumerate((AP_CHUNK,) + PE_CHUNKS):
                pool.wait_ge(value_ready, j + 1)
                rows = upad[:, k, :, HALF:HALF + TG]
                nc.gpsimd.tensor_tensor(rows, rows, sq[:, k, :].rearrange("p (g t) -> p g t", g=2),
                                        ALU.mult).then_inc(gated_u_ready, 1)
            total = conv[:, AP_CHUNK, :]
            for t in range(1, TAPS):
                pool.wait_ge(product_ready, t + 1)
                if t > 1:
                    pool.wait_ge(sum_done, t - 1)
                nc.gpsimd.tensor_tensor(total, total, sq[:, t % 4, :], ALU.add).then_inc(sum_done, 1)

        @block.vector
        def _(dve):
            chain = [0]
            V = nc.vector

            def link(ins):
                chain[0] += 1
                ins.then_inc(s_dve, 1)
                dve.wait_ge(s_dve, chain[0])

            def take_mod(l, p0, p1):
                dve.wait_ge(mod_done, ADA["ada", l, 2 * p1 - 1] + 1)
                a, b = 8 * p0, 8 * p1
                link(V.tensor_tensor(mod[:, l, a:b, :], ps_ada[:, a:b, :],
                                     bias[:, l, a:b].unsqueeze(2).to_broadcast([P, b - a, 2]), ALU.add))
                for which, p, v in ((0, 1, V_NMIX), (1, 4, V_NFFN)):
                    if p0 <= p < p1:
                        g = vec[:, v + DC * l:v + DC * (l + 1)].unsqueeze(2).to_broadcast([P, DC, 2])
                        link(V.scalar_tensor_tensor(out=gain[:, l, which], in0=mod[:, l, 8 * p:8 * p + 8, :],
                                                    scalar=1.0, in1=g, op0=ALU.add, op1=ALU.mult))
                dve.sem_inc(mod_taken, 1)

            def norm_root(n):
                dve.wait_ge(root_ready[n], 1)
                link(V.reciprocal(rstd[:, :], root[:, :]))

            def norm_dve(n, g_of):
                norm_root(n)
                norm_rows(n, g_of)

            def norm_rows(n, g_of):
                for k in range(DC):
                    for g in range(2):
                        t = slice(g * TG, (g + 1) * TG)
                        last = V.scalar_tensor_tensor(out=hT[:, k, t], in0=xT[:, k, t], scalar=g_of(k, g),
                                                      in1=rstd[:, t], op0=ALU.mult, op1=ALU.mult)
                    last.then_inc(hpre_ready[n], 1)

            def residual(n, y, l, part, ready):
                for k in range(DC):
                    ready(k)
                    for g in range(2):
                        t = slice(g * TG, (g + 1) * TG)
                        last = V.scalar_tensor_tensor(out=xT[:, k, t], in0=y[:, k, t],
                                                      scalar=mod[:, l, 8 * part + k, g:g + 1],
                                                      in1=xT[:, k, t], op0=ALU.mult, op1=ALU.add)
                    last.then_inc(x_ready[n], 1)

            for k in range(DC):
                dve.wait_ge(s_xt, k // 2 + 1)
                V.tensor_copy(xT[:, k, :], psx[:, k, :]).then_inc(x_ready[0], 1)
            dve.wait_ge(s_vt, 1)
            V.tensor_copy(vec[:, :], ps[:, 4, 0:V_ROWS]).then_inc(s_vec, 1)
            V.tensor_copy(bias[:, :, :], ps[:, 4, 128:224].rearrange("p (l m) -> p l m", l=2))
            V.tensor_copy(sink[:, :], ps[:, 4, 256:256 + NH])
            pr = ps[:, 6, 0:320].rearrange("p (e r) -> p e r", e=4)
            for l in range(2):
                for g in range(4):
                    V.tensor_copy(wr[:, l, :, 4 * g:4 * g + 4],
                                  pr[:, :, 32 * l + 8 * g:32 * l + 8 * g + 8].rearrange("p e c -> p c e"))
                last = V.tensor_copy(wr[:, l, :, 16:20], pr[:, :, 64 + 8 * l:72 + 8 * l].rearrange("p e c -> p c e"))
            last.then_inc(s_prep, 1)
            dve.wait_ge(s_prep, 1)
            norm_root(0)
            take_mod(0, 1, 2)
            norm_rows(0, lambda k, g: gain[:, 0, 0, k, g:g + 1])
            take_mod(0, 0, 1)
            dve.wait_ge(dw_turned, 1)
            V.tensor_copy(dw[:, :, :], ps[:, 4, 0:DC * TAPS].rearrange("p (c t) -> p c t", c=DC)).then_inc(dw_ready, 1)

            dve.wait_ge(qkv_done, 1)
            V.tensor_copy(qT, psx[:, 4:8, :]).then_inc(qraw_ready, 1)
            V.tensor_copy(kT[:, 0, :], ps[:, 4, 0:NT])
            V.tensor_copy(vlat[:, :], ps[:, 4, NT:NT + P])
            V.tensor_copy(ckT[:, 0, :], ps[:, 4, NT + P:NT + 2 * P]).then_inc(qraw_ready, 1)
            dve.wait_ge(qraw_ready, 2)
            V.tensor_copy(kT[0:64, 1, 0:TG], kT[64:128, 0, 0:TG])
            V.tensor_copy(kT[64:128, 1, 0:TG], kT[0:64, 0, 0:TG])
            V.tensor_copy(ckT[0:64, 1, :], ckT[64:128, 0, :])
            V.tensor_copy(ckT[64:128, 1, :], ckT[0:64, 0, :])
            V.tensor_tensor(rt[:, 0:4, :], qT[:, :, TG:NT], cos.unsqueeze(1).to_broadcast([P, 4, TG]), ALU.mult)
            link(V.tensor_tensor(rt[:, 4, :], kT[:, 0, TG:NT], cos, ALU.mult))
            dve.wait_ge(rot_done, 1)
            V.tensor_tensor(rt2[:, 0:4, :], ps[:, 2, :].rearrange("p (c t) -> p c t", c=4),
                            sin.unsqueeze(1).to_broadcast([P, 4, TG]), ALU.mult)
            link(V.tensor_tensor(rt2[:, 4, :], ps[:, 4, 0:P], sin, ALU.mult))
            V.tensor_tensor(qT[:, :, TG:NT], rt[:, 0:4, :], rt2[:, 0:4, :], ALU.add).then_inc(qk_ready, 1)
            link(V.tensor_tensor(kT[:, 0, TG:NT], rt[:, 4, :], rt2[:, 4, :], ALU.add))
            V.tensor_copy(kT[0:64, 1, TG:NT], kT[64:128, 0, TG:NT])
            V.tensor_copy(kT[64:128, 1, TG:NT], kT[0:64, 0, TG:NT]).then_inc(qk_ready, 1)
            take_mod(0, 2, 4)

            dve.wait_ge(scores_done, 1)
            V.tensor_reduce(smax[:, 0, :], ps[:, 0:2, :].rearrange("p b (h k) -> p (b h) k", h=4), AX.X, ALU.max)
            link(V.tensor_reduce(smax[:, 1, :], ps[:, 2:6, :].rearrange("p b (h k) -> p (b h) k", h=2), AX.X, ALU.max))
            link(V.scalar_tensor_tensor(out=nmax[:, :, :], in0=smax[:, :, :], scalar=SCALE,
                                        in1=sink[:, :].unsqueeze(1).to_broadcast([P, 2, NH]),
                                        op0=ALU.mult, op1=ALU.max))
            V.tensor_scalar(nmax[:, :, :], nmax[:, :, :], -1.0, None, ALU.mult).then_inc(nmax_ready, 1)
            dve.wait_ge(nmax_ready, 1)
            V.tensor_tensor(esink[:, :, :], nmax[:, :, :], sink[:, :].unsqueeze(1).to_broadcast([P, 2, NH]),
                            ALU.add).then_inc(nmax_ready, 1)
            dve.wait_ge(exp_ready, 17)
            link(V.tensor_tensor(rden[:, :, :], rsum[:, :, :], esink[:, :, :], ALU.add))
            link(V.reciprocal(rden[:, :, :], rden[:, :, :]))
            for h in range(NH):
                last = V.tensor_scalar(probs[:, h, :], probs[:, h, :], rden[:, 0, h:h + 1], None, ALU.mult)
            last.then_inc(probs_ready, 1)
            for h in range(NH):
                last = V.tensor_scalar(probs[:, 8 + 2 * h:10 + 2 * h, :], probs[:, 8 + 2 * h:10 + 2 * h, :],
                                       rden[:, 1, h:h + 1], None, ALU.mult)
                if h % 4 == 3:
                    last.then_inc(probs_ready, 1)
            take_mod(0, 4, 5)
            for b in (0, 2, 4):
                dve.wait_ge(pt_done, b + 1)
                V.tensor_copy(probsT[:, 4 * b:4 * b + 4, :], ps[:, b, :].rearrange("p (n k) -> p n k", n=4)).then_inc(
                    pt_ready, 1)
            dve.wait_ge(pool_done, 1)
            for m in range(4):
                last = V.tensor_scalar(mixT[:, m, :], psx[:, 4 + m, :], vec[:, V_PSC + m:V_PSC + m + 1], None,
                                       ALU.mult)
            last.then_inc(mix_ready, 1)
            residual(1, psx, 0, 2, lambda k: product(dve, y_done[0], "out", 0, k))
            norm_dve(1, lambda k, g: gain[:, 0, 1, k, g:g + 1])

            def first_match(out, eq, a, top):
                link(V.tensor_tensor(a, eq, first.unsqueeze(1).to_broadcast([P, 2, 4]), ALU.mult))
                link(V.tensor_reduce(top, a, AX.X, ALU.max))
                link(V.tensor_tensor(out, a, wide(top), ALU.is_equal))

            def wide(v, n=4):
                return v.unsqueeze(2).to_broadcast([P, 2, n])

            def route(l):
                dve.wait_ge(route_done, l + 1)
                link(V.tensor_copy(lg[:, :, :], ps_logit[:, :, 0:20]))
                gl = lg[:, :, 16:20]
                gmax, m1, m2, gsum, t0 = rs[:, 4], rs[:, 5], rs[:, 6], rs[:, 7], rs[:, 8]
                link(V.tensor_reduce(gmax, gl, AX.X, ALU.max))
                link(V.tensor_tensor(rg[:, 0], gl, wide(gmax), ALU.subtract))
                link(V.tensor_tensor(rg[:, 2], gl, wide(gmax), ALU.is_equal))
                first_match(rg[:, 3], rg[:, 2], rg[:, 4], rs[:, 11])
                sel = rg[:, 3].unsqueeze(3).to_broadcast([P, 2, 4, 4])
                r4 = r1[:, :, :].rearrange("p g (a e) -> p g a e", a=4)
                link(V.tensor_tensor(r4, lg[:, :, 0:16].rearrange("p g (a e) -> p g a e", a=4), sel, ALU.mult))
                link(V.tensor_reduce(rg[:, 6], r4.rearrange("p g a e -> p g e a"), AX.X, ALU.add))
                link(V.tensor_reduce(m1, rg[:, 6], AX.X, ALU.max))
                link(V.tensor_tensor(rg[:, 2], rg[:, 6], wide(m1), ALU.is_equal))
                first_match(rg[:, 7], rg[:, 2], rg[:, 4], rs[:, 11])
                link(V.scalar_tensor_tensor(out=rg[:, 8], in0=rg[:, 7], scalar=-1e30, in1=rg[:, 6],
                                            op0=ALU.mult, op1=ALU.add))
                link(V.tensor_reduce(m2, rg[:, 8], AX.X, ALU.max))
                link(V.tensor_tensor(rg[:, 2], rg[:, 8], wide(m2), ALU.is_equal))
                first_match(rg[:, 9], rg[:, 2], rg[:, 4], rs[:, 11])
                link(V.tensor_tensor(rg[:, 11], rg[:, 7], rg[:, 9], ALU.add))
                V.tensor_tensor(mask[:, :, :].rearrange("p g (a e) -> p g a e", a=4), sel,
                                rg[:, 11].unsqueeze(2).to_broadcast([P, 2, 4, 4]), ALU.mult).then_inc(mask_ready, 1)
                V.tensor_tensor(rs[:, 0], m1, m1, ALU.subtract)
                V.tensor_tensor(rs[:, 1], m2, m1, ALU.subtract).then_inc(gexp_in, 1)
                dve.wait_ge(gexp_out, 2 * l + 2)
                link(V.tensor_reduce(gsum, rg[:, 1], AX.X, ALU.add))
                link(V.tensor_tensor(t0, rs[:, 2], rs[:, 3], ALU.add))
                link(V.tensor_tensor(t0, t0, gsum, ALU.mult))
                link(V.reciprocal(t0, t0))
                link(V.tensor_tensor(rs[:, 9], rs[:, 2], t0, ALU.mult))
                link(V.tensor_tensor(rs[:, 10], rs[:, 3], t0, ALU.mult))
                link(V.tensor_tensor(rg[:, 7], rg[:, 7], wide(rs[:, 9]), ALU.mult))
                link(V.tensor_tensor(rg[:, 9], rg[:, 9], wide(rs[:, 10]), ALU.mult))
                link(V.tensor_tensor(rg[:, 10], rg[:, 7], rg[:, 9], ALU.add))
                link(V.tensor_tensor(gate[:, :, 0:NE].rearrange("p g (a e) -> p g a e", a=4), sel,
                                     rg[:, 10].unsqueeze(2).to_broadcast([P, 2, 4, 4]), ALU.mult))
                dve.wait_ge(rank_done, l + 1)
                link(V.scalar_tensor_tensor(out=slot[:, :, 0:NE], in0=ps_rank[:, 0:2, :], scalar=1.0,
                                            in1=mask[:, :, :], op0=ALU.add, op1=ALU.mult))
                V.tensor_scalar(slot[:, :, 0:NE], slot[:, :, 0:NE], -1.0, None, ALU.add)
                link(V.tensor_reduce(crowd[:, :], ps_rank[:, 2, :].rearrange("p (i u) -> p i u", u=2), AX.X, ALU.max))
                link(V.tensor_scalar(over[:, :], crowd[:, :], LIMITS[1], None, ALU.is_gt))
                V.scalar_tensor_tensor(out=path[:, :], in0=crowd[:, :], scalar=LIMITS[0], in1=over[:, :],
                                       op0=ALU.is_gt, op1=ALU.add).then_inc(gate_ready, 1)
                dve.wait_ge(gate_ready, l + 1)

            def choose(l, i, later, r):
                shape = [P, 2, 2, CAP]
                e = slice(0, 2) if i is None else bass.ds(i * 2 + 2 * later, 2)
                V.tensor_tensor(pick.rearrange("p g (u j) -> p g u j", u=2),
                                iota[:, r * CAP:(r + 1) * CAP].unsqueeze(1).unsqueeze(1).to_broadcast(shape),
                                slot[:, :, e].unsqueeze(3).to_broadcast(shape), ALU.is_equal).then_inc(picked[r], 1)
                base = l * (PAIRS + 1) + later if r == 0 else l * PAIRS
                dve.wait_ge(picked[r], base + 1 if i is None else i + (base + 1))
                V.tensor_tensor(pick_gate.rearrange("p g (u j) -> p g u j", u=2),
                                pick.rearrange("p g (u j) -> p g u j", u=2),
                                gate[:, :, e].unsqueeze(3).to_broadcast(shape), ALU.mult).then_inc(pick_ready[r], 1)

            def experts(l):
                first = TILE["w1", l, 0]
                choose(l, None, 0, 0)
                dve.wait_ge(mod_done, ADA[(ADA_ROUTE_0, ADA_ROOT[1])[l][0]] + 1)
                if l == 0:
                    take_mod(0, 5, 6)
                    take_mod(1, 0, 2)
                else:
                    take_mod(1, 5, 6)
                with dve.Fori(0, PAIRS) as i:
                    n = i + l * PAIRS
                    way = dve.value_load(path[0:1, bass.ds(i, 1)], min_val=0, max_val=2)
                    def compact(r, last_round):
                        dve.wait_ge(spread_done[r], n + 1)
                        V.tensor_copy(spread, ps[:, 7, 0:NT]).then_inc(spread_ready[r], 1)
                        dve.wait_ge(gather_done[r], n * 2 + 2)
                        V.tensor_copy(hsel[:, 4:8, :], ps[:, 5, :].rearrange("p (k j) -> p k j", k=4)).then_inc(
                            hsel_hi[r], 1)
                        dve.wait_ge(sil_ready[r], n + 1)
                        dve.wait_ge(hid_done[r], n * 2 + 2)
                        for h in range(2):
                            c = slice(h * 2 * P, (h + 1) * 2 * P)
                            V.tensor_tensor(hid[:, c], sil[:, c], ps[:, 7, c], ALU.mult).then_inc(hid_ready[r], 1)
                        dve.wait_ge(turn_done[r], n * 2 + 2)
                        V.tensor_copy(hidT[:, 2:4, :], ps[:, 7, 0:2 * P].rearrange("p (f j) -> p f j", f=2)).then_inc(
                            hidT_hi[r], 1)
                        if last_round:
                            choose(l, i, 1, 0)
                        else:
                            choose(l, i, 0, 1)
                        dve.wait_ge(ysel_done[r], n * 2 + 2)
                        V.tensor_copy(ysel[:, 512:1024], ps[:, 5, :]).then_inc(ysel_hi[r], 1)

                    with dve.If(way == 0):
                        compact(0, True)
                        dve.sem_inc(picked[1], 1)
                        dve.sem_inc(pick_ready[1], 1)
                        dve.sem_inc(spread_ready[1], 1)
                        dve.sem_inc(hsel_hi[1], 1)
                        dve.sem_inc(hid_ready[1], 2)
                        dve.sem_inc(hidT_hi[1], 1)
                        dve.sem_inc(ysel_hi[1], 1)
                        dve.sem_inc(gdiag_ready, 1)
                        dve.sem_inc(gatebc_ready, 1)
                        dve.sem_inc(dense_act_ready, 2 * FC)
                        dve.sem_inc(gated, 2 * FC)
                    with dve.Else():
                        with dve.If(way == 1):
                            compact(0, False)
                            compact(1, True)
                            dve.sem_inc(gdiag_ready, 1)
                            dve.sem_inc(gatebc_ready, 1)
                            dve.sem_inc(dense_act_ready, 2 * FC)
                            dve.sem_inc(gated, 2 * FC)
                        with dve.Else():
                            shape = [P, 2, 2, TG]
                            V.tensor_tensor(gate_diag.rearrange("p (u g) t -> p u g t", u=2),
                                            ident.unsqueeze(1).unsqueeze(1).to_broadcast(shape),
                                            gate[:, :, bass.ds(i * 2, 2)].rearrange("p g u -> p u g").unsqueeze(
                                                3).to_broadcast(shape), ALU.mult).then_inc(gdiag_ready, 1)
                            dve.wait_ge(gatebc_done, n + 1)
                            V.tensor_copy(gatebc, ps[:, 4, :].rearrange("p (u t) -> p u t", u=2)).then_inc(
                                gatebc_ready, 1)
                            dve.wait_ge(gatebc_ready, n + 1)
                            for u in range(2):
                                for m in range(FC):
                                    turn = FC * u + m + 1
                                    dve.wait_ge(dense_sil_ready, n * 2 * FC + turn)
                                    V.tensor_tensor(dense_sil[:, m, :], dense_sil[:, m, :], gatebc[:, u, :],
                                                    ALU.mult).then_inc(gated, 1)
                                    dve.wait_ge(gated, n * 2 * FC + turn)
                                    V.tensor_tensor(dense_act[:, m, :], dense_sil[:, m, :], ps[:, 4 + m, NT:2 * NT],
                                                    ALU.mult).then_inc(dense_act_ready, 1)
                            choose(l, i, 1, 0)
                            for r in range(2):
                                if r:
                                    dve.sem_inc(picked[1], 1)
                                    dve.sem_inc(pick_ready[1], 1)
                                dve.sem_inc(spread_ready[r], 1)
                                dve.sem_inc(hsel_hi[r], 1)
                                dve.sem_inc(hid_ready[r], 2)
                                dve.sem_inc(hidT_hi[r], 1)
                                dve.sem_inc(ysel_hi[r], 1)
                dve.wait_ge(pair_done, (l + 1) * PAIRS)

            route(0)
            experts(0)
            residual(2, psx, 0, 5, lambda k: None)
            norm_dve(2, lambda k, g: gain[:, 1, 0, k, g:g + 1])

            link(V.memset(upad[:, :, :, :], 0.0))
            cv = [conv[:, k, :].rearrange("p (g t) -> p g t", g=2) for k in range(DC)]

            def glu(m):
                dve.wait_ge(sig_ready, m + 1)
                V.scalar_tensor_tensor(out=upad[:, m, :, HALF:HALF + TG],
                                       in0=ps[:, m % 6, 0:NT].rearrange("p (g t) -> p g t", g=2),
                                       scalar=vec[:, V_CB1 + m:V_CB1 + m + 1],
                                       in1=sq[:, m, :].rearrange("p (g t) -> p g t", g=2),
                                       op0=ALU.add, op1=ALU.mult).then_inc(u_ready, 1)

            def convolve(r):
                chunks = DVE_CHUNKS[r]
                base, n = TAPS * sum(len(c) for c in DVE_CHUNKS[:r]), len(chunks)
                dve.wait_ge(u_ready, chunks[-1] + 1)
                for k in chunks:
                    V.tensor_scalar(cv[k], upad[:, k, :, 0:TG], dw[:, k, 0:1], vec[:, V_DWB + k:V_DWB + k + 1],
                                    ALU.mult, ALU.add).then_inc(tap_done, 1)
                with dve.Fori(0, (TAPS - 1) // UNROLL) as i:
                    for s in range(UNROLL):
                        tap = i * UNROLL + (s + 1)
                        for j, k in enumerate(chunks):
                            dve.wait_ge(tap_done, i * (UNROLL * n) + (base + s * n + j + 1))
                            V.scalar_tensor_tensor(out=cv[k], in0=upad[:, k, :, bass.ds(tap, TG)],
                                                   scalar=dw[:, k, bass.ds(tap, 1)], in1=cv[k],
                                                   op0=ALU.mult, op1=ALU.add).then_inc(tap_done, 1)
                dve.wait_ge(tap_done, base + TAPS * n)

            for m in range(4):
                glu(m)
            convolve(0)
            for m in range(4, AP_CHUNK):
                glu(m)
            convolve(1)
            dve.sem_inc(conv_ready, 1)
            take_mod(1, 2, 4)
            dve.wait_ge(mean_ready, 1)
            for k in range(DC):
                V.tensor_tensor(conv[:, k, :], conv[:, k, :], mean[:, :], ALU.subtract).then_inc(cent_ready, 1)
            dve.wait_ge(croot_ready, 1)
            link(V.reciprocal(rstd[:, :], root[:, :]))
            for k in range(DC):
                V.tensor_tensor(conv[:, k, :], conv[:, k, :], rstd[:, :], ALU.mult).then_inc(cn_ready, 1)
            residual(3, sq, 1, 2, lambda k: dve.wait_ge(yb_ready, k + 1))
            take_mod(1, 4, 5)
            norm_dve(3, lambda k, g: gain[:, 1, 1, k, g:g + 1])
            route(1)
            experts(1)
            residual(4, psx, 1, 5, lambda k: None)
            dve.wait_ge(root_ready[4], 1)
            for g in range(2):
                t = slice(g * TG, (g + 1) * TG)
                link(V.reciprocal(rstd[:, t], root[:, t]))
                for k in range(DC):
                    V.scalar_tensor_tensor(out=hT[:, k, t], in0=xT[:, k, t], scalar=vec[:, V_FIN + k:V_FIN + k + 1],
                                           in1=rstd[:, t], op0=ALU.mult, op1=ALU.mult).then_inc(hpre_ready[4], 1)
            dve.wait_ge(out_t, 4)
            V.tensor_copy(xtok[:, 1, 512:1024], ps[:, 3, :]).then_inc(out_ready[1], 1)


def shape_constants():
    t = np.zeros((P, C_W), np.float32)
    t[:, C_ID:C_ID + P] = np.eye(P, dtype=np.float32)
    axis, half = HD // 2, HD // 4
    for d in range(P):
        j = d % axis
        if j < half:
            t[d + half, C_ROT + d] = -1.0
        else:
            t[d - half, C_ROT + d] = 1.0
    inv = (10000.0 ** (-np.arange(0, axis, 2, dtype=np.float32) / axis)).astype(np.float32)
    tok = np.arange(TG)
    pos = {0: (tok // 64).astype(np.float32), 1: (tok % 64).astype(np.float32)}
    for d in range(P):
        ang = pos[(d % HD) // axis] * inv[d % half]
        t[d, C_COS:C_COS + TG] = np.cos(ang)
        t[d, C_SIN:C_SIN + TG] = np.sin(ang)
    for j in range(4):
        for r in range(2 * ADA_MOST):
            t[32 * j + r, C_SEL + r] = 1.0
    t[:, C_IOTA:C_IOTA + 2 * CAP] = np.arange(2 * CAP, dtype=np.float32)
    t[:, C_FIRST:C_FIRST + 4] = (4.0, 3.0, 2.0, 1.0)
    t[:, C_UPPER:C_UPPER + P] = np.triu(np.ones((P, P), np.float32), 1)
    for w, size in enumerate(WINDOWS):
        lo, hi = size // 2, size - size // 2 - 1
        count = np.clip(tok + hi + 1, 0, TG) - np.clip(tok - lo, 0, TG)
        t[:, C_CNT + w * P:C_CNT + (w + 1) * P] = (1.0 / count).astype(np.float32)
    return t


INPUTS = ("x_prompt", "x_sample", "cache_k", "cache_v", "c", "c_ctx", "w_ada", "b_ada", "norm_mix_g",
          "norm_ffn_g", "w_in_ab", "pool_w", "pool_scale", "attn_sink", "w_out_ab", "conv_w1", "conv_b1",
          "conv_dw", "conv_dw_b", "conv_ln_g", "conv_ln_b", "conv_w2", "conv_b2", "router_grp", "router_exp",
          "moe_w1", "moe_w3", "moe_w2", "final_g")
OUTPUTS = (("y_prompt", (1, TG, D)), ("y_sample", (1, TG, D)), ("state_k", (1, 1, TG, 2, HD)),
           ("state_v", (1, 1, TG, 2, HD)))


def kernel(**inputs):
    import concourse.bacc as bacc
    from concourse.bass_utils import run_bass_kernel_spmd

    nc = bacc.Bacc("TRN2", target_bir_lowering=False, num_devices=1)
    arrays, args = {}, []
    for name in INPUTS:
        a = np.ascontiguousarray(inputs[name])
        arrays[f"in_{name}"] = a
        args.append(nc.dram_tensor(f"in_{name}", a.shape, mybir.dt.from_np(a.dtype), kind="ExternalInput").ap())
    arrays["in_shape_consts"] = shape_constants()
    args.append(nc.dram_tensor("in_shape_consts", (P, C_W), F32, kind="ExternalInput").ap())
    for name, shape in OUTPUTS:
        args.append(nc.dram_tensor(f"out_{name}", shape, F32, kind="ExternalOutput").ap())
    backbone(nc, *args)
    result = run_bass_kernel_spmd(nc, [arrays], core_ids=[0])
    return tuple(result.results[0][f"out_{name}"] for name, _ in OUTPUTS)
```
